# Optimizing a Trainium2 kernel written in Bass

```python
import math
import jax, jax.numpy as jnp
from jax import lax
import numpy as np

D_MODEL = 1024
BATCH = 1
SEQ = 512
DEPTH = 1

GDN_HEADS = 8
GDN_DK = 128
GDN_DV = 128
SSD_HEADS = 16
SSD_HEADDIM = 64
SSD_GROUPS = 2
SSD_STATE = 128
CONV_K = 4
CHUNK = 64
D_FF = 2816
FFN_CONV_K = 3
EPS = 1e-6

GDN_QK = GDN_HEADS * GDN_DK
GDN_V = GDN_HEADS * GDN_DV
SSD_D = SSD_HEADS * SSD_HEADDIM
SSD_BC = SSD_GROUPS * SSD_STATE
SSD_HPG = SSD_HEADS // SSD_GROUPS
MIX_WIDTH = GDN_V + SSD_D
GDN_CONV_CH = 2 * GDN_QK + GDN_V
SSD_CONV_CH = SSD_D + 2 * SSD_BC
IN_SPLITS = (GDN_QK, GDN_QK, GDN_V, GDN_V, GDN_HEADS, GDN_HEADS,
             SSD_D, SSD_D, SSD_BC, SSD_BC, SSD_HEADS)
D_IN_PROJ = sum(IN_SPLITS)


def rms_norm(x, w):
    xf = x.astype(jnp.float32)
    y = xf * lax.rsqrt(jnp.mean(xf * xf, axis=-1, keepdims=True) + EPS)
    return (y * w.astype(jnp.float32)).astype(x.dtype)

def l2_normalize(x):
    xf = x.astype(jnp.float32)
    return xf * lax.rsqrt(jnp.sum(xf * xf, axis=-1, keepdims=True) + EPS)

def causal_dwconv(x, w, b=None):
    k_w, ch = w.shape
    y = lax.conv_general_dilated(
        x, w[:, None, :].astype(x.dtype), window_strides=(1,), padding=[(k_w - 1, 0)],
        dimension_numbers=("NWC", "WIO", "NWC"), feature_group_count=ch)
    if b is not None:
        y = y + b.astype(x.dtype)
    return y

def gdn_chunked(q, k, v, g, beta):
    bsz, s, h, dk = q.shape
    dv = v.shape[-1]
    n = s // CHUNK

    def chunk(t):
        return jnp.moveaxis(t.reshape(bsz, n, CHUNK, h, *t.shape[3:]), 3, 1)

    q, k, v, g, beta = (chunk(t) for t in (q, k, v, g, beta))
    gc = jnp.cumsum(g, axis=-1)
    causal = jnp.tril(jnp.ones((CHUNK, CHUNK), dtype=bool))
    strict = jnp.tril(jnp.ones((CHUNK, CHUNK), dtype=bool), -1)
    decay = jnp.exp(jnp.where(causal, gc[..., :, None] - gc[..., None, :], -jnp.inf))
    kb = k * beta[..., None]
    a_in = jnp.einsum("bhnid,bhnjd->bhnij", kb, k) * decay
    lmat = jnp.where(strict, a_in, 0.0) + jnp.eye(CHUNK, dtype=a_in.dtype)
    rhs = jnp.concatenate([v * beta[..., None], kb * jnp.exp(gc)[..., None]], axis=-1)
    sol = lax.linalg.triangular_solve(lmat, rhs, left_side=True, lower=True, unit_diagonal=True)
    u, w = sol[..., :dv], sol[..., dv:]
    qk = jnp.einsum("bhnid,bhnjd->bhnij", q, k) * decay
    q_dec = q * jnp.exp(gc)[..., None]
    k_dec = k * jnp.exp(gc[..., -1:] - gc)[..., None]
    g_last = jnp.exp(gc[..., -1])

    def step(state, xs):
        u_i, w_i, qk_i, q_i, k_i, gl = xs
        v_new = u_i - jnp.einsum("bhcd,bhde->bhce", w_i, state)
        o = jnp.einsum("bhcd,bhde->bhce", q_i, state) + jnp.einsum("bhij,bhje->bhie", qk_i, v_new)
        state = state * gl[..., None, None] + jnp.einsum("bhcd,bhce->bhde", k_i, v_new)
        return state, o

    xs = tuple(jnp.moveaxis(t, 2, 0) for t in (u, w, qk, q_dec, k_dec, g_last))
    s0 = jnp.zeros((bsz, h, dk, dv), dtype=q.dtype)
    _, o = lax.scan(step, s0, xs)
    return jnp.transpose(o, (1, 0, 3, 2, 4)).reshape(bsz, s, h, dv)

def ssd_chunked(x, dt, a_neg, bmat, cmat):
    bsz, s, grp, hg, p = x.shape
    nst = bmat.shape[-1]
    n = s // CHUNK
    xdt = x * dt[..., None]
    adt = dt * a_neg

    def chunk(t):
        return jnp.moveaxis(t.reshape(bsz, n, CHUNK, *t.shape[2:]), 1, 0)

    xs = tuple(chunk(t) for t in (xdt, adt, bmat, cmat))
    causal = jnp.tril(jnp.ones((CHUNK, CHUNK), dtype=bool))

    def step(state, xs):
        xdt_i, adt_i, b_i, c_i = xs
        acs = jnp.cumsum(jnp.moveaxis(adt_i, 1, -1), axis=-1)
        lmat = jnp.exp(jnp.where(causal, acs[..., :, None] - acs[..., None, :], -jnp.inf))
        cb = jnp.einsum("blgn,bsgn->bgls", c_i, b_i)
        y_diag = jnp.einsum("bgls,bghls,bsghp->blghp", cb, lmat, xdt_i)
        y_off = jnp.einsum("blgn,bghpn,bghl->blghp", c_i, state, jnp.exp(acs))
        decay_s = jnp.exp(acs[..., -1:] - acs)
        state = state * jnp.exp(acs[..., -1])[..., None, None] + jnp.einsum(
            "bsgn,bghs,bsghp->bghpn", b_i, decay_s, xdt_i)
        return state, y_diag + y_off

    s0 = jnp.zeros((bsz, grp, hg, p, nst), dtype=x.dtype)
    _, y = lax.scan(step, s0, xs)
    return jnp.moveaxis(y, 0, 1).reshape(bsz, s, grp, hg, p)

def hybrid_layer(x, pre_mix_norm, w_in, gdn_conv_w, gdn_a_log, gdn_dt_bias, gdn_norm_w,
                 ssd_conv_w, ssd_conv_b, ssd_a_log, ssd_dt_bias, ssd_d, ssd_norm_w,
                 w_out, post_mix_norm, pre_ffn_norm, w_up, ffn_conv_w, ffn_conv_b,
                 w_down, post_ffn_norm):
    f32 = jnp.float32
    bsz, s, _ = x.shape
    h = rms_norm(x, pre_mix_norm)
    proj = h @ w_in
    offsets = np.cumsum(IN_SPLITS)[:-1].tolist()
    q, k, v, z_a, b_a, a_a, z_s, x_s, b_s, c_s, dt_s = jnp.split(proj, offsets, axis=-1)

    qkv = jax.nn.silu(causal_dwconv(jnp.concatenate([q, k, v], axis=-1), gdn_conv_w))
    q, k, v = jnp.split(qkv, [GDN_QK, 2 * GDN_QK], axis=-1)
    q = l2_normalize(q.reshape(bsz, s, GDN_HEADS, GDN_DK)) * (GDN_DK ** -0.5)
    k = l2_normalize(k.reshape(bsz, s, GDN_HEADS, GDN_DK))
    v = v.reshape(bsz, s, GDN_HEADS, GDN_DV).astype(f32)
    beta = jax.nn.sigmoid(b_a.astype(f32))
    g = -jnp.exp(gdn_a_log.astype(f32)) * jax.nn.softplus(a_a.astype(f32) + gdn_dt_bias.astype(f32))
    o_a = gdn_chunked(q, k, v, g, beta)
    o_a = rms_norm(o_a, gdn_norm_w) * jax.nn.silu(z_a.reshape(bsz, s, GDN_HEADS, GDN_DV).astype(f32))
    o_a = o_a.reshape(bsz, s, GDN_V).astype(x.dtype)

    xbc = jax.nn.silu(causal_dwconv(jnp.concatenate([x_s, b_s, c_s], axis=-1), ssd_conv_w, ssd_conv_b))
    xs_, bm, cm = jnp.split(xbc, [SSD_D, SSD_D + SSD_BC], axis=-1)
    xs_ = xs_.reshape(bsz, s, SSD_GROUPS, SSD_HPG, SSD_HEADDIM).astype(f32)
    bm = bm.reshape(bsz, s, SSD_GROUPS, SSD_STATE).astype(f32)
    cm = cm.reshape(bsz, s, SSD_GROUPS, SSD_STATE).astype(f32)
    dt = jax.nn.softplus(dt_s.astype(f32) + ssd_dt_bias.astype(f32)).reshape(bsz, s, SSD_GROUPS, SSD_HPG)
    a_neg = -jnp.exp(ssd_a_log.astype(f32)).reshape(SSD_GROUPS, SSD_HPG)
    y = ssd_chunked(xs_, dt, a_neg, bm, cm)
    y = y + ssd_d.astype(f32).reshape(SSD_GROUPS, SSD_HPG)[..., None] * xs_
    y = y.reshape(bsz, s, SSD_D) * jax.nn.silu(z_s.astype(f32))
    y = rms_norm(y.reshape(bsz, s, SSD_GROUPS, SSD_D // SSD_GROUPS),
                 ssd_norm_w.reshape(SSD_GROUPS, SSD_D // SSD_GROUPS))
    o_s = y.reshape(bsz, s, SSD_D).astype(x.dtype)

    mix = jnp.concatenate([o_a, o_s], axis=-1) @ w_out
    x = x + rms_norm(mix, post_mix_norm)

    h = rms_norm(x, pre_ffn_norm)
    u = causal_dwconv(h @ w_up, ffn_conv_w, ffn_conv_b)
    gate, up = jnp.split(u, 2, axis=-1)
    f = (jax.nn.silu(gate) * up) @ w_down
    return x + rms_norm(f, post_ffn_norm)

def first_inputs(seed: int = 0) -> dict:
    key = jax.random.key(seed)
    ks = jax.random.split(key, 24)
    f32 = jnp.float32
    L = DEPTH

    def nrm(k, shape, scale):
        return jax.random.normal(k, shape, f32) * scale

    def gain(k, shape):
        return 1.0 + 0.05 * jax.random.normal(k, shape, f32)

    def dt_bias(k, shape):
        dt = jnp.exp(jax.random.uniform(k, shape, f32, math.log(1e-3), math.log(1e-1)))
        return dt + jnp.log(-jnp.expm1(-dt))

    def a_log(k, shape):
        return jnp.log(jax.random.uniform(k, shape, f32, 1.0, 16.0))

    return {
        "x": nrm(ks[0], (BATCH, SEQ, D_MODEL), 1.0),
        "pre_mix_norm": gain(ks[1], (L, D_MODEL)),
        "w_in": nrm(ks[2], (L, D_MODEL, D_IN_PROJ), D_MODEL ** -0.5),
        "gdn_conv_w": nrm(ks[3], (L, CONV_K, GDN_CONV_CH), CONV_K ** -0.5),
        "gdn_a_log": a_log(ks[4], (L, GDN_HEADS)),
        "gdn_dt_bias": dt_bias(ks[5], (L, GDN_HEADS)),
        "gdn_norm_w": gain(ks[6], (L, GDN_DV)),
        "ssd_conv_w": nrm(ks[7], (L, CONV_K, SSD_CONV_CH), CONV_K ** -0.5),
        "ssd_conv_b": nrm(ks[8], (L, SSD_CONV_CH), 0.02),
        "ssd_a_log": a_log(ks[9], (L, SSD_HEADS)),
        "ssd_dt_bias": dt_bias(ks[10], (L, SSD_HEADS)),
        "ssd_d": gain(ks[11], (L, SSD_HEADS)),
        "ssd_norm_w": gain(ks[12], (L, SSD_D)),
        "w_out": nrm(ks[13], (L, MIX_WIDTH, D_MODEL), MIX_WIDTH ** -0.5),
        "post_mix_norm": gain(ks[14], (L, D_MODEL)),
        "pre_ffn_norm": gain(ks[15], (L, D_MODEL)),
        "w_up": nrm(ks[16], (L, D_MODEL, 2 * D_FF), D_MODEL ** -0.5),
        "ffn_conv_w": nrm(ks[17], (L, FFN_CONV_K, 2 * D_FF), FFN_CONV_K ** -0.5),
        "ffn_conv_b": nrm(ks[18], (L, 2 * D_FF), 0.02),
        "w_down": nrm(ks[19], (L, D_FF, D_MODEL), D_FF ** -0.5),
        "post_ffn_norm": gain(ks[20], (L, D_MODEL)),
    }

def first_block(x, pre_mix_norm, w_in, gdn_conv_w, gdn_a_log, gdn_dt_bias, gdn_norm_w,
              ssd_conv_w, ssd_conv_b, ssd_a_log, ssd_dt_bias, ssd_d, ssd_norm_w,
              w_out, post_mix_norm, pre_ffn_norm, w_up, ffn_conv_w, ffn_conv_b,
              w_down, post_ffn_norm):
    for l in range(DEPTH):
        x = hybrid_layer(x, pre_mix_norm[l], w_in[l], gdn_conv_w[l], gdn_a_log[l], gdn_dt_bias[l],
                         gdn_norm_w[l], ssd_conv_w[l], ssd_conv_b[l], ssd_a_log[l], ssd_dt_bias[l],
                         ssd_d[l], ssd_norm_w[l], w_out[l], post_mix_norm[l], pre_ffn_norm[l],
                         w_up[l], ffn_conv_w[l], ffn_conv_b[l], w_down[l], post_ffn_norm[l])
    return x


DEPTH_2 = 2

Q_BLOCK = 128
NORM_EPS = 1e-6

SB_HEADS = 8
SB_HEAD_DIM = 64
SB_WIDTH = SB_HEADS * SB_HEAD_DIM
POOL_WINDOWS = (2, 4, 8, 16)
POOL_GROUPS = len(POOL_WINDOWS)
POOL_WIDTH = D_MODEL - SB_WIDTH
POOL_GROUP_DIM = POOL_WIDTH // POOL_GROUPS
EVEN_IN_WIDTH = 3 * SB_WIDTH + POOL_WIDTH
EVEN_MIX_WIDTH = SB_WIDTH + POOL_WIDTH

GLA_HEADS = 4
GLA_KEY_WIDTH = D_MODEL // 2
GLA_VALUE_WIDTH = D_MODEL
GLA_KEY_DIM = GLA_KEY_WIDTH // GLA_HEADS
GLA_VALUE_DIM = GLA_VALUE_WIDTH // GLA_HEADS
GLA_GATE_RANK = 16
GLA_TAU = 16.0
ODD_IN_WIDTH = 2 * GLA_KEY_WIDTH + 2 * GLA_VALUE_WIDTH + GLA_GATE_RANK

FFN_HIDDEN = 2816
CONV_WIDTH = 3

N_EVEN = (DEPTH_2 + 1) // 2
N_ODD = DEPTH_2 // 2


def rms_norm_2(x, gain):
    xf = x.astype(jnp.float32)
    y = xf * lax.rsqrt(jnp.mean(xf * xf, axis=-1, keepdims=True) + NORM_EPS)
    return (y * gain.astype(jnp.float32)).astype(x.dtype)

def stick_breaking_attention(q, k, v):
    b, s, h, dh = q.shape
    qh = jnp.transpose(q, (0, 2, 1, 3))
    kh = jnp.transpose(k, (0, 2, 1, 3))
    vh = jnp.transpose(v, (0, 2, 1, 3))
    scale = dh ** -0.5
    key_pos = jnp.arange(s)

    def block(i):
        start = i * Q_BLOCK
        q_blk = lax.dynamic_slice_in_dim(qh, start, Q_BLOCK, axis=2)
        z = jnp.einsum('bhqd,bhkd->bhqk', q_blk, kh,
                       preferred_element_type=jnp.float32) * scale
        q_pos = start + jnp.arange(Q_BLOCK)
        visible = key_pos[None, :] < q_pos[:, None]
        log_fail = jnp.where(visible, jax.nn.log_sigmoid(-z), 0.0)
        cum_rev = lax.cumsum(log_fail, axis=3, reverse=True)
        later = jnp.concatenate([cum_rev[..., 1:], jnp.zeros_like(cum_rev[..., :1])], axis=-1)
        weights = jnp.where(visible, jnp.exp(jax.nn.log_sigmoid(z) + later), 0.0)
        return jnp.einsum('bhqk,bhkd->bhqd', weights.astype(vh.dtype), vh)

    out = lax.map(block, jnp.arange(s // Q_BLOCK))
    return jnp.transpose(out, (1, 0, 3, 2, 4)).reshape(b, s, h * dh)

def multiscale_pool(xb, pool_w, pool_scale):
    b, s, _ = xb.shape
    groups = xb.reshape(b, s, POOL_GROUPS, POOL_GROUP_DIM)
    prefix = jnp.cumsum(groups.astype(jnp.float32), axis=1)
    prefix = jnp.pad(prefix, ((0, 0), (1, 0), (0, 0), (0, 0)))
    pos = jnp.arange(1, s + 1, dtype=jnp.float32)
    outs = []
    for g, w in enumerate(POOL_WINDOWS):
        pg = jnp.pad(prefix[:, :, g], ((0, 0), (w - 1, 0), (0, 0)))
        window_sum = pg[:, w:] - pg[:, :s]
        count = jnp.minimum(pos, float(w))[None, :, None]
        pooled = window_sum / count - groups[:, :, g].astype(jnp.float32)
        outs.append(jnp.einsum('bsc,cd->bsd', pooled.astype(xb.dtype), pool_w[g]))
    return jnp.concatenate(outs, axis=-1) * pool_scale

def gated_linear_attention(q, k, v, log_alpha):
    b, s, h, dk = q.shape
    dv = v.shape[-1]
    n = s // CHUNK

    def chunks(t):
        return jnp.moveaxis(t.reshape(b, n, CHUNK, h, t.shape[-1]), 1, 0)

    qc = chunks(q.astype(jnp.float32))
    kc = chunks(k.astype(jnp.float32))
    vc = chunks(v.astype(jnp.float32))
    cum = jnp.cumsum(chunks(log_alpha), axis=2)
    total = cum[:, :, -1]
    k_dec = kc * jnp.exp(total[:, :, None] - cum)
    chunk_decay = jnp.exp(total)

    def step(state, inp):
        q_c, k_c, v_c, decay_c = inp
        state = decay_c[..., None] * state + jnp.einsum('bchk,bchv->bhkv', k_c, v_c)
        return state, jnp.einsum('bchk,bhkv->bchv', q_c, state)

    state0 = jnp.zeros((b, h, dk, dv), jnp.float32)
    _, out = lax.scan(step, state0, (qc, k_dec, vc, chunk_decay))
    return jnp.moveaxis(out, 0, 1).reshape(b, s, h, dv)

def even_mixer(h, w_in, q_gain, k_gain, pool_w, pool_scale, w_out):
    b, s, _ = h.shape
    proj = h @ w_in
    q, k, v, xb = jnp.split(proj, [SB_WIDTH, 2 * SB_WIDTH, 3 * SB_WIDTH], axis=-1)
    q = rms_norm_2(q.reshape(b, s, SB_HEADS, SB_HEAD_DIM), q_gain)
    k = rms_norm_2(k.reshape(b, s, SB_HEADS, SB_HEAD_DIM), k_gain)
    v = v.reshape(b, s, SB_HEADS, SB_HEAD_DIM)
    o_a = stick_breaking_attention(q, k, v)
    o_b = multiscale_pool(xb, pool_w, pool_scale)
    return jnp.concatenate([o_a.astype(h.dtype), o_b.astype(h.dtype)], axis=-1) @ w_out

def odd_mixer(h, w_in, w_a2, b_a, o_gain, w_out):
    b, s, _ = h.shape
    proj = h @ w_in
    q, k, v, r, a_low = jnp.split(
        proj, [GLA_KEY_WIDTH, 2 * GLA_KEY_WIDTH, 2 * GLA_KEY_WIDTH + GLA_VALUE_WIDTH,
               2 * GLA_KEY_WIDTH + 2 * GLA_VALUE_WIDTH], axis=-1)
    q = q.reshape(b, s, GLA_HEADS, GLA_KEY_DIM) * (GLA_KEY_DIM ** -0.5)
    k = k.reshape(b, s, GLA_HEADS, GLA_KEY_DIM)
    v = v.reshape(b, s, GLA_HEADS, GLA_VALUE_DIM)
    gate_logit = (a_low @ w_a2 + b_a).astype(jnp.float32).reshape(b, s, GLA_HEADS, GLA_KEY_DIM)
    log_alpha = jax.nn.log_sigmoid(gate_logit) / GLA_TAU
    o = gated_linear_attention(q, k, v, log_alpha)
    o = rms_norm_2(o, o_gain).reshape(b, s, GLA_VALUE_WIDTH).astype(h.dtype)
    return (o * jax.nn.silu(r)) @ w_out

def conv_ffn(h, w_up, conv_w, conv_b, w_down):
    s = h.shape[1]
    u = h @ w_up
    up = jnp.pad(u, ((0, 0), (CONV_WIDTH - 1, 0), (0, 0)))
    conv = conv_b
    for j in range(CONV_WIDTH):
        conv = conv + conv_w[j] * up[:, j:j + s]
    a, g = jnp.split(conv, 2, axis=-1)
    return (jax.nn.silu(a) * g) @ w_down

def second_inputs(seed: int = 0) -> dict:
    key = jax.random.key(seed)
    ks = jax.random.split(key, 20)
    f32 = jnp.float32

    def nrm(k, shape, scale):
        return jax.random.normal(k, shape, f32) * scale

    return {
        "x": nrm(ks[0], (BATCH, SEQ, D_MODEL), 1.0),
        "mix_norm_even": 1.0 + nrm(ks[1], (N_EVEN, D_MODEL), 0.02),
        "w_in_even": nrm(ks[2], (N_EVEN, D_MODEL, EVEN_IN_WIDTH), D_MODEL ** -0.5),
        "sb_q_gain": 1.0 + nrm(ks[3], (N_EVEN, SB_HEAD_DIM), 0.02),
        "sb_k_gain": 1.0 + nrm(ks[4], (N_EVEN, SB_HEAD_DIM), 0.02),
        "pool_w": nrm(ks[5], (N_EVEN, POOL_GROUPS, POOL_GROUP_DIM, POOL_GROUP_DIM), POOL_GROUP_DIM ** -0.5),
        "pool_scale": 1.0 + nrm(ks[6], (N_EVEN, POOL_WIDTH), 0.1),
        "w_out_even": nrm(ks[7], (N_EVEN, EVEN_MIX_WIDTH, D_MODEL), EVEN_MIX_WIDTH ** -0.5),
        "mix_norm_odd": 1.0 + nrm(ks[8], (N_ODD, D_MODEL), 0.02),
        "w_in_odd": nrm(ks[9], (N_ODD, D_MODEL, ODD_IN_WIDTH), D_MODEL ** -0.5),
        "gla_w_a2": nrm(ks[10], (N_ODD, GLA_GATE_RANK, GLA_KEY_WIDTH), GLA_GATE_RANK ** -0.5),
        "gla_b_a": nrm(ks[11], (N_ODD, GLA_KEY_WIDTH), 0.01),
        "gla_o_gain": 1.0 + nrm(ks[12], (N_ODD, GLA_VALUE_DIM), 0.02),
        "w_out_odd": nrm(ks[13], (N_ODD, GLA_VALUE_WIDTH, D_MODEL), GLA_VALUE_WIDTH ** -0.5),
        "ffn_norm": 1.0 + nrm(ks[14], (DEPTH_2, D_MODEL), 0.02),
        "ffn_w_up": nrm(ks[15], (DEPTH_2, D_MODEL, 2 * FFN_HIDDEN), D_MODEL ** -0.5),
        "ffn_conv_w": nrm(ks[16], (DEPTH_2, CONV_WIDTH, 2 * FFN_HIDDEN), CONV_WIDTH ** -0.5),
        "ffn_conv_b": nrm(ks[17], (DEPTH_2, 2 * FFN_HIDDEN), 0.01),
        "ffn_w_down": nrm(ks[18], (DEPTH_2, FFN_HIDDEN, D_MODEL), FFN_HIDDEN ** -0.5),
    }

def second_block(x, mix_norm_even, w_in_even, sb_q_gain, sb_k_gain, pool_w, pool_scale, w_out_even,
              mix_norm_odd, w_in_odd, gla_w_a2, gla_b_a, gla_o_gain, w_out_odd,
              ffn_norm, ffn_w_up, ffn_conv_w, ffn_conv_b, ffn_w_down):
    for layer in range(DEPTH_2):
        if layer % 2 == 0:
            i = layer // 2
            x = x + even_mixer(rms_norm_2(x, mix_norm_even[i]), w_in_even[i], sb_q_gain[i],
                               sb_k_gain[i], pool_w[i], pool_scale[i], w_out_even[i])
        else:
            i = layer // 2
            x = x + odd_mixer(rms_norm_2(x, mix_norm_odd[i]), w_in_odd[i], gla_w_a2[i],
                              gla_b_a[i], gla_o_gain[i], w_out_odd[i])
        x = x + conv_ffn(rms_norm_2(x, ffn_norm[layer]), ffn_w_up[layer], ffn_conv_w[layer],
                         ffn_conv_b[layer], ffn_w_down[layer])
    return x


def setup_inputs(seed=0):
    out = dict(first_inputs(seed))
    for name, value in second_inputs(seed + 1).items():
        if name != "x":
            out[name + "_2"] = value
    return out


def reference(
    x, pre_mix_norm, w_in, gdn_conv_w, gdn_a_log, gdn_dt_bias, gdn_norm_w, ssd_conv_w,
    ssd_conv_b, ssd_a_log, ssd_dt_bias, ssd_d, ssd_norm_w, w_out, post_mix_norm, pre_ffn_norm,
    w_up, ffn_conv_w, ffn_conv_b, w_down, post_ffn_norm, mix_norm_even_2, w_in_even_2,
    sb_q_gain_2, sb_k_gain_2, pool_w_2, pool_scale_2, w_out_even_2, mix_norm_odd_2, w_in_odd_2,
    gla_w_a2_2, gla_b_a_2, gla_o_gain_2, w_out_odd_2, ffn_norm_2, ffn_w_up_2, ffn_conv_w_2,
    ffn_conv_b_2, ffn_w_down_2,
):
    x = first_block(
        x, pre_mix_norm, w_in, gdn_conv_w, gdn_a_log, gdn_dt_bias, gdn_norm_w, ssd_conv_w,
        ssd_conv_b, ssd_a_log, ssd_dt_bias, ssd_d, ssd_norm_w, w_out, post_mix_norm,
        pre_ffn_norm, w_up, ffn_conv_w, ffn_conv_b, w_down, post_ffn_norm,
    )
    return second_block(
        x, mix_norm_even_2, w_in_even_2, sb_q_gain_2, sb_k_gain_2, pool_w_2, pool_scale_2,
        w_out_even_2, mix_norm_odd_2, w_in_odd_2, gla_w_a2_2, gla_b_a_2, gla_o_gain_2,
        w_out_odd_2, ffn_norm_2, ffn_w_up_2, ffn_conv_w_2, ffn_conv_b_2, ffn_w_down_2,
    )


_drawn_inputs = setup_inputs


def setup_inputs(seed=0):
    import zlib

    import numpy as np

    out = dict(_drawn_inputs(seed))
    spreads = {}
    factors = {'ffn_conv_b': 2.775,
     'mix_norm_even_2': 5.283,
     'sb_q_gain_2': 8.0,
     'sb_k_gain_2': 8.0,
     'mix_norm_odd_2': 4.386,
     'gla_b_a_2': 26.933,
     'gla_o_gain_2': 23.639,
     'ffn_norm_2': 4.37,
     'ffn_conv_b_2': 8.0}
    for name, (base, spread) in spreads.items():
        noise = np.random.default_rng([zlib.crc32(name.encode()), seed]).standard_normal(out[name].shape)
        drawn = base * np.exp(spread * noise) if base else spread * noise
        out[name] = __import__('jax').numpy.asarray(drawn.astype(out[name].dtype))
    for name, factor in factors.items():
        out[name] = (out[name] * factor).astype(out[name].dtype)
    return out
```

```python
from contextlib import ExitStack

import numpy as np

import concourse.bass as bass
from concourse import mybir

F32 = mybir.dt.float32
F32R = mybir.dt.float32r
ALU = mybir.AluOpType
ACT = mybir.ActivationFunctionType

P = 128
S = 512
D = 1024
KD = D // P
F = 2816
KF = F // P
HALF = KF // 2
TILE = 4 * S
RAW = 4
SPLIT = 2
EPS = 1e-6


def at(base, i, per):
    return base if i is None else base + per * i


class Columns:

    def __init__(self):
        self.start, self.n = {}, 0

    def add(self, name, n):
        self.start[name] = self.n
        self.n += n


def columns():
    c = Columns()
    for name, n in (("eps", 1), ("g_pre_mix", 8), ("g_post_mix", 8), ("g_pre_ffn", 8), ("g_post_ffn", 8),
                    ("g_even", 8), ("g_odd", 8), ("g_ffn_2", 16), ("ffn", 3 * 44 * 4), ("conv", 24 * 5),
                    ("gdn_norm", 1), ("ssd_conv", 12 * 5), ("ssd_d", 8), ("ssd_norm", 8), ("sb_gain", 2),
                    ("pool_scale", 4), ("gla_b", 4), ("gla_gain", 2),
                    ("rows", 48), ("pool_count", 64)):
        c.add(name, n)
    return c
def program(nc, x_in, w8, w11, par_in, cst_in, small_in, small1_in, out, plan):
    cols = columns()
    ctx = ExitStack()
    with ctx:
        top = [(nc.sbuf_base + 31) // 32 * 32]

        def fixed(name, shape, dt=F32):
            t = nc.alloc_sbuf_tensor_at(name, shape, dt, offset=top[0])
            top[0] += (4 * shape[1] + 31) // 32 * 32
            return t

        X = fixed("X", [P, KD * S])
        base_h = top[0]
        HH = fixed("HH", [P, KD * S], F32R)
        HL = fixed("HL", [P, KD * S], F32R)
        Y = nc.alloc_sbuf_tensor_at("Y", [P, KD * S], F32, offset=base_h)
        raw = [fixed(f"raw{j}", [P, HALF * P]) for j in range(RAW)]
        whi = [fixed(f"whi{j}", [P, HALF * P], F32R) for j in range(SPLIT)]
        wlo = [fixed(f"wlo{j}", [P, HALF * P], F32R) for j in range(SPLIT)]
        par = fixed("par", [P, cols.n])
        cst = fixed("cst", [P, 15 * P])
        small = fixed("small", [P, small_in.shape[1]])
        top[0] = (top[0] + 31) // 32 * 32
        FREE = top[0]
        TMP = nc.sbuf_usable_end // 32 * 32 - 6 * TILE
        used = {}

        def place(name, n, offset, dt=F32):
            assert offset >= FREE and offset + 4 * n <= nc.sbuf_usable_end, name
            return nc.alloc_sbuf_tensor_at(name, [P, n], dt, offset=offset)

        ident, ones, upper, lower, halves = (cst[:, k * P:(k + 1) * P] for k in range(5))
        neg_lower, neg_ones, hidden = (cst[:, k * P:(k + 1) * P] for k in range(12, 15))
        level = [cst[:, (5 + k) * P:(6 + k) * P] for k in range(7)]

        def col(name, k=0, n=1):
            c = cols.start[name] + k
            return par[:, c:c + n]

        def dcol(name, k):
            return par[:, bass.ds(k + cols.start[name], 1)]

        def tile(t, k):
            return t[:, k * S:(k + 1) * S]

        def dtile(t, k):
            return t[:, bass.ds(k * S, S)]

        sq = [place(f"sq{j}", S, TMP + j * TILE) for j in range(2)]
        hn = [place(f"hn{j}", S, TMP + (2 + j) * TILE) for j in range(2)]
        rs = place("rs", S, TMP + 4 * TILE)
        ln = place("ln", S, TMP + 5 * TILE)
        taps = [place(f"taps{j}", S, TMP + j * TILE) for j in range(4)]
        prod = [place(f"prod{j}", S, TMP + (4 + j) * TILE) for j in range(2)]
        FH = place("FH", KF * S, FREE, F32R)
        FL = place("FL", KF * S, FREE + KF * TILE, F32R)
        assert FREE + 2 * KF * TILE <= TMP

        acc = [ctx.enter_context(nc.psum_tensor(f"acc{j}", [P, S], F32)) for j in range(2)]
        bank = [ctx.enter_context(nc.psum_tensor(f"bank{j}", [P, S], F32)) for j in range(2, 8)]
        ss = bank[0]

        sems = {}

        def sem(name):
            if name not in sems:
                sems[name] = ctx.enter_context(nc.semaphore(name))
            return sems[name]

        params_in, x_loaded = sem("params_in"), sem("x_loaded")
        raw_in = [sem(f"raw_in{j}") for j in range(RAW)]
        w_hi_ready, w_lo_ready = sem("w_hi_ready"), sem("w_lo_ready")
        unit_done = sem("unit_done")
        acc_read = sem("acc_read")
        sq_ready, sq_summed, rms_ready = sem("sq_ready"), sem("sq_summed"), sem("rms_ready")
        hn_ready, hh_ready, h_ready = sem("hn_ready"), sem("hh_ready"), sem("h_ready")
        tap_ready, conv_step = sem("tap_ready"), sem("conv_step")
        silu_ready, prod_ready, fh_ready, f_ready = (sem(n) for n in ("silu_ready", "prod_ready", "fh_ready", "f_ready"))
        rms_used = sem("rms_used")
        x_ready = sem("x_ready")
        ln_ready, y_step = sem("ln_ready"), sem("y_step")
        out_stored = sem("out_stored")

        def load_units(sp, src, n0, u0, count):
            kt = src.shape[2] // P

            def group(n0, u0, size, i):
                for j in range(size):
                    u, unit = u0 + j, n0 + j if i is None else i * RAW + (n0 + j)
                    if u >= RAW:
                        sp.wait_ge(w_lo_ready, at(u - RAW + 1, i, RAW))
                    sp.dma_start(raw[u % RAW][:, 0:kt * P],
                                 src[bass.ds(unit, 1), :, :].rearrange("a p c -> p (a c)")
                                 ).then_inc(raw_in[u % RAW], 16)

            head = count % RAW + (RAW if u0 == 0 else 0)
            group(n0, u0, head, None)
            with sp.Fori(0, (count - head) // RAW) as i:
                group(n0 + head, u0 + head, RAW, i)

        def split_hi(act, u, i, per, kt):
            j = u % SPLIT
            act.wait_ge(raw_in[u % RAW], at(16 * (u // RAW + 1), i, 16 * per // RAW))
            if u >= SPLIT:
                act.wait_ge(unit_done, at(u - SPLIT + 1, i, per))
            nc.scalar.activation(whi[j][:, 0:kt * P], raw[u % RAW][:, 0:kt * P], ACT.Copy).then_inc(w_hi_ready, 1)

        def split_lo(dve, u, i, per, kt):
            j = u % SPLIT
            dve.wait_ge(w_hi_ready, at(u + 1, i, per))
            nc.vector.tensor_tensor(wlo[j][:, 0:kt * P], raw[u % RAW][:, 0:kt * P],
                                    whi[j][:, 0:kt * P].bitcast(F32), ALU.subtract).then_inc(w_lo_ready, 1)

        def multiply(pe, u, t, i, per, per_t, kt, hi, lo, start=True, stop=True, ready=None, part=None):
            w, a = u % SPLIT, acc[t % 2]
            if not part:
                pe.wait_ge(w_lo_ready, at(u + 1, i, per))
                if start and t >= 2:
                    pe.wait_ge(acc_read, at(t - 1, i, per_t))
            for k in range(kt) if part is None else range(kt * part // 4, kt * (part + 1) // 4):
                if ready:
                    pe.wait_ge(ready[0], ready[1] + k + 1)
                wh, wl = whi[w][:, k * P:(k + 1) * P], wlo[w][:, k * P:(k + 1) * P]
                nc.tensor.matmul(a[:, :], wh, tile(hi, k), start=start and k == 0, stop=False)
                nc.tensor.matmul(a[:, :], wh, tile(lo, k), start=False, stop=False)
                last = nc.tensor.matmul(a[:, :], wl, tile(hi, k), start=False, stop=stop and k == kt - 1)
            if part in (None, 3):
                last.then_inc(unit_done, 1)

        def sums_act(act, c, src, made, n):
            for k in range(n):
                tick = c["sq"] + k
                act.wait_ge(made[0], made[1](k))
                if tick >= 2:
                    act.wait_ge(sq_summed, tick - 1)
                nc.scalar.activation(sq[tick % 2][:, :], tile(src, k), ACT.Square).then_inc(sq_ready, 1)

        def rms_act(act, summed, r, width):
            log_exp(act)
            act.wait_ge(sq_summed, summed)
            if r:
                act.wait_ge(rms_used, r)
            nc.scalar.activation(ln[:, :], ss[:, :], ACT.Ln, scale=1.0 / width, bias=col("eps")).then_inc(ln_ready, 1)
            act.wait_ge(ln_ready, r + 1)
            nc.scalar.activation(rs[:, :], ln[:, :], ACT.Exp, scale=-0.5).then_inc(rms_ready, 1)

        def sums_pe(pe, c, n):
            for k in range(n):
                pe.wait_ge(sq_ready, c["sq"] + k + 1)
                nc.tensor.matmul(ss[:, :], ones, sq[(c["sq"] + k) % 2][:, :], start=k == 0,
                                 stop=k == n - 1).then_inc(sq_summed, 1)

        def norm_act(act, c, made):
            sums_act(act, c, X, made, KD)
            rms_act(act, c["sq"] + KD, c["rms"], D)
            for k in range(KD):
                act.wait_ge(hn_ready, c["hn"] + k + 1)
                nc.scalar.activation(tile(HH, k), hn[k % 2][:, :], ACT.Copy).then_inc(hh_ready, 1)

        def scaled_dve(dve, c, src, gain, used, u0):
            dve.wait_ge(rms_ready, c["rms"] + 1)
            for k in range(KD):
                if k >= 2:
                    dve.wait_ge(used, u0 + k - 1)
                last = nc.vector.scalar_tensor_tensor(out=hn[k % 2][:, :], in0=tile(src, k),
                                                      scalar=col(gain[0], gain[1] + k), in1=rs[:, :],
                                                      op0=ALU.mult, op1=ALU.mult).then_inc(hn_ready, 1)
            dve.wait_ge(hn_ready, c["hn"] + KD)
            dve.sem_inc(rms_used, 1)

        def norm_pool(pool, c):
            for k in range(KD):
                pool.wait_ge(hh_ready, c["h"] + k + 1)
                nc.gpsimd.tensor_tensor(tile(HL, k), hn[k % 2][:, :], tile(HH, k).bitcast(F32),
                                        ALU.subtract).then_inc(h_ready, 1)

        def post_act(act, c, y):
            sums_act(act, c, y, (acc_read, lambda k: c["t"] - KD + k + 1), KD)
            rms_act(act, c["sq"] + KD, c["rms"], D)

        def post_pool(pool, c):
            for k in range(KD):
                pool.wait_ge(hn_ready, c["hn"] + k + 1)
                nc.gpsimd.tensor_tensor(tile(X, k), tile(X, k), hn[k % 2][:, :], ALU.add).then_inc(x_ready, 1)

        def groups(eng, count, body):
            body(0, None)
            if count > 2:
                with eng.Fori(0, count - 2) as i:
                    body(1, i)
            body(count - 1, None)

        def up_act(act, c):
            u0, t0, p0 = c["u"], c["t"], c["pair"]

            def body(g, i):
                def n(base, per):
                    return at(base + per * g, i, per)
                for j in range(4):
                    u, p = u0 + 4 * g + j, p0 + 2 * g + j // 2
                    act.wait_ge(unit_done, n(u0 + j + 1, 4))
                    split_hi(act, u + 2, i, 4, HALF if g == KF // 2 - 1 and j >= 2 else KD)
                    if p >= 2:
                        act.wait_ge(prod_ready, n(p0 + j // 2 - 1, 2))
                    k = n((c["ffn"] * 2 * KF + j) * 4, 16)
                    w = (lambda m: col("ffn", k + m)) if i is None else (lambda m: dcol("ffn", k + m))
                    nc.scalar.activation(taps[j][:, :], acc[(t0 + j) % 2][:, :], ACT.Identity, scale=w(2),
                                         bias=w(3)).then_inc(tap_ready, 1)
                    if j % 2:
                        act.wait_ge(acc_read, n(t0 + j, 4))
                        nc.scalar.activation(taps[j - 1][:, :], taps[j - 1][:, :], ACT.Silu).then_inc(silu_ready, 1)
                        act.wait_ge(prod_ready, n(p0 + j // 2 + 1, 2))
                        pair = n(j // 2, 2)
                        o = tile(FH, pair) if i is None else dtile(FH, pair)
                        nc.scalar.activation(o, prod[j // 2][:, :], ACT.Copy).then_inc(fh_ready, 1)
            groups(act, KF // 2, body)

        def up_dve(dve, c):
            u0, t0 = c["u"], c["t"]

            def body(g, i):
                def n(base, per):
                    return at(base + per * g, i, per)
                for j in range(4):
                    split_lo(dve, u0 + 4 * g + j + 2, i, 4, HALF if g == KF // 2 - 1 and j >= 2 else KD)
                    k = n((c["ffn"] * 2 * KF + j) * 4, 16)
                    w = (lambda m: col("ffn", k + m)) if i is None else (lambda m: dcol("ffn", k + m))
                    dve.wait_ge(tap_ready, n(c["tap"] + j + 1, 4))
                    nc.vector.scalar_tensor_tensor(out=taps[j][:, 1:S], in0=acc[(t0 + j) % 2][:, 0:S - 1], scalar=w(1),
                                                   in1=taps[j][:, 1:S], op0=ALU.mult,
                                                   op1=ALU.add).then_inc(conv_step, 1)
                    dve.wait_ge(conv_step, n(c["conv"] + j + 1, 4))
                    nc.vector.scalar_tensor_tensor(out=taps[j][:, 2:S], in0=acc[(t0 + j) % 2][:, 0:S - 2], scalar=w(0),
                                                   in1=taps[j][:, 2:S], op0=ALU.mult,
                                                   op1=ALU.add).then_inc(acc_read, 1)
            groups(dve, KF // 2, body)

        def up_pool(pool, c):
            t0, p0 = c["t"], c["pair"]

            def body(g, i):
                def n(base, per):
                    return at(base + per * g, i, per)
                for b in range(2):
                    pool.wait_ge(silu_ready, n(p0 + b + 1, 2))
                    pool.wait_ge(acc_read, n(t0 + 2 * b + 2, 4))
                    nc.gpsimd.tensor_tensor(prod[b][:, :], taps[2 * b][:, :], taps[2 * b + 1][:, :],
                                            ALU.mult).then_inc(prod_ready, 1)
                    pool.wait_ge(fh_ready, n(p0 + b + 1, 2))
                    pair = n(b, 2)
                    o, h = (tile(FL, pair), tile(FH, pair)) if i is None else (dtile(FL, pair), dtile(FH, pair))
                    nc.gpsimd.tensor_tensor(o, prod[b][:, :], h.bitcast(F32), ALU.subtract).then_inc(f_ready, 1)
            groups(pool, KF // 2, body)

        def up_pe(pe, c):
            u0, t0 = c["u"], c["t"]

            def body(g, i):
                for j in range(4):
                    multiply(pe, u0 + 4 * g + j, t0 + 4 * g + j, i, 4, 4, KD, HH, HL,
                             ready=(h_ready, c["h"] - KD) if g == 0 and j == 0 else None)
            groups(pe, KF // 2, body)

        def back_pe(pe, c, kt, units, hi, lo, ready):
            u0, t0 = c["u"], c["t"]
            per = 4 // units

            def body(g, i):
                for j in range(4):
                    h = j % units
                    multiply(pe, u0 + 4 * g + j, t0 + per * g + j // units, i, 4, per, kt,
                             hi[h] if isinstance(hi, tuple) else hi[:, h * kt * S:(h + 1) * kt * S],
                             lo[h] if isinstance(lo, tuple) else lo[:, h * kt * S:(h + 1) * kt * S],
                             start=h == 0, stop=h == units - 1,
                             ready=(ready[0], ready[1] + h * kt) if g == 0 and j < units else None)
            groups(pe, 2 * units, body)

        def back_act(act, c, kt, units, kt_next):
            def body(g, i):
                for j in range(4):
                    act.wait_ge(unit_done, at(c["u"] + 4 * g + j + 1, i, 4))
                    u, last = c["u"] + 4 * g + j + 2, g == 2 * units - 1 and j >= 2
                    if not (last and kt_next is None):
                        split_hi(act, u, i, 4, kt_next if last else kt)
            groups(act, 2 * units, body)

        def back_dve(dve, c, kt, units, kt_next, dst=None):
            per = 4 // units

            def body(g, i):
                for j in range(4):
                    u, last = c["u"] + 4 * g + j + 2, g == 2 * units - 1 and j >= 2
                    if not (last and kt_next is None):
                        split_lo(dve, u, i, 4, kt_next if last else kt)
                    if (j + 1) % units == 0:
                        t, k = c["t"] + per * g + j // units, at(per * g + j // units, i, per)
                        x, y = (tile if i is None else dtile)(X, k), dst and (tile if i is None else dtile)(dst, k)
                        dve.wait_ge(unit_done, at(c["u"] + 4 * g + j + 1, i, 4))
                        if dst:
                            nc.vector.tensor_copy(y, acc[t % 2][:, :]).then_inc(acc_read, 1)
                        else:
                            nc.vector.tensor_tensor(x, x, acc[t % 2][:, :], ALU.add).then_inc(acc_read, 1)
            groups(dve, 2 * units, body)


        GH, GC, CH = 4, 8, 64
        off = [FREE]

        def scratch(name, tiles):
            t = place(name, tiles * S, off[0])
            off[0] += tiles * TILE
            assert off[0] <= TMP
            return t

        gla_kf, gla_q, gla_vf, gla_vtok = (scratch(n, k) for n, k in (("gla_kf", 4), ("gla_q", 4), ("gla_vf", 2), ("gla_vtok", 8)))
        gla_r, gla_o, gla_ktok, gla_s = (scratch(n, k) for n, k in (("gla_r", 8), ("gla_o", 8), ("gla_ktok", 4), ("gla_s", 4)))
        gla_low, gla_reset = scratch("gla_low", 1), gla_vf
        gla_low_, gla_decay = gla_low, place("gla_decay", GH * GC, TMP + 6 * TILE - 4 * GH * GC)
        gla_abs, gla_min, gla_cum, gla_exp0, gla_exp1 = (place(n, S, TMP + k * TILE) for k, n in
                                                         enumerate(("gla_abs", "gla_min", "gla_cum", "gla_exp0", "gla_exp1")))
        gla_exp = [gla_exp0, gla_exp1]
        gla_sq = [place(f"gla_sq{j}", S, FREE + j * TILE) for j in range(2)]
        gla_rs = [place(f"gla_rs{j}", S, FREE + (2 + j) * TILE) for j in range(4)]
        K0, V0, Q0, R0 = 1, 1 + GH, 1 + 3 * GH, 1 + 4 * GH

        g_gate, g_abs, g_soft, g_step, g_diff = (sem("gla_" + n) for n in ("gate_done", "abs_ready", "soft_ready", "dve_step", "diff_ready"))
        g_exp, g_kdec, g_kturned, g_kcopied = (sem("gla_" + n) for n in ("exp_ready", "kdec_ready", "k_turned", "k_copied"))
        g_vturned, g_vcopied, g_reset = (sem("gla_" + n) for n in ("v_turned", "v_copied", "reset_ready"))
        g_kv, g_state, g_odone, g_ocopied = (sem("gla_" + n) for n in ("kv_done", "state_ready", "o_done", "o_copied"))
        g_sq, g_sum, g_ln, g_rs, g_on = (sem("gla_" + n) for n in ("sq_ready", "sum_done", "ln_ready", "rs_ready", "o_normed"))

        def gla_act(act, c):
            u0, t0 = c["u"], c["t"]

            def read(j, out, func=ACT.Copy, scale=1.0, rows=P):
                act.wait_ge(unit_done, u0 + j + 1)
                split_hi(act, u0 + j + 2, None, 0, KD)
                nc.scalar.activation(out, acc[(t0 + j) % 2][0:rows, :], func, scale=scale).then_inc(acc_read, 1)

            def gates(h):
                act.wait_ge(g_diff, h + 1)
                nc.scalar.activation(gla_exp[h % 2][:, :], gla_exp[h % 2][:, :], ACT.Exp,
                                     scale=1 / 16).then_inc(g_exp, 1)
                nc.scalar.activation(gla_decay[:, h * GC:(h + 1) * GC], gla_cum[:, CH - 1:S:CH], ACT.Exp,
                                     scale=1 / 16).then_inc(g_exp, 1)

            log_exp(act)
            read(0, gla_low[0:16, :], rows=16)
            for h in range(GH):
                read(K0 + h, tile(gla_kf, h))
                act.wait_ge(g_gate, h + 1)
                if h:
                    act.wait_ge(g_step, 3 * h - 1)
                nc.scalar.activation(gla_abs[:, :], bank[h % 2][:, :], ACT.Abs, bias=col("gla_b", h)).then_inc(g_abs, 1)
                act.wait_ge(g_abs, h + 1)
                nc.scalar.activation(gla_abs[:, :], gla_abs[:, :], ACT.Exp, scale=-1.0).then_inc(g_soft, 1)
                act.wait_ge(g_soft, 2 * h + 1)
                nc.scalar.activation(gla_abs[:, :], gla_abs[:, :], ACT.Ln, bias=1.0).then_inc(g_soft, 1)
                gates(h)
            for j in range(2 * GH):
                act.wait_ge(g_vturned, j - 1) if j >= 2 else act.wait_ge(g_reset, 2)
                if j == 0:
                    act.wait_ge(g_diff, GH)
                read(V0 + j, tile(gla_vf, j % 2))
            for h in range(GH):
                read(Q0 + h, tile(gla_q, h), scale=P ** -0.5)
            for j in range(2 * GH):
                read(R0 + j, tile(gla_r, j), ACT.Silu)
                if j:
                    gla_o_act(act, j - 1)
            gla_o_act(act, GC - 1)
            for j in range(2 * GH):
                if j >= 2:
                    act.wait_ge(g_sum, j - 1)
                act.wait_ge(g_ocopied, GC)
                nc.scalar.activation(gla_sq[j % 2][:, :], tile(gla_o, j), ACT.Square).then_inc(g_sq, 1)
            log_exp(act)
            for h in range(GH):
                act.wait_ge(g_sum, 2 * h + 2)
                nc.scalar.activation(gla_rs[h][:, :], bank[h][:, :], ACT.Ln, scale=1 / 256,
                                     bias=col("eps")).then_inc(g_ln, 1)
            for h in range(GH):
                act.wait_ge(g_ln, h + 1)
                nc.scalar.activation(gla_rs[h][:, :], gla_rs[h][:, :], ACT.Exp, scale=-0.5).then_inc(g_rs, 1)
            split_high(act, c)

        def gla_o_act(act, n):
            act.wait_ge(g_odone, n + 1)
            nc.scalar.activation(gla_o[:, :].rearrange("p (j t) -> p j t", t=S)[:, :, n * CH:(n + 1) * CH],
                                 bank[4 + n % 2][:, :].rearrange("p (j t) -> p j t", t=CH), ACT.Copy).then_inc(g_ocopied, 1)

        def split_high(act, c):
            for k in range(KD):
                act.wait_ge(hn_ready, c["hn"] + k + 1)
                nc.scalar.activation(tile(HH, k), hn[k % 2][:, :], ACT.Copy).then_inc(hh_ready, 1)

        def gla_dve(dve, c):
            u0, t0 = c["u"], c["t"]

            def lo(j):
                split_lo(dve, u0 + j + 2, None, 0, KD)

            def kdec(h):
                dve.wait_ge(g_exp, 2 * h + 1)
                dve.wait_ge(acc_read, t0 + K0 + h + 1)
                nc.vector.tensor_tensor(tile(gla_kf, h), tile(gla_kf, h), gla_exp[h % 2][:, :], ALU.mult).then_inc(g_kdec, 1)

            lo(0)
            dve.wait_ge(g_reset, 2)
            for h in range(GH):
                lo(K0 + h)
                b = bank[h % 2]
                dve.wait_ge(g_abs, h + 1)
                nc.vector.tensor_scalar(gla_min[:, :], b[:, :], col("gla_b", h), 0.0, ALU.add, ALU.min).then_inc(g_step, 1)
                dve.wait_ge(g_soft, 2 * h + 2)
                dve.wait_ge(g_step, 3 * h + 1)
                nc.vector.tensor_tensor(gla_min[:, :], gla_min[:, :], gla_abs[:, :], ALU.subtract).then_inc(g_step, 1)
                dve.wait_ge(g_step, 3 * h + 2)
                if h:
                    dve.wait_ge(g_exp, 2 * h)
                nc.vector.tensor_tensor_scan(gla_cum[:, :], tile(gla_reset, 0), gla_min[:, :], 0.0, ALU.mult,
                                             ALU.add).then_inc(g_step, 1)
                dve.wait_ge(g_step, 3 * h + 3)
                cum = gla_cum[:, :].rearrange("p (n t) -> p n t", t=CH)
                nc.vector.tensor_tensor(gla_exp[h % 2][:, :].rearrange("p (n t) -> p n t", t=CH),
                                        cum[:, :, CH - 1:CH].to_broadcast([P, GC, CH]), cum,
                                        ALU.subtract).then_inc(g_diff, 1)
                if h:
                    kdec(h - 1)
            for j in range(2 * GH):
                lo(V0 + j)
                if j == 0:
                    kdec(GH - 1)
                turned_v(dve, j - 1) if j else None
            for h in range(GH):
                lo(Q0 + h)
                if h == 0:
                    turned_v(dve, 2 * GH - 1)
                dve.wait_ge(g_kturned, h + 1)
                nc.vector.tensor_copy(tile(gla_ktok, h), bank[2 + h % 2][:, :]).then_inc(g_kcopied, 1)
            for n in range(GC):
                lo(R0 + n)
                for h in range(GH):
                    dve.wait_ge(g_kv, n + 1)
                    if n >= 2:
                        dve.wait_ge(g_odone, n - 1)
                    kv = bank[2 * (n % 2) + h // 2][:, (h % 2) * 256:(h % 2 + 1) * 256]
                    new = gla_s[:, (n % 2) * 1024 + h * 256:(n % 2) * 1024 + (h + 1) * 256]
                    old = gla_s[:, ((n + 1) % 2) * 1024 + h * 256:((n + 1) % 2) * 1024 + (h + 1) * 256]
                    if n == 0:
                        nc.vector.tensor_copy(new, kv).then_inc(g_state, 1)
                    else:
                        dve.wait_ge(g_state, 4 * (n - 1) + h + 1)
                        nc.vector.scalar_tensor_tensor(out=new, in0=old, scalar=gla_decay[:, h * GC + n:h * GC + n + 1],
                                                       in1=kv, op0=ALU.mult, op1=ALU.add).then_inc(g_state, 1)
            for k in range(KD):
                dve.wait_ge(g_rs, k // 2 + 1)
                nc.vector.scalar_tensor_tensor(out=tile(gla_o, k), in0=tile(gla_o, k), scalar=col("gla_gain", k % 2),
                                               in1=gla_rs[k // 2][:, :], op0=ALU.mult, op1=ALU.mult).then_inc(g_on, 1)
                if k >= 2:
                    dve.wait_ge(h_ready, c["h"] + k - 1)
                dve.wait_ge(g_on, k + 1)
                nc.vector.tensor_tensor(hn[k % 2][:, :], tile(gla_o, k), tile(gla_r, k), ALU.mult).then_inc(hn_ready, 1)

        def turned_v(dve, j):
            dve.wait_ge(g_vturned, j + 1)
            nc.vector.tensor_copy(gla_vtok[:, :].rearrange("p (c v) -> p c v", c=4)[:, :, j * P:(j + 1) * P],
                                  bank[4 + j % 2][:, :].rearrange("p (c v) -> p c v", c=4)).then_inc(g_vcopied, 1)

        def gla_pool(pool, c):
            pool.wait_ge(acc_read, c["t"] + 1)
            nc.gpsimd.memset(tile(gla_reset, 0), 1.0).then_inc(g_reset, 1)
            pool.wait_ge(g_reset, 1)
            nc.gpsimd.memset(tile(gla_reset, 0)[:, 0:S:CH], 0.0).then_inc(g_reset, 1)
            norm_pool(pool, c)

        def turn(pe, out, src):
            for k in range(4):
                last = nc.tensor.transpose(out[:, k * P:(k + 1) * P], src[:, k * P:(k + 1) * P], ident)
            return last

        def gla_pe(pe, c):
            u0, t0 = c["u"], c["t"]

            def mult(j, ready=None):
                multiply(pe, u0 + j, t0 + j, None, 0, 0, KD, HH, HL, ready=ready)

            def o_step(n):
                pe.wait_ge(g_state, 4 * n + 4)
                if n >= 2:
                    pe.wait_ge(g_ocopied, n - 1)
                for j in range(2 * GH):
                    last = nc.tensor.matmul(bank[4 + n % 2][:, j * CH:(j + 1) * CH],
                                            gla_s[:, (n % 2) * 1024 + j * P:(n % 2) * 1024 + (j + 1) * P],
                                            tile(gla_q, j // 2)[:, n * CH:(n + 1) * CH], start=True, stop=True)
                last.then_inc(g_odone, 1)

            mult(0, ready=(h_ready, c["h"] - KD))
            for h in range(GH):
                mult(K0 + h)
                pe.wait_ge(acc_read, t0 + 1)
                if h >= 2:
                    pe.wait_ge(g_step, 3 * (h - 2) + 1)
                nc.tensor.matmul(bank[h % 2][:, :], small[0:16, h * P:(h + 1) * P], gla_low[0:16, :],
                                 start=True, stop=True).then_inc(g_gate, 1)
            for j in range(2 * GH):
                mult(V0 + j)
                pe.wait_ge(acc_read, t0 + V0 + j + 1)
                if j >= 2:
                    pe.wait_ge(g_vcopied, j - 1)
                turn(pe, bank[4 + j % 2], tile(gla_vf, j % 2)).then_inc(g_vturned, 1)
            for h in range(GH):
                mult(Q0 + h)
                pe.wait_ge(g_kdec, h + 1)
                if h >= 2:
                    pe.wait_ge(g_kcopied, h - 1)
                turn(pe, bank[2 + h % 2], tile(gla_kf, h)).then_inc(g_kturned, 1)
            for n in range(GC):
                mult(R0 + n)
                pe.wait_ge(g_kcopied, GH)
                pe.wait_ge(g_vcopied, 2 * GH)
                if n >= 2:
                    pe.wait_ge(g_state, 4 * (n - 1))
                lo = CH * (n % 2)
                for h in range(GH):
                    last = nc.tensor.matmul(bank[2 * (n % 2) + h // 2][:, (h % 2) * 256:(h % 2 + 1) * 256],
                                            gla_ktok[lo:lo + CH, h * S + (n // 2) * P:h * S + (n // 2 + 1) * P],
                                            gla_vtok[lo:lo + CH, (n // 2) * D + h * 256:(n // 2) * D + (h + 1) * 256],
                                            start=True, stop=True)
                last.then_inc(g_kv, 1)
                if n:
                    o_step(n - 1)
            o_step(GC - 1)
            for j in range(2 * GH):
                pe.wait_ge(g_sq, j + 1)
                nc.tensor.matmul(bank[j // 2][:, :], ones, gla_sq[j % 2][:, :], start=j % 2 == 0,
                                 stop=j % 2 == 1).then_inc(g_sum, 1)


        off[0] = FREE
        NP, HD = 4, 64
        MH = place("MH", KD * S, off[0], F32R)
        ML = place("ML", KD * S, off[0] + KD * TILE, F32R)
        off[0] += 2 * KD * TILE
        sb_sp, sb_w, sb_vtok, sb_xb = (scratch(n, 4) for n in ("sb_sp", "sb_w", "sb_vtok", "sb_xb"))
        sb_raw, sb_qn, sb_kn, sb_win = (scratch(n, 2) for n in ("sb_raw", "sb_qn", "sb_kn", "sb_win"))
        sb_vf, sb_pooled = sb_w, sb_sp
        b_vturned, b_vcopied, b_win, b_count, b_pooled, b_pool = (sem("sb_" + n) for n in (
            "v_turned", "v_copied", "window_step", "counted", "pooled", "pool_projected"))
        b_sq, b_sum, b_ln, b_rs, b_n = (sem("sb_" + n) for n in ("sq_ready", "sum_done", "ln_ready", "rs_ready", "qk_normed"))
        b_z, b_abs, b_soft, b_sp, b_arg, b_w, b_o = (sem("sb_" + n) for n in (
            "z_done", "act_step", "log_ready", "softplus_ready", "arg_done", "weights_ready", "o_done"))
        b_gain = sem("sb_gain_scaled")
        sb_qgain = place("sb_qgain", 1, TMP - 32)

        def span(kb):
            return slice(kb * P, S)

        def sb_act(act, c):
            u0, t0 = c["u"], c["t"]

            def read(j, out):
                act.wait_ge(unit_done, u0 + j + 1)
                split_hi(act, u0 + j + 2, None, 0, KD)
                nc.scalar.activation(out, acc[(t0 + j) % 2][:, :], ACT.Copy).then_inc(acc_read, 1)

            def high(k):
                act.wait_ge(hn_ready, c["hn"] + k + 1)
                nc.scalar.activation(tile(MH, k), hn[k % 2][:, :], ACT.Copy).then_inc(hh_ready, 1)

            def read_qk(m):
                if m >= 2:
                    act.wait_ge(b_n, m - 1)
                if m == 0:
                    act.wait_ge(b_win, 20)
                read(8 + m, tile(sb_raw, m % 2))
                act.wait_ge(acc_read, t0 + 8 + m + 1)
                if m:
                    act.wait_ge(b_sum, m)
                nc.scalar.activation(sq[0][:, :], tile(sb_raw, m % 2), ACT.Square).then_inc(b_sq, 1)

            def rms_qk(m):
                act.wait_ge(b_sum, m + 1)
                if m:
                    act.wait_ge(b_n, m)
                nc.scalar.activation(ln[:, :], bank[5][:, :], ACT.Ln, scale=1 / HD, bias=col("eps")).then_inc(b_ln, 1)
                act.wait_ge(b_ln, m + 1)
                nc.scalar.activation(rs[:, :], ln[:, :], ACT.Exp, scale=-0.5).then_inc(b_rs, 1)

            nc.scalar.activation(sb_qgain[:, :], col("sb_gain"), ACT.Copy, scale=HD ** -0.5).then_inc(b_gain, 1)
            for j in range(4):
                if j >= 2:
                    act.wait_ge(b_vturned, j - 1)
                read(j, tile(sb_vf, j % 2))
            for j in range(4):
                read(4 + j, tile(sb_xb, j))
            log_exp(act)
            read_qk(0)
            rms_qk(0)
            high(0)
            high(1)
            read_qk(1)
            rms_qk(1)
            high(2)
            high(3)
            for h in range(2 * NP):
                for kb in (3, 2, 1, 0):
                    step = 8 * h + 2 * (3 - kb)
                    a = tile(sb_sp, kb)[:, span(kb)]
                    act.wait_ge(b_z, 4 * h + 4 - kb)
                    nc.scalar.activation(a, bank[kb][:, span(kb)], ACT.Abs).then_inc(b_abs, 1)
                    act.wait_ge(b_abs, step + 1)
                    nc.scalar.activation(a, a, ACT.Exp, scale=-1.0).then_inc(b_abs, 1)
                    act.wait_ge(b_abs, step + 2)
                    nc.scalar.activation(a, a, ACT.Ln, bias=1.0).then_inc(b_soft, 1)
                if h < 6:
                    read_qk(2 + h)
                for kb in (3, 2, 1, 0):
                    act.wait_ge(b_arg, 4 * h + 4 - kb)
                    if h:
                        act.wait_ge(b_o, h)
                    nc.scalar.activation(tile(sb_w, kb)[:, span(kb)], bank[kb][:, span(kb)], ACT.Exp).then_inc(b_w, 1)
                if h < 6:
                    rms_qk(2 + h)
                if h % 2 == 0 and h:
                    high(4 + h // 2 - 1)
            high(7)

        def log_exp(act):
            nc.scalar.preload_act_table_set("natural_log_exp_and_others")

        def sb_dve(dve, c):
            u0, t0 = c["u"], c["t"]

            def lo(j):
                split_lo(dve, u0 + j + 2, None, 0, KD)

            def turned(j):
                dve.wait_ge(b_vturned, j + 1)
                nc.vector.tensor_copy(sb_vtok[:, :].rearrange("p (c v) -> p c v", c=4)[:, :, j * P:(j + 1) * P],
                                      bank[j % 2][:, :].rearrange("p (c v) -> p c v", c=4)).then_inc(b_vcopied, 1)

            def to_hn(k, wait, src, scalar):
                dve.wait_ge(*wait)
                if k >= 2:
                    dve.wait_ge(h_ready, c["h"] + k - 1)
                nc.vector.tensor_scalar(hn[k % 2][:, :], src, scalar, None, ALU.mult).then_inc(hn_ready, 1)

            def pooled(g):
                dve.wait_ge(b_win, 2 * (g + 1) + g * (g + 1))
                w, win = 2 << g, tile(sb_win, g % 2)
                nc.vector.tensor_tensor(win[:, 0:16], win[:, 0:16], col("pool_count", 16 * g, 16), ALU.mult).then_inc(b_count, 1)
                dve.wait_ge(b_count, g + 1)
                if g >= 2:
                    dve.wait_ge(b_pool, g - 1)
                nc.vector.scalar_tensor_tensor(out=tile(sb_pooled, g % 2), in0=win, scalar=1.0 / w, in1=tile(sb_xb, g),
                                               op0=ALU.mult, op1=ALU.subtract).then_inc(b_pooled, 1)

            def normed(m):
                dve.wait_ge(b_rs, m + 1)
                dst = tile((sb_qn, sb_kn)[m % 2], m // 2 % 2)
                if m >= 4:
                    dve.wait_ge(b_arg, 8 * (m // 2 - 1))
                gain = sb_qgain[:, 0:1] if m % 2 == 0 else col("sb_gain", 1)
                nc.vector.scalar_tensor_tensor(out=dst, in0=tile(sb_raw, m % 2), scalar=gain,
                                               in1=rs[:, :], op0=ALU.mult, op1=ALU.mult).then_inc(b_n, 1)

            for j in range(4):
                lo(j)
                turned(j - 1) if j else None
            for j in range(4):
                lo(4 + j)
                turned(3) if j == 0 else None
                if j:
                    pooled(j - 1)
                if j >= 2:
                    to_hn(j - 2, (b_pool, j - 1), bank[2 + j % 2][:, :], col("pool_scale", j - 2))
            dve.wait_ge(b_gain, 1)
            lo(8)
            pooled(3)
            normed(0)
            to_hn(2, (b_pool, 3), bank[2][:, :], col("pool_scale", 2))
            lo(9)
            normed(1)
            to_hn(3, (b_pool, 4), bank[3][:, :], col("pool_scale", 3))
            for h in range(2 * NP):
                for kb in (3, 2, 1, 0):
                    a = tile(sb_sp, kb)[:, span(kb)]
                    dve.wait_ge(b_soft, 4 * h + 4 - kb)
                    nc.vector.scalar_tensor_tensor(out=a, in0=bank[kb][:, span(kb)], scalar=0.0, in1=a,
                                                   op0=ALU.max, op1=ALU.add).then_inc(b_sp, 1)
                if h < 6:
                    lo(10 + h)
                if h % 2 == 0 and h:
                    to_hn(4 + h // 2 - 1, (b_o, h), bank[4][:, :], 1.0)
                if h < 6:
                    normed(2 + h)
            to_hn(7, (b_o, 8), bank[4][:, :], 1.0)

        def sb_pool(pool, c):
            step = 0
            for g in range(4):
                src, win = tile(sb_xb, g), tile(sb_win, g % 2)
                pool.wait_ge(acc_read, c["t"] + 4 + g + 1)
                for d in range(g + 1):
                    sh, dst = 1 << d, win if (g - d) % 2 == 0 else tile(sb_raw, 0)
                    if g >= 2 and d <= 1:
                        pool.wait_ge(b_pooled, g - 1)
                    if step:
                        pool.wait_ge(b_win, step)
                    nc.gpsimd.tensor_copy(dst[:, 0:sh], src[:, 0:sh]).then_inc(b_win, 1)
                    nc.gpsimd.tensor_tensor(dst[:, sh:S], src[:, sh:S], src[:, 0:S - sh], ALU.add).then_inc(b_win, 1)
                    src, step = dst, step + 2
            for k in range(KD):
                pool.wait_ge(hh_ready, c["h"] + k + 1)
                nc.gpsimd.tensor_tensor(tile(ML, k), hn[k % 2][:, :], tile(MH, k).bitcast(F32),
                                        ALU.subtract).then_inc(h_ready, 1)

        def sb_pe(pe, c):
            u0, t0 = c["u"], c["t"]

            def mult(j, ready=None):
                multiply(pe, u0 + j, t0 + j, None, 0, 0, KD, HH, HL, ready=ready)

            def project_pool(g):
                pe.wait_ge(b_pooled, g + 1)
                if g >= 2:
                    pe.wait_ge(hn_ready, c["hn"] + g - 1)
                nc.tensor.matmul(bank[2 + g % 2][:, :], small[:, S + g * P:S + (g + 1) * P], tile(sb_pooled, g % 2),
                                 start=True, stop=True).then_inc(b_pool, 1)

            def sum_qk(m):
                pe.wait_ge(b_sq, m + 1)
                if m:
                    pe.wait_ge(b_ln, m)
                nc.tensor.matmul(bank[5][:, :], halves, sq[0][:, :], start=True, stop=True).then_inc(b_sum, 1)

            def scores(h):
                i, r = h // 2, slice(HD * (h % 2), HD * (h % 2) + HD)
                if h % 2 == 0:
                    pe.wait_ge(b_n, 2 * i + 2)
                if h == 0:
                    pe.wait_ge(hn_ready, c["hn"] + 4)
                for kb in (3, 2, 1, 0):
                    if h:
                        pe.wait_ge(b_w, 4 * h - kb)
                    nc.tensor.matmul(bank[kb][:, span(kb)], tile(sb_kn, i % 2)[r, kb * P:(kb + 1) * P],
                                     tile(sb_qn, i % 2)[r, span(kb)], start=True, stop=False, skip_group_check=True)
                    nc.tensor.matmul(bank[kb][:, kb * P:(kb + 1) * P], ident, hidden, start=False, stop=True,
                                     skip_group_check=True).then_inc(b_z, 1)

            def sums(h):
                for kb in (3, 2, 1, 0):
                    pe.wait_ge(b_sp, 4 * h + 4 - kb)
                    last = nc.tensor.matmul(bank[kb][:, span(kb)], neg_lower, tile(sb_sp, kb)[:, span(kb)],
                                            start=False, stop=kb == 3, skip_group_check=True)
                    for jb in range(kb + 1, 4):
                        last = nc.tensor.matmul(bank[kb][:, span(jb)], neg_ones, tile(sb_sp, jb)[:, span(jb)],
                                                start=False, stop=jb == 3, skip_group_check=True)
                    last.then_inc(b_arg, 1)

            def values(h):
                r = slice(HD * (h % 2), HD * (h % 2) + HD)
                pe.wait_ge(b_w, 4 * h + 4)
                if h and h % 2 == 0:
                    pe.wait_ge(hn_ready, c["hn"] + 4 + h // 2)
                for kb in range(4):
                    last = nc.tensor.matmul(bank[4][r, span(kb)], sb_vtok[:, kb * S + h * HD:kb * S + (h + 1) * HD],
                                            tile(sb_w, kb)[:, span(kb)], start=kb == 0, stop=kb == 3)
                last.then_inc(b_o, 1)

            for j in range(4):
                mult(j, ready=(h_ready, c["h"] - KD) if j == 0 else None)
                pe.wait_ge(acc_read, t0 + j + 1)
                if j >= 2:
                    pe.wait_ge(b_vcopied, j - 1)
                turn(pe, bank[j % 2], tile(sb_vf, j % 2)).then_inc(b_vturned, 1)
            for j in range(4):
                mult(4 + j)
                if j >= 2:
                    project_pool(j - 2)
            mult(8)
            project_pool(2)
            sum_qk(0)
            mult(9)
            sum_qk(1)
            project_pool(3)
            for h in range(2 * NP):
                if h == 0:
                    pe.wait_ge(b_vcopied, 4)
                scores(h)
                if h:
                    values(h - 1)
                if h < 6:
                    mult(10 + h)
                sums(h)
                if h < 6:
                    sum_qk(2 + h)
            values(7)


        NC, NH = S // P, 8
        off[0] = FREE

        def scratch1(name, n, dt=F32):
            t = place(name, n * S, off[0], dt)
            off[0] += n * TILE
            assert off[0] <= FREE + 32 * TILE
            return t

        O = place("O", 16 * S, FREE + 32 * TILE)
        OH = place("OH", 8 * S, FREE, F32R)
        OL = place("OL", 8 * S, FREE + 16 * TILE, F32R)
        Y1 = place("Y1", 8 * S, FREE + 32 * TILE)
        tab0 = FREE + 48 * TILE
        t_soft, t_ld, t_exp, t_nbe, t_beta, t_neg = (place(n, k, tab0 + 4 * o) for n, k, o in (
            ("t_soft", 128, 0), ("t_ld", 96, 128), ("t_exp", 288, 224), ("t_nbe", 32, 512), ("t_beta", 32, 544),
            ("t_neg", 24, 576)))
        conv_out = scratch1("conv_out", 4)
        l_qt, l_kt, l_qd, l_gb, l_u, l_ed, l_edt, l_a, l_qk, l_vb, l_kd = (scratch1("l_" + n, 1) for n in (
            "qt", "kt", "qd", "gb", "u", "ed", "edt", "a", "qk", "vb", "kd"))
        l_m = [scratch1(f"l_m{j}", 1) for j in range(2)]
        l_x, l_xt, l_yt, l_small, l_z, l_t = (scratch1("l_" + n, 1) for n in ("x", "xt", "yt", "small", "z", "t"))
        l_rs = [scratch1(f"l_rs{j}", 1) for j in range(2)]
        l_sq = [scratch1(f"l_sq{j}", 1) for j in range(2)]
        small1 = place("small1", 256, FREE + 28 * TILE)
        small1_hi = place("small1_hi", 256, FREE + 29 * TILE, F32R)
        small1_lo = place("small1_lo", 256, FREE + 30 * TILE, F32R)
        l_r, l_vn, l_s = l_small[:, 0:P], None, [l_small[:, 3 * P:4 * P], None]
        l_vn = [l_small[:, P:2 * P], l_small[:, 2 * P:3 * P]]
        l_state = l_small[:, 3 * P:4 * P]

        def chunk(t, k):
            return t[:, k * P:(k + 1) * P]

        def by_chunk(t):
            return t[:, :].rearrange("p (c n) -> p c n", c=NC)

        def each_chunk(m):
            return m.unsqueeze(1).to_broadcast([P, NC, P])

        def head_of(table, cols_, base, h0, i):
            v = table[:, base:base + NC * cols_].rearrange("p (c n) -> p c n", c=NC)
            v = v[:, :, h0:h0 + 1] if i is None else v[:, :, bass.ds(i + h0, 1)]
            return v.to_broadcast([P, NC, P])

        def head_col(table, k, h0, i):
            return table[:, k + h0:k + h0 + 1] if i is None else table[:, bass.ds(i + (k + h0), 1)]

        a_small, a_steps, a_pe, a_dve = sem("small1_in"), sem("tables_act"), sem("tables_pe"), sem("tables_dve")

        def tables_act(act, c):
            act.wait_ge(a_small, 16)
            nc.scalar.activation(small1_hi[:, :], small1[:, :], ACT.Copy).then_inc(a_steps, 1)
            nc.scalar.activation(t_neg[:, :], col("rows", 24, 24), ACT.Exp).then_inc(a_steps, 1)
            act.wait_ge(a_dve, 3)
            nc.scalar.activation(l_t[:, 0:128], l_a[:, 0:128], ACT.Abs).then_inc(a_steps, 1)
            act.wait_ge(a_steps, 3)
            nc.scalar.activation(l_t[:, 0:128], l_t[:, 0:128], ACT.Exp, scale=-1.0).then_inc(a_steps, 1)
            act.wait_ge(a_steps, 4)
            nc.scalar.activation(l_t[:, 0:128], l_t[:, 0:128], ACT.Ln, bias=1.0).then_inc(a_steps, 1)
            act.wait_ge(a_dve, 4)
            beta = t_beta[:, :].rearrange("p (c n) -> p c n", c=NC)
            nc.scalar.activation(beta, by_chunk(t_soft)[:, :, 0:8], ACT.Exp, scale=-1.0).then_inc(a_steps, 1)

        def sums_exp_act(act):
            act.wait_ge(a_pe, 4)
            nc.scalar.activation(t_exp[:, :], bank[1][:, 0:288], ACT.Exp).then_inc(a_steps, 1)

        def tables_dve(dve, c):
            dve.wait_ge(a_steps, 1)
            nc.vector.tensor_tensor(small1_lo[:, :], small1[:, :], small1_hi[:, :].bitcast(F32), ALU.subtract).then_inc(a_dve, 1)
            dve.wait_ge(a_pe, 1)
            arg, ps = l_a[:, 0:128].rearrange("p (c n) -> p c n", c=NC), bank[0][:, 0:128].rearrange("p (c n) -> p c n", c=NC)
            nc.vector.tensor_scalar(arg[:, :, 0:8], ps[:, :, 0:8], -1.0, None, ALU.mult).then_inc(a_dve, 1)
            nc.vector.tensor_tensor(arg[:, :, 8:32], ps[:, :, 8:32],
                                    col("rows", 0, 24).unsqueeze(1).to_broadcast([P, NC, 24]), ALU.add).then_inc(a_dve, 1)
            dve.wait_ge(a_steps, 5)
            dve.wait_ge(a_dve, 3)
            nc.vector.scalar_tensor_tensor(out=t_soft[:, :], in0=l_a[:, 0:128], scalar=0.0, in1=l_t[:, 0:128],
                                           op0=ALU.max, op1=ALU.add).then_inc(a_dve, 1)
            dve.wait_ge(a_dve, 4)
            nc.vector.scalar_tensor_tensor(out=t_ld[:, :].rearrange("p (c n) -> p c n", c=NC),
                                           in0=by_chunk(t_soft)[:, :, 8:32], scalar=-1.0,
                                           in1=t_neg[:, :].unsqueeze(1).to_broadcast([P, NC, 24]),
                                           op0=ALU.mult, op1=ALU.mult).then_inc(a_dve, 1)

        def beta_exp_dve(dve):
            dve.wait_ge(a_steps, 7)
            eg = t_exp[:, 0:96].rearrange("p (c n) -> p c n", c=NC)[:, :, 0:8]
            nc.vector.scalar_tensor_tensor(out=t_nbe[:, :].rearrange("p (c n) -> p c n", c=NC), in0=eg, scalar=-1.0,
                                           in1=t_beta[:, :].rearrange("p (c n) -> p c n", c=NC),
                                           op0=ALU.mult, op1=ALU.mult).then_inc(a_dve, 1)

        def tables_pe(pe, c):
            pe.wait_ge(a_dve, 1)
            pe.wait_ge(h_ready, c["h"])
            for k in range(NC):
                for d in range(KD):
                    w = slice(32 * d, 32 * d + 32)
                    x, y = chunk(tile(HH, d), k), chunk(tile(HL, d), k)
                    o = bank[0][:, 32 * k:32 * k + 32]
                    nc.tensor.matmul(o, x, small1_hi[:, w], start=d == 0, stop=False)
                    nc.tensor.matmul(o, x, small1_lo[:, w], start=False, stop=False)
                    last = nc.tensor.matmul(o, y, small1_hi[:, w], start=False, stop=d == KD - 1)
            last.then_inc(a_pe, 1)

        def chunk_sums_pe(pe):
            pe.wait_ge(a_dve, 5)
            for k, m in enumerate((upper, ones, lower)):
                nc.tensor.matmul(bank[1][:, 96 * k:96 * k + 96], m, t_ld[:, :], start=True, stop=True).then_inc(a_pe, 1)

        c_tap, c_step, c_silu, c_free = sem("l_tap_ready"), sem("l_conv_step"), sem("l_silu_ready"), sem("l_slot_free")

        class Slots:

            def __init__(self, c, h0, i, u, t, cols_, taps_):
                self.c, self.i, self.h0 = c, i, h0
                self.u, self.t, self.cols, self.taps = u, t, cols_, taps_

        def slots(c, h0, i=None):
            return Slots(c, h0, i, c["u"] + 4 * h0, c["t"] + 4 * h0,
                         cols.start["conv"] + 15 * h0 if h0 < NH else cols.start["ssd_conv"], 3 if h0 < NH else 4)

        def conv_col(s, j, m):
            k = s.cols + 5 * j + m
            return par[:, k:k + 1] if s.i is None else par[:, bass.ds(s.i * 15 + k, 1)]

        def slot_act(act, s, j):
            act.wait_ge(unit_done, at(s.u + j + 1, s.i, 4))
            split_hi(act, s.u + j + 2, s.i, 4, KD)
            if j < s.taps:
                if s.h0:
                    act.wait_ge(*[(c_qt, at(s.h0, s.i, 1)), (c_kt, at(s.h0, s.i, 1)), (p_vt, at(s.h0, s.i, 1)),
                                  (g_z, at(s.h0, s.i, 1))][j])
                nc.scalar.activation(tile(conv_out, j), acc[(s.t + j) % 2][:, :], ACT.Identity, scale=conv_col(s, j, 3),
                                     bias=conv_col(s, j, 4)).then_inc(c_tap, 1)

        def slot_lo(dve, s, j):
            split_lo(dve, s.u + j + 2, s.i, 4, KD)

        def slot_tap(dve, s, j, m):
            a, o = acc[(s.t + j) % 2], tile(conv_out, j)
            if j >= s.taps:
                if m == 3:
                    dve.wait_ge(unit_done, at(s.u + j + 1, s.i, 4))
                    if s.h0:
                        dve.wait_ge(g_z, at(s.h0, s.i, 1))
                    nc.vector.tensor_copy(o, a[:, :]).then_inc(acc_read, 1)
                return
            step = 2 * (3 * s.h0 + j)
            if m == 1:
                dve.wait_ge(c_tap, at(3 * s.h0 + j + 1, s.i, 3))
            else:
                dve.wait_ge(c_step, at(step + m - 1, s.i, 6))
            nc.vector.scalar_tensor_tensor(out=o[:, m:S], in0=a[:, 0:S - m], scalar=conv_col(s, j, 3 - m), in1=o[:, m:S],
                                           op0=ALU.mult, op1=ALU.add).then_inc(acc_read if m == 3 else c_step, 1)

        def slot_silu(act, s):
            for j in range(4):
                act.wait_ge(acc_read, at(s.t + j + 1, s.i, 4))
                nc.scalar.activation(tile(conv_out, j), tile(conv_out, j), ACT.Silu).then_inc(c_silu, 1)

        def slot_pe(pe, s, j, part=None):
            multiply(pe, s.u + j, s.t + j, s.i, 4, 4, KD, HH, HL, part=part)

        g_gb, g_u, g_etm, g_qd, g_m, g_x0, g_z, g_o = (sem("l_" + n) for n in (
            "gb_ready", "u_ready", "edt_masked", "qd_ready", "m_ready", "x0_ready", "z_kept", "o_ready"))
        s_sq, s_ln, s_rs, s_egb, s_ed, s_edt, s_yt, s_vn = (sem("l_" + n) for n in (
            "sq_ready", "ln_ready", "rs_ready", "egb_ready", "ed_ready", "edt_ready", "yt_copied", "vn_copied"))
        p_sum, p_gcb, p_d, p_dt, p_vt, p_kk, p_qk, p_kt, p_m0t = (sem("l_" + n) for n in (
            "sum_done", "gcb_done", "d_done", "dt_done", "v_turned", "kk_done", "qk_done", "k_turned", "m0_turned"))
        p_yt, p_xyt, p_xy, p_p1, p_vn, p_s, p_o = (sem("l_" + n) for n in (
            "yt_done", "xyt_done", "xy_done", "p1_done", "vn_done", "s_done", "o_done"))
        c_qt, c_kt, c_vb, c_a, c_qk, c_kd, c_xt, c_x, c_r, c_st, c_t = (sem("l_" + n) for n in (
            "qt_ready", "kt_ready", "vb_ready", "a_ready", "qk_ready", "kd_ready", "xt_ready", "x_ready", "r_ready",
            "state_ready", "t_ready"))

        def gdn_act(act, s, h0, i):
            def n(base, per=1):
                return at(base + per * h0, i, per)

            def rms(k, width, src, out):
                act.wait_ge(p_sum, n(k + 1, 3))
                nc.scalar.activation(out[:, :], src[:, :], ACT.Ln, scale=1.0 / width, bias=col("eps")).then_inc(s_ln, 1)
                act.wait_ge(s_ln, n(k + 1, 3))
                nc.scalar.activation(out[:, :], out[:, :], ACT.Exp, scale=-0.5).then_inc(s_rs, 1)

            def copy_vn(k):
                act.wait_ge(p_vn, n(k + 1, 4))
                nc.scalar.activation(l_vn[k % 2], bank[0][:, P:2 * P], ACT.Copy).then_inc(s_vn, 1)

            log_exp(act)
            for done, b, out, ready in ((p_gcb, 2, l_gb, s_egb), (p_d, 3, l_ed, s_ed), (p_dt, 4, l_edt, s_edt)):
                act.wait_ge(done, n(1))
                nc.scalar.activation(out[:, :], bank[b][:, :], ACT.Exp).then_inc(ready, 1)
            for k in range(2):
                act.wait_ge(c_silu, n(k + 1, 4))
                nc.scalar.activation(l_sq[k][:, :], tile(conv_out, k), ACT.Square).then_inc(s_sq, 1)
            for k in range(2):
                rms(k, 1.0, bank[k], l_rs[k])
            slot_act(act, s, 0)
            for l in range(1, 7):
                act.wait_ge(p_yt, n(l, 6))
                nc.scalar.activation(l_yt[:, :], bank[4][:, :], ACT.Copy).then_inc(s_yt, 1)
                if l == 4:
                    slot_act(act, s, 1)
            copy_vn(0)
            slot_act(act, s, 2)
            for k in range(1, NC):
                copy_vn(k)
            act.wait_ge(p_o, n(1))
            nc.scalar.activation(l_sq[0][:, :], bank[2][:, :], ACT.Square).then_inc(s_sq, 1)
            slot_act(act, s, 3)
            rms(2, P, bank[3], l_rs[0])
            slot_silu(act, s)

        def gdn_dve(dve, s, h0, i):
            def n(base, per=1):
                return at(base + per * h0, i, per)

            dve.wait_ge(s_rs, n(1, 3))
            nc.vector.scalar_tensor_tensor(out=l_qt[:, :], in0=tile(conv_out, 0), scalar=P ** -0.5, in1=l_rs[0][:, :],
                                           op0=ALU.mult, op1=ALU.mult).then_inc(c_qt, 1)
            dve.wait_ge(s_rs, n(2, 3))
            nc.vector.tensor_tensor(l_kt[:, :], tile(conv_out, 1), l_rs[1][:, :], ALU.mult).then_inc(c_kt, 1)
            dve.wait_ge(p_vt, n(1))
            nc.vector.tensor_tensor(by_chunk(l_vb), by_chunk(bank[5]), head_of(t_beta, 8, 0, h0, i), ALU.mult).then_inc(c_vb, 1)
            dve.wait_ge(p_kk, n(1))
            dve.wait_ge(s_ed, n(1))
            for k in range(NC):
                last = nc.vector.scalar_tensor_tensor(out=chunk(l_a, k), in0=chunk(bank[0], k),
                                                      scalar=head_col(t_beta, 8 * k, h0, i), in1=chunk(l_ed, k),
                                                      op0=ALU.mult, op1=ALU.mult)
            last.then_inc(c_a, 1)
            dve.wait_ge(p_qk, n(1))
            dve.wait_ge(g_etm, n(1))
            nc.vector.tensor_tensor(l_qk[:, :], bank[1][:, :], l_edt[:, :], ALU.mult).then_inc(c_qk, 1)
            dve.wait_ge(p_kt, n(1))
            nc.vector.tensor_tensor(by_chunk(l_kd), by_chunk(bank[2]), head_of(t_exp, 24, 192, h0, i), ALU.mult).then_inc(c_kd, 1)
            dve.wait_ge(p_m0t, n(1))
            nc.vector.tensor_tensor(by_chunk(l_xt), each_chunk(ident), by_chunk(bank[3]), ALU.subtract).then_inc(c_xt, 1)
            slot_lo(dve, s, 0)

            def stream(k):
                slot_tap(dve, s, k // 4, k % 4) if k % 4 else slot_lo(dve, s, k // 4)

            for l in range(1, 7):
                dve.wait_ge(p_xyt, n(l, 6))
                dve.wait_ge(c_xt, n(l, 7))
                nc.vector.tensor_tensor(l_xt[:, :], l_xt[:, :], bank[5][:, :], ALU.subtract).then_inc(c_xt, 1)
                if l < 6:
                    dve.wait_ge(p_xy, n(l, 5))
                    dve.wait_ge(g_x0, n(1)) if l == 1 else dve.wait_ge(c_x, n(l - 1, 5))
                    nc.vector.tensor_tensor(l_x[:, :], l_x[:, :], bank[3][:, :], ALU.subtract).then_inc(c_x, 1)
                stream(l)
            stream(7)

            def state(k):
                dve.wait_ge(p_s, n(k + 1, 3))
                if k == 0:
                    nc.vector.tensor_copy(l_state, bank[1][:, 0:P]).then_inc(c_st, 1)
                else:
                    dve.wait_ge(c_st, n(k, 3))
                    nc.vector.scalar_tensor_tensor(out=l_state, in0=l_state, scalar=head_col(t_exp, 96 + 24 * k, h0, i),
                                                   in1=bank[1][:, 0:P], op0=ALU.mult, op1=ALU.add).then_inc(c_st, 1)

            def rest(k):
                dve.wait_ge(p_p1, n(k, 3))
                nc.vector.scalar_tensor_tensor(out=l_r, in0=bank[0][:, 0:P], scalar=head_col(t_nbe, 8 * k, h0, i),
                                               in1=chunk(l_vb, k), op0=ALU.mult, op1=ALU.add).then_inc(c_r, 1)

            state(0)
            rest(1)
            state(1)
            stream(8)
            rest(2)
            state(2)
            stream(9)
            rest(3)
            for k in range(10, 16):
                stream(k)
            dve.wait_ge(s_rs, n(3, 3))
            if i is not None or h0:
                dve.wait_ge(g_o, n(0))
            nc.vector.scalar_tensor_tensor(out=l_t[:, :], in0=bank[2][:, :], scalar=col("gdn_norm"), in1=l_rs[0][:, :],
                                           op0=ALU.mult, op1=ALU.mult).then_inc(c_t, 1)

        def decays_pool(pool, h0, i):
            pool.wait_ge(p_gcb, at(h0, i, 1)) if h0 or i is not None else None
            if h0 or i is not None:
                pool.wait_ge(g_qd, at(h0, i, 1))
                pool.wait_ge(p_dt, at(h0, i, 1))
            nc.gpsimd.tensor_tensor(by_chunk(l_gb), head_of(t_ld, 24, 0, h0, i), each_chunk(ones), ALU.mult).then_inc(g_gb, 1)
            nc.gpsimd.tensor_tensor(by_chunk(l_u), head_of(t_ld, 24, 0, h0, i), each_chunk(lower), ALU.mult).then_inc(g_u, 1)

        def gdn_pool(pool, s, h0, i):
            def n(base, per=1):
                return at(base + per * h0, i, per)

            def mask(l):
                if l >= 2:
                    pool.wait_ge(p_m0t, n(1)) if l == 2 else pool.wait_ge(p_yt, n(l - 2, 6))
                nc.gpsimd.tensor_tensor(by_chunk(l_m[l % 2]), by_chunk(l_a), each_chunk(level[l]), ALU.mult).then_inc(g_m, 1)

            pool.wait_ge(s_edt, n(1))
            nc.gpsimd.tensor_tensor(by_chunk(l_edt), by_chunk(l_edt), each_chunk(upper), ALU.mult).then_inc(g_etm, 1)
            pool.wait_ge(c_a, n(1))
            mask(0)
            mask(1)
            pool.wait_ge(g_m, n(1, 7))
            nc.gpsimd.tensor_tensor(by_chunk(l_x), each_chunk(ident), by_chunk(l_m[0]), ALU.subtract).then_inc(g_x0, 1)
            pool.wait_ge(g_x0, n(1))
            mask(2)
            pool.wait_ge(c_qt, n(1))
            pool.wait_ge(s_egb, n(1))
            nc.gpsimd.tensor_tensor(l_qd[:, :], l_qt[:, :], l_gb[:, :], ALU.mult).then_inc(g_qd, 1)
            pool.wait_ge(c_silu, n(4, 4))
            if h0 or i is not None:
                pool.wait_ge(g_o, n(0))
            nc.gpsimd.tensor_tensor(by_chunk(l_z), tile(conv_out, 3).rearrange("p (c n) -> p c n", c=NC),
                                    each_chunk(ones), ALU.mult).then_inc(g_z, 1)
            for l in range(3, 7):
                mask(l)
            if s.taps == 3:
                decays_pool(pool, h0 + 1, i)
            pool.wait_ge(c_t, n(1))
            pool.wait_ge(g_z, n(1))
            nc.gpsimd.tensor_tensor(tile(O, h0) if i is None else O[:, bass.ds(i * S + h0 * S, S)], l_t[:, :], l_z[:, :],
                                    ALU.mult).then_inc(g_o, 1)

        def gdn_pe(pe, s, h0, i):
            def n(base, per=1):
                return at(base + per * h0, i, per)

            def four(out, lhs, rhs):
                for k in range(NC):
                    last = nc.tensor.matmul(chunk(out, k), chunk(lhs, k) if lhs is not upper else upper,
                                            chunk(rhs, k) if rhs is not upper and rhs is not ident else rhs, start=True, stop=True)
                return last

            pe.wait_ge(g_gb, n(1))
            if h0 or i is not None:
                pe.wait_ge(c_t, n(0))
            four(bank[2], l_gb, upper).then_inc(p_gcb, 1)
            pe.wait_ge(g_u, n(1))
            nc.tensor.matmul(bank[3][:, :], upper, l_u[:, :], start=True, stop=True).then_inc(p_d, 1)
            four(bank[4], l_u, upper).then_inc(p_dt, 1)
            slot_pe(pe, s, 0, 0)
            for k in range(2):
                pe.wait_ge(s_sq, n(k + 1, 3))
                nc.tensor.matmul(bank[k][:, :], ones, l_sq[k][:, :], start=True, stop=True).then_inc(p_sum, 1)
            pe.wait_ge(c_silu, n(3, 4))
            turn(pe, bank[5], tile(conv_out, 2)).then_inc(p_vt, 1)
            slot_pe(pe, s, 0, 1)
            pe.wait_ge(c_kt, n(1))
            four(bank[0], l_kt, l_kt).then_inc(p_kk, 1)
            pe.wait_ge(c_qt, n(1))
            four(bank[1], l_kt, l_qt).then_inc(p_qk, 1)
            pe.wait_ge(s_egb, n(1))
            turn(pe, bank[2], l_kt).then_inc(p_kt, 1)
            slot_pe(pe, s, 0, 2)
            pe.wait_ge(g_m, n(1, 7))
            four(bank[3], l_m[0], ident).then_inc(p_m0t, 1)
            slot_pe(pe, s, 0, 3)
            pe.wait_ge(s_edt, n(1))
            pe.wait_ge(c_vb, n(1))
            for l in range(1, 7):
                pe.wait_ge(g_m, n(l + 1, 7))
                pe.wait_ge(c_xt, n(l, 7))
                four(bank[4], l_m[l % 2], l_xt).then_inc(p_yt, 1)
                slot_pe(pe, s, *divmod(l + 3, 4))
                pe.wait_ge(s_yt, n(l, 6))
                pe.wait_ge(g_x0, n(1)) if l == 1 else pe.wait_ge(c_x, n(l - 1, 5))
                four(bank[5], l_x, l_yt).then_inc(p_xyt, 1)
                if l < 6:
                    four(bank[3], l_yt, l_x).then_inc(p_xy, 1)
            pe.wait_ge(c_qk, n(1))
            pe.wait_ge(c_kd, n(1))
            pe.wait_ge(g_qd, n(1))
            for k in range(NC):
                if k:
                    pe.wait_ge(c_st, n(k, 3))
                    nc.tensor.matmul(bank[0][:, 0:P], chunk(l_kt, k), l_state, start=True, stop=True).then_inc(p_p1, 1)
                    slot_pe(pe, s, *divmod(11 + k, 4))
                    pe.wait_ge(c_r, n(k, 3))
                else:
                    pe.wait_ge(c_xt, n(7, 7))
                nc.tensor.matmul(bank[0][:, P:2 * P], chunk(l_xt, k), l_r if k else chunk(l_vb, 0), start=True,
                                 stop=True).then_inc(p_vn, 1)
                if k == 0:
                    slot_pe(pe, s, 2, 2)
                pe.wait_ge(s_vn, n(k + 1, 4))
                if k < NC - 1 and k:
                    nc.tensor.matmul(chunk(bank[2], k), l_state, chunk(l_qd, k), start=True, stop=False, skip_group_check=True)
                if k < NC - 1:
                    nc.tensor.matmul(bank[1][:, 0:P], chunk(l_kd, k), l_vn[k % 2], start=True, stop=True).then_inc(p_s, 1)
                elif k:
                    nc.tensor.matmul(chunk(bank[2], k), l_state, chunk(l_qd, k), start=True, stop=False, skip_group_check=True)
                last = nc.tensor.matmul(chunk(bank[2], k), l_vn[k % 2], chunk(l_qk, k), start=k == 0, stop=True,
                                        skip_group_check=True)
                if k == 0:
                    slot_pe(pe, s, 2, 3)
            last.then_inc(p_o, 1)
            slot_pe(pe, s, 3, 3)
            pe.wait_ge(s_sq, n(3, 3))
            nc.tensor.matmul(bank[3][:, :], ones, l_sq[0][:, :], start=True, stop=True).then_inc(p_sum, 1)

        def heads(eng, c, head):
            head(eng, slots(c, 1), 0, None)
            with eng.Fori(0, NH - 2) as i:
                head(eng, slots(c, 2, i), 1, i)
            head(eng, slots(c, NH), NH - 1, None)

        def gdn_first(c, act=None, dve=None, pe=None):
            s = slots(c, 0)
            for j in range(4):
                if act:
                    slot_act(act, s, j)
                if dve:
                    slot_lo(dve, s, j)
                    for m in (1, 2, 3):
                        slot_tap(dve, s, j, m)
                if pe:
                    slot_pe(pe, s, j)
            if act:
                slot_silu(act, s)


        def at_tile(name, k, n=1):
            return place(name, n * S, FREE + k * TILE)

        x_rest, b_c, x_second = at_tile("sd_x_rest", 4, 2), at_tile("sd_b_c", 6, 2), at_tile("sd_x_second", 8, 4)
        sd_b, sd_c = [tile(conv_out, 0), tile(b_c, 0)], [tile(conv_out, 1), tile(b_c, 1)]
        sd_x = [[tile(conv_out, 2), tile(conv_out, 3), tile(x_rest, 0), tile(x_rest, 1)],
                [tile(x_second, k) for k in range(4)]]
        sd_z, sd_btok, sd_xdt, sd_cbm, sd_xdd, sd_ytok, sd_t, sd_st = (at_tile("sd_" + n, k, m) for n, k, m in (
            ("z", 12, 4), ("btok", 16, 1), ("xdt", 17, 4), ("cbm", 25, 1), ("xdd", 26, 1), ("ytok", 27, 1), ("t", 28, 1),
            ("st", 29, 1)))
        sd_u, sd_e, sd_sq = ([at_tile(f"sd_{n}{j}", k + j) for j in range(2)] for n, k in (("u", 21), ("e", 23), ("sq", 30)))
        d_u, d_xdd, d_scaled = sem("ssd_u_ready"), sem("ssd_xdd_ready"), sem("ssd_state_scaled")
        d_bt, d_cb, d_d, d_xt, d_yo, d_yd, d_s, d_yt, d_sum = (sem("ssd_" + n) for n in (
            "b_turned", "cb_done", "decay_done", "x_turned", "yoff_done", "ydiag_done", "state_done", "y_turned", "sum_done"))
        d_e, d_sq, d_ln, d_rs, d_zs = (sem("ssd_" + n) for n in ("exp_ready", "sq_ready", "ln_ready", "rs_ready", "z_silu"))
        d_btok, d_cbm, d_xdt, d_g, d_t, d_ytok, d_st, d_yf, d_yg, d_o = (sem("ssd_" + n) for n in (
            "btok_ready", "cbm_ready", "xdt_ready", "g_ready", "t_ready", "ytok_ready", "state_ready", "yf_ready",
            "gated", "o_ready"))

        def of_heads(table, col0, heads_, width):
            return table[:, col0:col0 + heads_].unsqueeze(2).to_broadcast([P, heads_, width])

        def by_head(t, heads_=8):
            return t[:, :].rearrange("p (h n) -> p h n", h=heads_)

        REST = [(sd_x[0][2], 4), (sd_x[0][3], 5)] + [(tile(sd_z, k), None) for k in range(4)] + [
            (sd_b[1], 6), (sd_c[1], 7)] + [(sd_x[1][k], 8 + k) for k in range(4)] + [
            (tile(sd_z, k), None) for k in range(4)]

        def unit_counts(c, k):
            return c["u"] + 36 + k, c["t"] + 36 + k, 24 + (REST[k][1] or 0)

        def rest_act(act, c, k):
            u, t, m = unit_counts(c, k)
            act.wait_ge(unit_done, u + 1)
            split_hi(act, u + 2, None, 0, KD)
            if REST[k][1]:
                w = cols.start["ssd_conv"] + 5 * REST[k][1]
                nc.scalar.activation(REST[k][0][:, :], acc[t % 2][:, :], ACT.Identity, scale=par[:, w + 3:w + 4],
                                     bias=par[:, w + 4:w + 5]).then_inc(c_tap, 1)

        def rest_dve(dve, c, k):
            u, t, m = unit_counts(c, k)
            o, a = REST[k][0], acc[t % 2]
            split_lo(dve, u + 2, None, 0, KD)
            if REST[k][1]:
                w = cols.start["ssd_conv"] + 5 * REST[k][1]
                dve.wait_ge(c_tap, m + 1)
                for b in (1, 2, 3):
                    if b > 1:
                        dve.wait_ge(c_step, 2 * m + b - 1)
                    nc.vector.scalar_tensor_tensor(out=o[:, b:S], in0=a[:, 0:S - b], scalar=par[:, w + 3 - b:w + 4 - b],
                                                   in1=o[:, b:S], op0=ALU.mult, op1=ALU.add
                                                   ).then_inc(acc_read if b == 3 else c_step, 1)
            else:
                dve.wait_ge(unit_done, u + 1)
                nc.vector.tensor_copy(o[:, :], a[:, :]).then_inc(acc_read, 1)

        def rest_silu(act, c, k, done=None):
            act.wait_ge(acc_read, c["t"] + 36 + k + 1)
            o = REST[k][0]
            nc.scalar.activation(o[:, :], o[:, :], ACT.Silu).then_inc(done or c_silu, 1)

        def rest_pe(pe, c, k, part=None):
            u, t, _ = unit_counts(c, k)
            multiply(pe, u, t, None, 0, 0, KD, HH, HL, part=part)

        def ssd_act(act, c):
            def chunks(g, first):
                log_exp(act)
                for k in range(NC):
                    n = 4 * g + k
                    for q in range(2):
                        act.wait_ge(d_d, 2 * n + q + 1)
                        if n:
                            act.wait_ge(d_yd, n)
                        nc.scalar.activation(sd_e[q][:, :], bank[q][:, :], ACT.Exp).then_inc(d_e, 1)
                    rest_act(act, c, first + k)
                for k in range(NC):
                    rest_silu(act, c, first + k, d_zs)

            def gate(g):
                log_exp(act)
                for k in range(4):
                    act.wait_ge(d_yg, 4 * g + k + 1)
                    if k >= 2:
                        act.wait_ge(d_sum, 4 * g + k - 1)
                    nc.scalar.activation(sd_sq[k % 2][:, :], sd_x[g][k], ACT.Square).then_inc(d_sq, 1)
                act.wait_ge(d_sum, 4 * g + 4)
                nc.scalar.activation(sd_t[:, :], bank[3][:, :], ACT.Ln, scale=1 / 512, bias=col("eps")).then_inc(d_ln, 1)
                act.wait_ge(d_ln, g + 1)
                nc.scalar.activation(sd_t[:, :], sd_t[:, :], ACT.Exp, scale=-0.5).then_inc(d_rs, 1)

            act.wait_ge(g_o, NH)
            for k in range(2):
                rest_act(act, c, k)
            for k in range(2):
                rest_silu(act, c, k)
            chunks(0, 2)
            rest_act(act, c, 6)
            gate(0)
            for k in range(7, 12):
                rest_act(act, c, k)
            for k in range(6, 12):
                rest_silu(act, c, k)
            chunks(1, 12)
            for k in range(8):
                nc.scalar.activation(tile(HH, k), tile(O, k), ACT.Copy).then_inc(hh_ready, 1)
            gate(1)
            for k in range(8):
                act.wait_ge(d_o, k + 1)
                nc.scalar.activation(tile(OH, k), tile(O, 8 + k), ACT.Copy).then_inc(hh_ready, 1)

        def ssd_dve(dve, c):
            def start(g):
                dve.wait_ge(d_bt, g + 1)
                nc.vector.tensor_copy(sd_btok[:, :], bank[4][:, :]).then_inc(d_btok, 1)
                dve.wait_ge(d_cb, g + 1)
                nc.vector.tensor_tensor(by_chunk(sd_cbm), by_chunk(bank[5]), each_chunk(upper), ALU.mult).then_inc(d_cbm, 1)

            def chunks(g, first):
                for k in range(NC):
                    n, head0 = 4 * g + k, 8 + 8 * g
                    dve.wait_ge(d_xt, n + 1)
                    nc.vector.tensor_tensor(by_head(tile(sd_xdt, k)), by_head(bank[2]),
                                            of_heads(t_soft, 32 * k + 16 + 8 * g, 8, 64), ALU.mult).then_inc(d_xdt, 1)
                    for q in range(2):
                        dve.wait_ge(d_e, 2 * n + q + 1)
                        dve.wait_ge(d_cbm, g + 1)
                        nc.vector.tensor_tensor(by_chunk(sd_e[q]), by_chunk(sd_e[q]), each_chunk(chunk(sd_cbm, k)),
                                                ALU.mult).then_inc(d_g, 1)
                    if n:
                        dve.wait_ge(d_yt, n)
                    if k:
                        dve.wait_ge(d_yo, 3 * g + k)
                        nc.vector.tensor_tensor(by_head(sd_t), by_head(bank[3]), of_heads(t_exp, 24 * k + head0, 8, 64),
                                                ALU.mult).then_inc(d_t, 1)
                        dve.wait_ge(d_yd, n + 1)
                        dve.wait_ge(d_t, 3 * g + k)
                        nc.vector.tensor_tensor(sd_ytok[:, :], sd_t[:, :], bank[4][:, :], ALU.add).then_inc(d_ytok, 1)
                    else:
                        dve.wait_ge(d_yd, n + 1)
                        nc.vector.tensor_copy(sd_ytok[:, :], bank[4][:, :]).then_inc(d_ytok, 1)
                    if k < NC - 1:
                        dve.wait_ge(d_s, 3 * g + k + 1)
                        if k:
                            dve.wait_ge(d_scaled, 2 * g + k)
                            nc.vector.tensor_tensor(sd_st[:, :], sd_st[:, :], bank[2][:, :], ALU.add).then_inc(d_st, 1)
                        else:
                            nc.vector.tensor_copy(sd_st[:, :], bank[2][:, :]).then_inc(d_st, 1)
                    if g and k == 0:
                        dve.wait_ge(d_yg, 4)
                    rest_dve(dve, c, first + k)
                    dve.wait_ge(d_yt, n + 1)
                    for j in range(4):
                        x = chunk(sd_x[g][j], k)
                        last = nc.vector.scalar_tensor_tensor(out=x, in0=x, scalar=col("ssd_d", 4 * g + j),
                                                              in1=chunk(bank[5], j), op0=ALU.mult, op1=ALU.add)
                    last.then_inc(d_yf, 1)

            def gated(g):
                for k in range(4):
                    dve.wait_ge(d_zs, 4 * g + k + 1)
                    dve.wait_ge(d_yf, 4 * g + 4)
                    x = sd_x[g][k]
                    nc.vector.tensor_tensor(x, x, tile(sd_z, k), ALU.mult).then_inc(d_yg, 1)

            def normed(g):
                dve.wait_ge(d_rs, g + 1)
                for k in range(4):
                    nc.vector.scalar_tensor_tensor(out=tile(O, 8 + 4 * g + k), in0=sd_x[g][k],
                                                   scalar=col("ssd_norm", 4 * g + k), in1=sd_t[:, :], op0=ALU.mult,
                                                   op1=ALU.mult).then_inc(d_o, 1)

            dve.wait_ge(g_o, NH)
            rest_dve(dve, c, 0)
            rest_dve(dve, c, 1)
            start(0)
            chunks(0, 2)
            gated(0)
            rest_dve(dve, c, 6)
            normed(0)
            for k in range(7, 12):
                rest_dve(dve, c, k)
            start(1)
            chunks(1, 12)
            gated(1)
            for k in range(8):
                dve.wait_ge(hh_ready, c["h"] + k + 1)
                nc.vector.tensor_tensor(tile(HL, k), tile(O, k), tile(HH, k).bitcast(F32), ALU.subtract).then_inc(h_ready, 1)
            normed(1)
            for k in range(8):
                dve.wait_ge(hh_ready, c["h"] + 8 + k + 1)
                nc.vector.tensor_tensor(tile(OL, k), tile(O, 8 + k), tile(OH, k).bitcast(F32), ALU.subtract).then_inc(h_ready, 1)

        def ssd_pool(pool, c):
            def u_of(g, k):
                n = 4 * g + k
                for q in range(2):
                    if n:
                        pool.wait_ge(d_d, 2 * (n - 1) + q + 1)
                    nc.gpsimd.tensor_tensor(by_chunk(sd_u[q]), of_heads(t_ld, 24 * k + 8 + 8 * g + 4 * q, 4, P),
                                            each_chunk(lower), ALU.mult).then_inc(d_u, 1)

            pool.wait_ge(g_o, NH)
            u_of(0, 0)
            for g in range(2):
                for k in range(NC):
                    n = 4 * g + k
                    if k < NC - 1:
                        u_of(g, k + 1)
                        pool.wait_ge(d_xdt, n + 1)
                        if 3 * g + k:
                            pool.wait_ge(d_s, 3 * g + k)
                        nc.gpsimd.tensor_tensor(by_head(sd_xdd), by_head(tile(sd_xdt, k)),
                                                of_heads(t_exp, 192 + 24 * k + 8 + 8 * g, 8, 64), ALU.mult).then_inc(d_xdd, 1)
                        if k:
                            pool.wait_ge(d_yo, 3 * g + k)
                            pool.wait_ge(d_st, 3 * g + k)
                            nc.gpsimd.tensor_tensor(by_head(sd_st), by_head(sd_st),
                                                    of_heads(t_exp, 96 + 24 * k + 8 + 8 * g, 8, 64), ALU.mult).then_inc(d_scaled, 1)
                    elif g == 0:
                        u_of(1, 0)

        def ssd_pe(pe, c):
            def decays(g, k):
                n = 4 * g + k
                for q in range(2):
                    pe.wait_ge(d_u, 2 * n + q + 1)
                    if n:
                        pe.wait_ge(d_e, 2 * (n - 1) + q + 1)
                    for j in range(4):
                        last = nc.tensor.matmul(chunk(bank[q], j), chunk(sd_u[q], j), upper, start=True, stop=True)
                    last.then_inc(d_d, 1)

            def start(g):
                pe.wait_ge(c_silu, 38 + 6 * g)
                if g:
                    pe.wait_ge(d_ytok, 4 * g)
                    pe.wait_ge(d_yf, 4 * g)
                turn(pe, bank[4], sd_b[g]).then_inc(d_bt, 1)
                for k in range(NC):
                    last = nc.tensor.matmul(chunk(bank[5], k), chunk(sd_b[g], k), chunk(sd_c[g], k), start=True, stop=True)
                last.then_inc(d_cb, 1)
                decays(g, 0)

            def chunks(g, first):
                for k in range(NC):
                    n = 4 * g + k
                    if k:
                        pe.wait_ge(d_st, 3 * g + k)
                    for j in range(4):
                        last = nc.tensor.transpose(chunk(bank[2], j), chunk(sd_x[g][j], k), ident)
                    last.then_inc(d_xt, 1)
                    rest_pe(pe, c, first + k, 0)
                    rest_pe(pe, c, first + k, 1)
                    if k:
                        if n > 1:
                            pe.wait_ge(d_t, 3 * g + k - 1)
                        nc.tensor.matmul(bank[3][:, :], chunk(sd_c[g], k), sd_st[:, :], start=True, stop=True).then_inc(d_yo, 1)
                    pe.wait_ge(d_xdt, n + 1)
                    pe.wait_ge(d_g, 2 * n + 2)
                    pe.wait_ge(d_btok, g + 1)
                    if n:
                        pe.wait_ge(d_ytok, n)
                    for j in range(8):
                        last = nc.tensor.matmul(bank[4][:, 64 * j:64 * j + 64], chunk(sd_e[j // 4], j % 4),
                                                tile(sd_xdt, k)[:, 64 * j:64 * j + 64], start=True, stop=True)
                    last.then_inc(d_yd, 1)
                    if k < NC - 1:
                        pe.wait_ge(d_xdd, 3 * g + k + 1)
                        nc.tensor.matmul(bank[2][:, :], chunk(sd_btok, k), sd_xdd[:, :], start=True, stop=True).then_inc(d_s, 1)
                        decays(g, k + 1)
                    rest_pe(pe, c, first + k, 2)
                    rest_pe(pe, c, first + k, 3)
                    pe.wait_ge(d_ytok, n + 1)
                    pe.wait_ge(d_yf, n) if n else pe.wait_ge(d_cbm, 1)
                    for j in range(4):
                        last = nc.tensor.transpose(chunk(bank[5], j), chunk(sd_ytok, j), ident)
                    last.then_inc(d_yt, 1)

            def sums(g):
                for k in range(4):
                    pe.wait_ge(d_sq, 4 * g + k + 1)
                    nc.tensor.matmul(bank[3][:, :], ones, sd_sq[k % 2][:, :], start=k == 0, stop=k == 3).then_inc(d_sum, 1)

            rest_pe(pe, c, 0)
            rest_pe(pe, c, 1)
            pe.wait_ge(g_o, NH)
            start(0)
            chunks(0, 2)
            rest_pe(pe, c, 6)
            sums(0)
            for k in range(7, 12):
                rest_pe(pe, c, k)
            start(1)
            chunks(1, 12)
            sums(1)

        def l1_act(act, c):
            log_exp(act)
            tables_act(act, c)
            gdn_first(c, act=act)
            sums_exp_act(act)
            heads(act, c, lambda eng, s, h0, i: gdn_act(eng, s, h0, i))
            ssd_act(act, c)

        def l1_dve(dve, c):
            tables_dve(dve, c)
            gdn_first(c, dve=dve)
            beta_exp_dve(dve)
            dve.wait_ge(a_dve, 6)
            heads(dve, c, lambda eng, s, h0, i: gdn_dve(eng, s, h0, i))
            ssd_dve(dve, c)

        def l1_pool(pool, c):
            pool.wait_ge(a_dve, 5)
            decays_pool(pool, 0, None)
            heads(pool, c, lambda eng, s, h0, i: gdn_pool(eng, s, h0, i))
            ssd_pool(pool, c)

        def l1_pe(pe, c):
            tables_pe(pe, c)
            gdn_first(c, pe=pe)
            chunk_sums_pe(pe)
            heads(pe, c, lambda eng, s, h0, i: gdn_pe(eng, s, h0, i))
            ssd_pe(pe, c)

        n = dict(u=0, t=0, sq=0, rms=0, hn=0, h=0, ffn=0, pair=0, tap=0, conv=0, x=0, w8=0, w11=0)
        made = (x_loaded, lambda k: 16)
        stages = []
        for at_, (kind, arg) in enumerate(plan):
            c = dict(n)
            if kind == "norm":
                stages.append((kind, arg, c, made))
                for key, more in (("sq", KD), ("rms", 1), ("hn", KD), ("h", KD)):
                    n[key] += more
            elif kind == "post":
                stages.append((kind, arg, c, Y1 if plan[at_ - 1][0] == "project1" else Y))
                for key, more in (("sq", KD), ("rms", 1), ("hn", KD), ("x", KD)):
                    n[key] += more
                made = (x_ready, lambda k, x0=c["x"]: x0 + k + 1)
            elif kind == "up":
                stages.append((kind, arg, c, None))
                for key, more in (("u", 2 * KF), ("t", 2 * KF), ("w8", 2 * KF), ("ffn", 1), ("pair", KF),
                                  ("tap", 2 * KF), ("conv", 2 * KF)):
                    n[key] += more
            elif kind == "gla":
                stages.append((kind, arg, c, None))
                for key, more in (("u", 25), ("t", 25), ("w8", 25), ("hn", KD), ("h", KD)):
                    n[key] += more
            elif kind == "l1":
                stages.append((kind, arg, c, None))
                for key, more in (("u", 52), ("t", 52), ("w8", 52), ("h", 2 * KD)):
                    n[key] += more
            elif kind == "project1":
                stages.append((kind, arg, c, all(k == "post" for k, _ in plan[at_ + 1:])))
                for key, more in (("u", 2 * KD), ("t", KD), ("w8", 2 * KD)):
                    n[key] += more
            elif kind == "sb":
                stages.append((kind, arg, c, None))
                for key, more in (("u", 16), ("t", 16), ("w8", 16), ("hn", KD), ("h", KD)):
                    n[key] += more
            elif kind == "project":
                stages.append((kind, arg, c, at_ == len(plan) - 1))
                for key, more in (("u", KD), ("t", KD), ("w8", KD)):
                    n[key] += more
                made = (acc_read, lambda k, t0=c["t"]: t0 + k + 1)
            elif kind == "down":
                stages.append((kind, arg, c, at_ == len(plan) - 1 or all(k == "post" for k, _ in plan[at_ + 1:])))
                for key, more in (("u", 2 * KD), ("t", KD), ("w11", 2 * KD)):
                    n[key] += more
                made = (acc_read, lambda k, t0=c["t"]: t0 + k + 1)

        block = ctx.enter_context(nc.Block())

        @block.sync
        def _(sp):
            sp.dma_start(X[:, :], x_in).then_inc(x_loaded, 16)
            sp.dma_start(par[:, :], par_in).then_inc(params_in, 16)
            sp.dma_start(cst[:, :], cst_in).then_inc(params_in, 16)
            sp.dma_start(small[:, :], small_in).then_inc(params_in, 16)
            for kind, arg, c, _ in stages:
                if kind == "up":
                    load_units(sp, w8, c["w8"], c["u"], 2 * KF)
                if kind == "gla":
                    load_units(sp, w8, c["w8"], c["u"], 25)
                if kind == "l1":
                    sp.dma_start(small1[:, :], small1_in).then_inc(a_small, 16)
                    load_units(sp, w8, c["w8"], c["u"], 52)
                if kind == "project1":
                    load_units(sp, w8, c["w8"], c["u"], 2 * KD)
                if kind == "sb":
                    load_units(sp, w8, c["w8"], c["u"], 16)
                if kind == "project":
                    load_units(sp, w8, c["w8"], c["u"], KD)
                if kind == "down":
                    load_units(sp, w11, c["w11"], c["u"], 2 * KD)
            for k in range(KD):
                sp.wait_ge(made[0], made[1](k))
                sp.dma_start(out[:, k * S:(k + 1) * S], tile(X, k)).then_inc(out_stored, 16)
            sp.wait_ge(out_stored, 16 * KD)

        @block.scalar
        def _(act):
            act.wait_ge(params_in, 48)
            for u in range(SPLIT):
                split_hi(act, u, None, 0, KD)
            for kind, arg, c, more in stages:
                if kind == "norm":
                    norm_act(act, c, more)
                elif kind == "post":
                    post_act(act, c, more)
                elif kind == "up":
                    up_act(act, c)
                elif kind == "l1":
                    l1_act(act, c)
                elif kind == "project1":
                    back_act(act, c, KD, 2, None if more else KD)
                elif kind == "sb":
                    sb_act(act, c)
                elif kind == "gla":
                    gla_act(act, c)
                elif kind == "project":
                    back_act(act, c, KD, 1, None if more else KD)
                elif kind == "down":
                    back_act(act, c, HALF, 2, None if more else KD)

        @block.vector
        def _(dve):
            dve.wait_ge(params_in, 48)
            for u in range(SPLIT):
                split_lo(dve, u, None, 0, KD)
            for kind, arg, c, more in stages:
                if kind == "norm":
                    scaled_dve(dve, c, X, arg, h_ready, c["h"])
                elif kind == "post":
                    scaled_dve(dve, c, more, arg, x_ready, c["x"])
                elif kind == "up":
                    up_dve(dve, c)
                elif kind == "l1":
                    l1_dve(dve, c)
                elif kind == "project1":
                    back_dve(dve, c, KD, 2, None if more else KD, Y1)
                elif kind == "sb":
                    sb_dve(dve, c)
                elif kind == "gla":
                    gla_dve(dve, c)
                elif kind == "project":
                    back_dve(dve, c, KD, 1, None if more else KD)
                elif kind == "down":
                    back_dve(dve, c, HALF, 2, None if more else KD, Y if arg else None)

        @block.gpsimd
        def _(pool):
            for kind, arg, c, more in stages:
                if kind == "norm":
                    norm_pool(pool, c)
                elif kind == "post":
                    post_pool(pool, c)
                elif kind == "l1":
                    l1_pool(pool, c)
                elif kind == "sb":
                    sb_pool(pool, c)
                elif kind == "gla":
                    gla_pool(pool, c)
                elif kind == "up":
                    up_pool(pool, c)

        @block.tensor
        def _(pe):
            pe.wait_ge(params_in, 48)
            for kind, arg, c, more in stages:
                if kind in ("norm", "post"):
                    sums_pe(pe, c, KD)
                elif kind == "up":
                    up_pe(pe, c)
                elif kind == "l1":
                    l1_pe(pe, c)
                elif kind == "project1":
                    back_pe(pe, c, KD, 2, (HH, OH), (HL, OL), (h_ready, c["h"] - 2 * KD))
                elif kind == "sb":
                    sb_pe(pe, c)
                elif kind == "gla":
                    gla_pe(pe, c)
                elif kind == "project":
                    back_pe(pe, c, KD, 1, *((HH, HL) if arg == "HH" else (MH, ML)), (h_ready, c["h"] - KD))
                elif kind == "down":
                    back_pe(pe, c, HALF, 2, FH, FL, (f_ready, c["pair"] - KF))


def channels(a):
    return a.reshape(-1, P).T


def units(w, kt):
    k, m = w.shape
    return w.reshape(k // (kt * P), kt, P, m // P, P).transpose(3, 0, 2, 1, 4).reshape(-1, P, kt * P)


def pairs(w):
    k, m = w.shape
    return w.reshape(k, 2, m // 2 // P, P).transpose(0, 2, 1, 3).reshape(k, m)


def constants():
    r = np.arange(P)
    p, f = r[:, None], r[None, :]
    parts = [p == f, np.ones((P, P)), p <= f, p > f, p // 64 == f // 64]
    for b in (1, 2, 4, 8, 16, 32, 64):
        parts.append((p // (2 * b) == f // (2 * b)) & (p // b % 2 == 1) & (f // b % 2 == 0))
    parts += [np.where(p >= f, -1.0, 0.0), -np.ones((P, P)), np.where(p >= f, -1e30, 0.0)]
    return np.concatenate([np.asarray(a, np.float32) for a in parts], axis=1)


def tile_of(w, j):
    return w[:, j * P:(j + 1) * P]


PLAN = [("norm", ("g_pre_mix", 0)), ("l1", None), ("project1", None), ("post", ("g_post_mix", 0)),
        ("norm", ("g_pre_ffn", 0)), ("up", 0), ("down", True), ("post", ("g_post_ffn", 0)),
        ("norm", ("g_even", 0)), ("sb", None), ("project", "MH"),
        ("norm", ("g_ffn_2", 0)), ("up", 1), ("down", False),
        ("norm", ("g_odd", 0)), ("gla", None), ("project", "HH"),
        ("norm", ("g_ffn_2", KD)), ("up", 2), ("down", False)]


def kernel(**a):
    import concourse.bacc as bacc
    from concourse.bass_utils import run_bass_kernel_spmd as run

    a = {name: np.asarray(value) for name, value in a.items()}
    x = a.pop("x")
    ffn_norm, ffn_up, ffn_down = a["ffn_norm_2"], a["ffn_w_up_2"], a["ffn_w_down_2"]
    ffn_conv = [np.concatenate([a["ffn_conv_w"][0], a["ffn_conv_b"][0][None]])] + [
        np.concatenate([a["ffn_conv_w_2"][k], a["ffn_conv_b_2"][k][None]]) for k in range(2)]
    a = {name: value[0] for name, value in a.items()}

    cols = columns()
    par = np.zeros((P, cols.n), np.float32)

    def put(name, value):
        par[:, cols.start[name]:cols.start[name] + value.shape[1]] = value

    put("eps", np.full((P, 1), EPS, np.float32))
    for name, source in (("g_pre_mix", "pre_mix_norm"), ("g_post_mix", "post_mix_norm"), ("g_pre_ffn", "pre_ffn_norm"),
                         ("g_post_ffn", "post_ffn_norm"), ("g_even", "mix_norm_even_2"), ("g_odd", "mix_norm_odd_2"),
                         ("gdn_norm", "gdn_norm_w"), ("ssd_norm", "ssd_norm_w"), ("pool_scale", "pool_scale_2"),
                         ("gla_b", "gla_b_a_2"), ("gla_gain", "gla_o_gain_2")):
        put(name, channels(a[source]))
    put("g_ffn_2", channels(ffn_norm))
    put("ssd_d", channels(np.repeat(a["ssd_d"], 64)))
    put("sb_gain", np.stack([np.tile(a["sb_q_gain_2"], 2), np.tile(a["sb_k_gain_2"], 2)], 1))
    put("ffn", np.concatenate([pairs(f).reshape(4, 2 * KF, P).transpose(2, 1, 0).reshape(P, -1) for f in ffn_conv], 1))
    taps = np.concatenate([a["gdn_conv_w"], np.zeros((1, 3 * D), np.float32)])
    put("conv", taps.reshape(5, 3, 8, P).transpose(3, 2, 1, 0).reshape(P, -1))
    taps = np.concatenate([a["ssd_conv_w"], a["ssd_conv_b"][None]]).reshape(5, 12, P)
    put("ssd_conv", taps[:, [8, 10, 0, 1, 2, 3, 9, 11, 4, 5, 6, 7]].transpose(2, 1, 0).reshape(P, -1))
    put("rows", np.tile(np.concatenate([a[n] for n in ("gdn_dt_bias", "ssd_dt_bias", "gdn_a_log", "ssd_a_log")]), (P, 1)))
    frames = np.arange(1, 17)
    put("pool_count", np.tile(np.concatenate([w / np.minimum(frames, w) for w in (2, 4, 8, 16)]), (P, 1)))

    small = np.zeros((P, 2 * S), np.float32)
    small[0:16, 0:S] = a["gla_w_a2_2"]
    small[:, S:] = a["pool_w_2"].transpose(1, 0, 2).reshape(P, S)

    q, k, v, z, b_a, a_a, z_s, x_s, b_s, c_s, dt_s = np.split(
        a["w_in"], np.cumsum([D, D, D, D, 8, 8, D, D, 2 * P, 2 * P]), axis=1)
    small1 = np.concatenate([b_a, a_a, dt_s], axis=1).reshape(KD, P, 32).transpose(1, 0, 2).reshape(P, -1)
    first = [tile_of(w, h) for h in range(8) for w in (q, k, v, z)]
    for g in range(2):
        first += [tile_of(b_s, g), tile_of(c_s, g)] + [tile_of(w, 4 * g + j) for w in (x_s, z_s) for j in range(4)]
    q, k, v, pooled = np.split(a["w_in_even_2"], 4, axis=1)
    even = [v, pooled] + [tile_of(w, i) for i in range(4) for w in (q, k)]
    even_out = np.concatenate([a["w_out_even_2"][S:], a["w_out_even_2"][:S]])
    q, k, v, r, low = np.split(a["w_in_odd_2"], [S, 2 * S, 2 * S + D, 2 * S + 2 * D], axis=1)
    odd = [np.pad(low, ((0, 0), (0, P - 16))), k, v, q, r]
    w8 = [np.concatenate(first, axis=1), a["w_out"], pairs(a["w_up"]), np.concatenate(even, axis=1), even_out,
          pairs(ffn_up[0]), np.concatenate(odd, axis=1), a["w_out_odd_2"], pairs(ffn_up[1])]
    arrays = {
        "x": x[0].T.reshape(KD, P, S).transpose(1, 0, 2).reshape(P, -1),
        "w8": np.concatenate([units(w, KD) for w in w8]),
        "w11": np.concatenate([units(w, HALF) for w in (a["w_down"], ffn_down[0], ffn_down[1])]),
        "par": par, "cst": constants(), "small": small, "small1": small1}

    nc = bacc.Bacc("TRN2", target_bir_lowering=False, num_devices=1)
    arrays = {name: np.ascontiguousarray(value) for name, value in arrays.items()}
    aps = [nc.dram_tensor(name, value.shape, F32, kind="ExternalInput").ap() for name, value in arrays.items()]
    out = nc.dram_tensor("out", [P, KD * S], F32, kind="ExternalOutput").ap()
    program(nc, *aps, out, PLAN)
    result = run(nc, [arrays], core_ids=[0])
    return result.results[0]["out"].reshape(P, KD, S).transpose(1, 0, 2).reshape(D, S).T[None]
```

```python
from contextlib import ExitStack

import numpy as np

import concourse.bass as bass
from concourse import mybir

F32 = mybir.dt.float32
F32R = mybir.dt.float32r
ALU = mybir.AluOpType
ACT = mybir.ActivationFunctionType

P = 128
S = 512
D = 1024
KD = D // P
F = 2816
KF = F // P
HALF = KF // 2
TILE = 4 * S
RAW = 4
SPLIT = 2
EPS = 1e-6


def at(base, i, per):
    return base if i is None else base + per * i


class Columns:

    def __init__(self):
        self.start, self.n = {}, 0

    def add(self, name, n):
        self.start[name] = self.n
        self.n += n


def columns():
    c = Columns()
    for name, n in (("eps", 1), ("g_pre_mix", 8), ("g_post_mix", 8), ("g_pre_ffn", 8), ("g_post_ffn", 8),
                    ("g_even", 8), ("g_odd", 8), ("g_ffn_2", 16), ("ffn", 3 * 44 * 4), ("conv", 24 * 5),
                    ("gdn_norm", 1), ("ssd_conv", 12 * 5), ("ssd_d", 8), ("ssd_norm", 8), ("sb_gain", 2),
                    ("pool_scale", 4), ("gla_b", 4), ("gla_gain", 2),
                    ("rows", 48), ("pool_count", 64)):
        c.add(name, n)
    return c
def program(nc, x_in, w8, w11, par_in, cst_in, small_in, out, plan):
    cols = columns()
    ctx = ExitStack()
    with ctx:
        top = [(nc.sbuf_base + 31) // 32 * 32]

        def fixed(name, shape, dt=F32):
            t = nc.alloc_sbuf_tensor_at(name, shape, dt, offset=top[0])
            top[0] += (4 * shape[1] + 31) // 32 * 32
            return t

        X = fixed("X", [P, KD * S])
        base_h = top[0]
        HH = fixed("HH", [P, KD * S], F32R)
        HL = fixed("HL", [P, KD * S], F32R)
        Y = nc.alloc_sbuf_tensor_at("Y", [P, KD * S], F32, offset=base_h)
        raw = [fixed(f"raw{j}", [P, HALF * P]) for j in range(RAW)]
        whi = [fixed(f"whi{j}", [P, HALF * P], F32R) for j in range(SPLIT)]
        wlo = [fixed(f"wlo{j}", [P, HALF * P], F32R) for j in range(SPLIT)]
        par = fixed("par", [P, cols.n])
        cst = fixed("cst", [P, 15 * P])
        small = fixed("small", [P, small_in.shape[1]])
        top[0] = (top[0] + 31) // 32 * 32
        FREE = top[0]
        TMP = nc.sbuf_usable_end // 32 * 32 - 6 * TILE
        used = {}

        def place(name, n, offset, dt=F32):
            assert offset >= FREE and offset + 4 * n <= nc.sbuf_usable_end, name
            return nc.alloc_sbuf_tensor_at(name, [P, n], dt, offset=offset)

        ident, ones, upper, lower, halves = (cst[:, k * P:(k + 1) * P] for k in range(5))
        neg_lower, neg_ones, hidden = (cst[:, k * P:(k + 1) * P] for k in range(12, 15))
        level = [cst[:, (5 + k) * P:(6 + k) * P] for k in range(7)]

        def col(name, k=0, n=1):
            c = cols.start[name] + k
            return par[:, c:c + n]

        def dcol(name, k):
            return par[:, bass.ds(k + cols.start[name], 1)]

        def tile(t, k):
            return t[:, k * S:(k + 1) * S]

        def dtile(t, k):
            return t[:, bass.ds(k * S, S)]

        sq = [place(f"sq{j}", S, TMP + j * TILE) for j in range(2)]
        hn = [place(f"hn{j}", S, TMP + (2 + j) * TILE) for j in range(2)]
        ln = place("ln", S, TMP + 4 * TILE)
        rs = place("rs", S, TMP + 5 * TILE)
        sq_sum = place("sq_sum", S, TMP + 2 * TILE)
        taps = [place(f"taps{j}", S, TMP + j * TILE) for j in range(4)]
        FH = place("FH", KF * S, FREE, F32R)
        FL = place("FL", KF * S, FREE + KF * TILE, F32R)
        assert FREE + 2 * KF * TILE <= TMP

        acc = [ctx.enter_context(nc.psum_tensor(f"acc{j}", [P, S], F32)) for j in range(2)]
        bank = [ctx.enter_context(nc.psum_tensor(f"bank{j}", [P, S], F32)) for j in range(2, 8)]
        ss = bank[0]

        sems = {}

        def sem(name):
            if name not in sems:
                sems[name] = ctx.enter_context(nc.semaphore(name))
            return sems[name]

        params_in, x_loaded = sem("params_in"), [sem(f"x_loaded{j}") for j in range(KD // 2)]
        raw_in = [sem(f"raw_in{j}") for j in range(RAW)]
        w_hi_ready, w_lo_ready = sem("w_hi_ready"), sem("w_lo_ready")
        unit_done = sem("unit_done")
        acc_read = sem("acc_read")
        sq_ready, sq_summed, rms_ready = sem("sq_ready"), sem("sq_summed"), sem("rms_ready")
        sq_added = sem("sq_added")
        hn_ready, hh_ready, h_ready = sem("hn_ready"), sem("hh_ready"), sem("h_ready")
        tap_ready, conv_step = sem("tap_ready"), sem("conv_step")
        silu_ready, prod_ready, fh_ready, f_ready = (sem(n) for n in ("silu_ready", "prod_ready", "fh_ready", "f_ready"))
        scaled = sem("scaled")
        x_ready = sem("x_ready")
        ln_ready, y_step = sem("ln_ready"), sem("y_step")
        out_stored = sem("out_stored")

        def load_units(sp, src, n0, u0, count):
            kt = src.shape[2] // P

            def group(n0, u0, size, i):
                for j in range(size):
                    u, unit = u0 + j, n0 + j if i is None else i * RAW + (n0 + j)
                    if u >= RAW:
                        sp.wait_ge(w_lo_ready, at(u - RAW + 1, i, RAW))
                    sp.dma_start(raw[u % RAW][:, 0:kt * P],
                                 src[bass.ds(unit, 1), :, :].rearrange("a p c -> p (a c)")
                                 ).then_inc(raw_in[u % RAW], 16)

            head = count % RAW + (RAW if u0 == 0 else 0)
            group(n0, u0, head, None)
            with sp.Fori(0, (count - head) // RAW) as i:
                group(n0 + head, u0 + head, RAW, i)

        def split_hi(act, u, i, per, kt):
            j = u % SPLIT
            act.wait_ge(raw_in[u % RAW], at(16 * (u // RAW + 1), i, 16 * per // RAW))
            if u >= SPLIT:
                act.wait_ge(unit_done, at(u - SPLIT + 1, i, per))
            nc.scalar.activation(whi[j][:, 0:kt * P], raw[u % RAW][:, 0:kt * P], ACT.Copy).then_inc(w_hi_ready, 1)

        def split_lo(dve, u, i, per, kt):
            j = u % SPLIT
            dve.wait_ge(w_hi_ready, at(u + 1, i, per))
            nc.vector.tensor_tensor(wlo[j][:, 0:kt * P], raw[u % RAW][:, 0:kt * P],
                                    whi[j][:, 0:kt * P].bitcast(F32), ALU.subtract).then_inc(w_lo_ready, 1)

        def multiply(pe, u, t, i, per, per_t, kt, hi, lo, start=True, stop=True, ready=None, part=None):
            w, a = u % SPLIT, acc[t % 2]
            if not part:
                pe.wait_ge(w_lo_ready, at(u + 1, i, per))
                if start and t >= 2:
                    pe.wait_ge(acc_read, at(t - 1, i, per_t))
            for k in range(kt) if part is None else range(kt * part // 4, kt * (part + 1) // 4):
                if ready:
                    pe.wait_ge(ready[0], ready[1] + k + 1)
                wh, wl = whi[w][:, k * P:(k + 1) * P], wlo[w][:, k * P:(k + 1) * P]
                nc.tensor.matmul(a[:, :], wh, tile(hi, k), start=start and k == 0, stop=False)
                nc.tensor.matmul(a[:, :], wh, tile(lo, k), start=False, stop=False)
                last = nc.tensor.matmul(a[:, :], wl, tile(hi, k), start=False, stop=stop and k == kt - 1)
            if part in (None, 3):
                last.then_inc(unit_done, 1)

        def sums_act(act, c, src, made, n):
            for k in range(n):
                act.wait_ge(*made(k))
                if k >= 2:
                    act.wait_ge(sq_summed, c["ssum"] + k - 1)
                nc.scalar.activation(sq[k % 2][:, :], tile(src, k), ACT.Square).then_inc(sq_ready, 1)

        def rms_act(act, summed, r, width):
            log_exp(act)
            act.wait_ge(sq_summed, summed)
            nc.scalar.activation(ln[:, :], ss[:, :], ACT.Ln, scale=1.0 / width, bias=col("eps")).then_inc(ln_ready, 1)
            act.wait_ge(ln_ready, r + 1)
            nc.scalar.activation(rs[:, :], ln[:, :], ACT.Exp, scale=-0.5).then_inc(rms_ready, 1)

        def sums_pe(pe, c, n):
            for k in range(n):
                pe.wait_ge(sq_ready, c["sq"] + k + 1)
                nc.tensor.matmul(ss[:, :], ones, sq[k % 2][:, :], start=k == 0,
                                 stop=k == n - 1).then_inc(sq_summed, 1)

        def norm_act(act, c, made):
            sums_act(act, c, X, made, KD)
            rms_act(act, c["ssum"] + KD, c["rms"], D)
            split_hi(act, 0, None, 0, KD)
            for k in range(KD):
                act.wait_ge(hn_ready, c["hn"] + k + 1)
                nc.scalar.activation(tile(HH, k), hn[k % 2][:, :], ACT.Copy).then_inc(hh_ready, 1)
            split_hi(act, 1, None, 0, KD)

        def scaled_dve(dve, c, src, gain, used, u0):
            dve.wait_ge(rms_ready, c["rms"] + 1)
            for k in range(KD):
                if k >= 2:
                    dve.wait_ge(used, u0 + k - 1)
                last = nc.vector.scalar_tensor_tensor(out=hn[k % 2][:, :], in0=tile(src, k),
                                                      scalar=col(gain[0], gain[1] + k), in1=rs[:, :],
                                                      op0=ALU.mult, op1=ALU.mult).then_inc(hn_ready, 1)

        POOLED = 4

        def later_act(act, c, gain, made):
            for k in range(KD):
                act.wait_ge(*made(k))
                nc.scalar.activation(tile(HH, k), tile(X, k), ACT.Copy, scale=col(gain[0], gain[1] + k)).then_inc(hh_ready, 1)
            for k in range(KD):
                if k >= POOLED + 2:
                    act.wait_ge(sq_summed, c["ssum"] + k - POOLED - 1)
                elif k >= 3:
                    act.wait_ge(sq_added, c["add"] + min(k, POOLED + 1) - 2)
                nc.scalar.activation(sq_sum[:, :] if k == 0 else sq[k % 2][:, :], tile(X, k), ACT.Square).then_inc(sq_ready, 1)
            rms_act(act, c["ssum"] + KD - POOLED + 1, c["rms"], D)

        def later_dve(dve, c, gain):
            for k in range(KD):
                dve.wait_ge(hh_ready, c["hh"] + k + 1)
                nc.vector.scalar_tensor_tensor(out=tile(HL, k), in0=tile(X, k), scalar=col(gain[0], gain[1] + k),
                                               in1=tile(HH, k).bitcast(F32), op0=ALU.mult,
                                               op1=ALU.subtract).then_inc(h_ready, 1)

        def later_pool(pool, c):
            for k in range(1, POOLED):
                pool.wait_ge(sq_ready, c["sq"] + k + 1)
                if k > 1:
                    pool.wait_ge(sq_added, c["add"] + k - 1)
                nc.gpsimd.tensor_tensor(sq_sum[:, :], sq_sum[:, :], sq[k % 2][:, :], ALU.add).then_inc(sq_added, 1)

        def later_pe(pe, c):
            for k in range(POOLED, KD):
                pe.wait_ge(sq_ready, c["sq"] + k + 1)
                nc.tensor.matmul(ss[:, :], ones, sq[k % 2][:, :], start=k == POOLED, stop=False).then_inc(sq_summed, 1)
            pe.wait_ge(sq_added, c["add"] + POOLED - 1)
            nc.tensor.matmul(ss[:, :], ones, sq_sum[:, :], start=False, stop=True).then_inc(sq_summed, 1)

        def scale(dve, c, j, i=None, per=0, u=None):
            dve.wait_ge(unit_done, at(c["u"] + j + 1, i, per))
            if j == 0:
                dve.wait_ge(rms_ready, c["rms"])
            a = acc[(c["t"] + j) % 2]
            nc.vector.tensor_tensor(a[:, :], a[:, :], rs[:, :], ALU.mult).then_inc(scaled, 1)

        def norm_pool(pool, c):
            for k in range(KD):
                pool.wait_ge(hh_ready, c["hh"] + k + 1)
                nc.gpsimd.tensor_tensor(tile(HL, k), hn[k % 2][:, :], tile(HH, k).bitcast(F32),
                                        ALU.subtract).then_inc(h_ready, 1)

        def post_act(act, c, y):
            sums_act(act, c, y, lambda k: (acc_read, c["t"] - KD + k + 1), KD)
            rms_act(act, c["ssum"] + KD, c["rms"], D)

        def post_pool(pool, c):
            for k in range(KD):
                pool.wait_ge(hn_ready, c["hn"] + k + 1)
                nc.gpsimd.tensor_tensor(tile(X, k), tile(X, k), hn[k % 2][:, :], ALU.add).then_inc(x_ready, 1)

        def groups(eng, count, body):
            body(0, None)
            if count > 2:
                with eng.Fori(0, count - 2) as i:
                    body(1, i)
            body(count - 1, None)

        def up_act(act, c):
            u0, t0, p0 = c["u"], c["t"], c["pair"]

            def body(g, i):
                def n(base, per):
                    return at(base + per * g, i, per)
                for j in range(4):
                    u, p = u0 + 4 * g + j, p0 + 2 * g + j // 2
                    act.wait_ge(unit_done, n(u0 + j + 1, 4))
                    split_hi(act, u + 2, i, 4, HALF if g == KF // 2 - 1 and j >= 2 else KD)
                    act.wait_ge(scaled, n(c["scaled"] + j + 1, 4))
                    if g or j >= 2 or c["pair"]:
                        act.wait_ge(f_ready, n(p0 + j // 2 - 1, 2)) if p >= 2 else None
                    k = n((c["ffn"] * 2 * KF + j) * 4, 16)
                    w = (lambda m: col("ffn", k + m)) if i is None else (lambda m: dcol("ffn", k + m))
                    nc.scalar.activation(taps[j][:, :], acc[(t0 + j) % 2][:, :], ACT.Identity, scale=w(2),
                                         bias=w(3)).then_inc(tap_ready, 1)
                    if j % 2:
                        act.wait_ge(acc_read, n(t0 + j, 4))
                        nc.scalar.activation(taps[j - 1][:, :], taps[j - 1][:, :], ACT.Silu).then_inc(silu_ready, 1)
                        act.wait_ge(prod_ready, n(p0 + j // 2 + 1, 2))
                        pair = n(j // 2, 2)
                        o = tile(FH, pair) if i is None else dtile(FH, pair)
                        nc.scalar.activation(o, taps[j - 1][:, :], ACT.Copy).then_inc(fh_ready, 1)
            groups(act, KF // 2, body)

        def up_dve(dve, c):
            u0, t0 = c["u"], c["t"]

            def body(g, i):
                def n(base, per):
                    return at(base + per * g, i, per)
                for j in range(4):
                    scale(dve, c, 4 * g + j, i, 4)
                    split_lo(dve, u0 + 4 * g + j + 2, i, 4, HALF if g == KF // 2 - 1 and j >= 2 else KD)
                    k = n((c["ffn"] * 2 * KF + j) * 4, 16)
                    w = (lambda m: col("ffn", k + m)) if i is None else (lambda m: dcol("ffn", k + m))
                    dve.wait_ge(tap_ready, n(c["tap"] + j + 1, 4))
                    nc.vector.scalar_tensor_tensor(out=taps[j][:, 1:S], in0=acc[(t0 + j) % 2][:, 0:S - 1], scalar=w(1),
                                                   in1=taps[j][:, 1:S], op0=ALU.mult,
                                                   op1=ALU.add).then_inc(conv_step, 1)
                    dve.wait_ge(conv_step, n(c["conv"] + j + 1, 4))
                    nc.vector.scalar_tensor_tensor(out=taps[j][:, 2:S], in0=acc[(t0 + j) % 2][:, 0:S - 2], scalar=w(0),
                                                   in1=taps[j][:, 2:S], op0=ALU.mult,
                                                   op1=ALU.add).then_inc(acc_read, 1)
            groups(dve, KF // 2, body)

        def up_pool(pool, c):
            t0, p0 = c["t"], c["pair"]

            def body(g, i):
                def n(base, per):
                    return at(base + per * g, i, per)
                for b in range(2):
                    pool.wait_ge(silu_ready, n(p0 + b + 1, 2))
                    pool.wait_ge(acc_read, n(t0 + 2 * b + 2, 4))
                    nc.gpsimd.tensor_tensor(taps[2 * b][:, :], taps[2 * b][:, :], taps[2 * b + 1][:, :],
                                            ALU.mult).then_inc(prod_ready, 1)
                    pool.wait_ge(fh_ready, n(p0 + b + 1, 2))
                    pair = n(b, 2)
                    o, h = (tile(FL, pair), tile(FH, pair)) if i is None else (dtile(FL, pair), dtile(FH, pair))
                    nc.gpsimd.tensor_tensor(o, taps[2 * b][:, :], h.bitcast(F32), ALU.subtract).then_inc(f_ready, 1)
            groups(pool, KF // 2, body)

        def up_pe(pe, c):
            u0, t0 = c["u"], c["t"]

            def body(g, i):
                for j in range(4):
                    multiply(pe, u0 + 4 * g + j, t0 + 4 * g + j, i, 4, 4, KD, HH, HL,
                             ready=(h_ready, c["h"] - KD) if g == 0 and j == 0 else None)
                    if g == 0 and j == 0:
                        later_pe(pe, c["norm"])
            groups(pe, KF // 2, body)

        def back_pe(pe, c, kt, units, hi, lo, ready):
            u0, t0 = c["u"], c["t"]
            per = 4 // units

            def body(g, i):
                for j in range(4):
                    h = j % units
                    multiply(pe, u0 + 4 * g + j, t0 + per * g + j // units, i, 4, per, kt,
                             hi[h] if isinstance(hi, tuple) else hi[:, h * kt * S:(h + 1) * kt * S],
                             lo[h] if isinstance(lo, tuple) else lo[:, h * kt * S:(h + 1) * kt * S],
                             start=h == 0, stop=h == units - 1,
                             ready=(ready[0], ready[1] + h * kt) if g == 0 and j < units else None)
            groups(pe, 2 * units, body)

        def back_act(act, c, kt, units, kt_next):
            def body(g, i):
                for j in range(4):
                    act.wait_ge(unit_done, at(c["u"] + 4 * g + j + 1, i, 4))
                    u, last = c["u"] + 4 * g + j + 2, g == 2 * units - 1 and j >= 2
                    if not (last and kt_next is None):
                        split_hi(act, u, i, 4, kt_next if last else kt)
            groups(act, 2 * units, body)

        def back_dve(dve, c, kt, units, kt_next, dst=None):
            per = 4 // units

            def body(g, i):
                for j in range(4):
                    u, last = c["u"] + 4 * g + j + 2, g == 2 * units - 1 and j >= 2
                    if not (last and kt_next is None):
                        split_lo(dve, u, i, 4, kt_next if last else kt)
                    if (j + 1) % units == 0:
                        t, k = c["t"] + per * g + j // units, at(per * g + j // units, i, per)
                        x, y = (tile if i is None else dtile)(X, k), dst and (tile if i is None else dtile)(dst, k)
                        dve.wait_ge(unit_done, at(c["u"] + 4 * g + j + 1, i, 4))
                        if dst:
                            nc.vector.tensor_copy(y, acc[t % 2][:, :]).then_inc(acc_read, 1)
                        else:
                            nc.vector.tensor_tensor(x, x, acc[t % 2][:, :], ALU.add).then_inc(acc_read, 1)
            groups(dve, 2 * units, body)


        GH, GC, CH = 4, 8, 64
        off = [FREE]

        def scratch(name, tiles):
            t = place(name, tiles * S, off[0])
            off[0] += tiles * TILE
            assert off[0] <= TMP
            return t

        gla_kf, gla_q, gla_vf, gla_vtok = (scratch(n, k) for n, k in (("gla_kf", 4), ("gla_q", 4), ("gla_vf", 2), ("gla_vtok", 8)))
        gla_r, gla_o, gla_ktok, gla_s = (scratch(n, k) for n, k in (("gla_r", 8), ("gla_o", 8), ("gla_ktok", 4), ("gla_s", 4)))
        gla_low, gla_reset = scratch("gla_low", 1), gla_vf
        gla_low_, gla_decay = gla_low, place("gla_decay", GH * GC, FREE + 43 * TILE)
        gla_abs, gla_min, gla_cum, gla_exp0, gla_exp1 = (place(n, S, TMP + k * TILE) for k, n in
                                                         enumerate(("gla_abs", "gla_min", "gla_cum", "gla_exp0", "gla_exp1")))
        gla_exp = [gla_exp0, gla_exp1]
        gla_sq = [place(f"gla_sq{j}", S, FREE + j * TILE) for j in range(2)]
        gla_rs = [place(f"gla_rs{j}", S, FREE + (2 + j) * TILE) for j in range(4)]
        K0, V0, Q0, R0 = 1, 1 + GH, 1 + 3 * GH, 1 + 4 * GH

        g_gate, g_abs, g_soft, g_step, g_diff = (sem("gla_" + n) for n in ("gate_done", "abs_ready", "soft_ready", "dve_step", "diff_ready"))
        g_exp, g_kdec, g_kturned, g_kcopied = (sem("gla_" + n) for n in ("exp_ready", "kdec_ready", "k_turned", "k_copied"))
        g_vturned, g_vcopied, g_reset = (sem("gla_" + n) for n in ("v_turned", "v_copied", "reset_ready"))
        g_kv, g_state, g_odone, g_ocopied = (sem("gla_" + n) for n in ("kv_done", "state_ready", "o_done", "o_copied"))
        g_sq, g_sum, g_ln, g_rs, g_on = (sem("gla_" + n) for n in ("sq_ready", "sum_done", "ln_ready", "rs_ready", "o_normed"))

        def gla_act(act, c):
            u0, t0 = c["u"], c["t"]

            def read(j, out, func=ACT.Copy, scale=1.0, rows=P):
                act.wait_ge(unit_done, u0 + j + 1)
                split_hi(act, u0 + j + 2, None, 0, KD)
                act.wait_ge(scaled, c["scaled"] + j + 1)
                nc.scalar.activation(out, acc[(t0 + j) % 2][0:rows, :], func, scale=scale).then_inc(acc_read, 1)

            def gates(h):
                act.wait_ge(g_diff, h + 1)
                nc.scalar.activation(gla_exp[h % 2][:, :], gla_exp[h % 2][:, :], ACT.Exp,
                                     scale=1 / 16).then_inc(g_exp, 1)
                nc.scalar.activation(gla_decay[:, h * GC:(h + 1) * GC], gla_cum[:, CH - 1:S:CH], ACT.Exp,
                                     scale=1 / 16).then_inc(g_exp, 1)

            log_exp(act)
            read(0, gla_low[0:16, :], rows=16)
            for h in range(GH):
                read(K0 + h, tile(gla_kf, h))
                act.wait_ge(g_gate, h + 1)
                if h:
                    act.wait_ge(g_step, 3 * h - 1)
                nc.scalar.activation(gla_abs[:, :], bank[h % 2][:, :], ACT.Abs, bias=col("gla_b", h)).then_inc(g_abs, 1)
                act.wait_ge(g_abs, h + 1)
                nc.scalar.activation(gla_abs[:, :], gla_abs[:, :], ACT.Exp, scale=-1.0).then_inc(g_soft, 1)
                act.wait_ge(g_soft, 2 * h + 1)
                nc.scalar.activation(gla_abs[:, :], gla_abs[:, :], ACT.Ln, bias=1.0).then_inc(g_soft, 1)
                gates(h)
            for j in range(2 * GH):
                act.wait_ge(g_vturned, j - 1) if j >= 2 else act.wait_ge(g_reset, 2)
                if j == 0:
                    act.wait_ge(g_diff, GH)
                read(V0 + j, tile(gla_vf, j % 2))
            for h in range(GH):
                read(Q0 + h, tile(gla_q, h), scale=P ** -0.5)
            for j in range(2 * GH):
                read(R0 + j, tile(gla_r, j), ACT.Silu)
                if j:
                    gla_o_act(act, j - 1)
            gla_o_act(act, GC - 1)
            for j in range(2 * GH):
                if j >= 2:
                    act.wait_ge(g_sum, j - 1)
                act.wait_ge(g_ocopied, GC)
                nc.scalar.activation(gla_sq[j % 2][:, :], tile(gla_o, j), ACT.Square).then_inc(g_sq, 1)
            log_exp(act)
            for h in range(GH):
                act.wait_ge(g_sum, 2 * h + 2)
                nc.scalar.activation(gla_rs[h][:, :], bank[h][:, :], ACT.Ln, scale=1 / 256,
                                     bias=col("eps")).then_inc(g_ln, 1)
            for h in range(GH):
                act.wait_ge(g_ln, h + 1)
                nc.scalar.activation(gla_rs[h][:, :], gla_rs[h][:, :], ACT.Exp, scale=-0.5).then_inc(g_rs, 1)
            split_high(act, c)

        def gla_o_act(act, n):
            act.wait_ge(g_odone, n + 1)
            nc.scalar.activation(gla_o[:, :].rearrange("p (j t) -> p j t", t=S)[:, :, n * CH:(n + 1) * CH],
                                 bank[4 + n % 2][:, :].rearrange("p (j t) -> p j t", t=CH), ACT.Copy).then_inc(g_ocopied, 1)

        def split_high(act, c):
            for k in range(KD):
                act.wait_ge(hn_ready, c["hn"] + k + 1)
                nc.scalar.activation(tile(HH, k), hn[k % 2][:, :], ACT.Copy).then_inc(hh_ready, 1)

        def gla_dve(dve, c):
            u0, t0 = c["u"], c["t"]

            def lo(j):
                scale(dve, c, j)
                split_lo(dve, u0 + j + 2, None, 0, KD)

            def kdec(h):
                dve.wait_ge(g_exp, 2 * h + 1)
                dve.wait_ge(acc_read, t0 + K0 + h + 1)
                nc.vector.tensor_tensor(tile(gla_kf, h), tile(gla_kf, h), gla_exp[h % 2][:, :], ALU.mult).then_inc(g_kdec, 1)

            lo(0)
            dve.wait_ge(g_reset, 2)
            for h in range(GH):
                lo(K0 + h)
                b = bank[h % 2]
                dve.wait_ge(g_abs, h + 1)
                nc.vector.tensor_scalar(gla_min[:, :], b[:, :], col("gla_b", h), 0.0, ALU.add, ALU.min).then_inc(g_step, 1)
                dve.wait_ge(g_soft, 2 * h + 2)
                dve.wait_ge(g_step, 3 * h + 1)
                nc.vector.tensor_tensor(gla_min[:, :], gla_min[:, :], gla_abs[:, :], ALU.subtract).then_inc(g_step, 1)
                dve.wait_ge(g_step, 3 * h + 2)
                if h:
                    dve.wait_ge(g_exp, 2 * h)
                nc.vector.tensor_tensor_scan(gla_cum[:, :], tile(gla_reset, 0), gla_min[:, :], 0.0, ALU.mult,
                                             ALU.add).then_inc(g_step, 1)
                dve.wait_ge(g_step, 3 * h + 3)
                cum = gla_cum[:, :].rearrange("p (n t) -> p n t", t=CH)
                nc.vector.tensor_tensor(gla_exp[h % 2][:, :].rearrange("p (n t) -> p n t", t=CH),
                                        cum[:, :, CH - 1:CH].to_broadcast([P, GC, CH]), cum,
                                        ALU.subtract).then_inc(g_diff, 1)
                if h:
                    kdec(h - 1)
            for j in range(2 * GH):
                lo(V0 + j)
                if j == 0:
                    kdec(GH - 1)
                turned_v(dve, j - 1) if j else None
            for h in range(GH):
                lo(Q0 + h)
                if h == 0:
                    turned_v(dve, 2 * GH - 1)
                dve.wait_ge(g_kturned, h + 1)
                nc.vector.tensor_copy(tile(gla_ktok, h), bank[2 + h % 2][:, :]).then_inc(g_kcopied, 1)
            for n in range(GC):
                lo(R0 + n)
                for h in range(GH):
                    dve.wait_ge(g_kv, n + 1)
                    if n >= 2:
                        dve.wait_ge(g_odone, n - 1)
                    kv = bank[2 * (n % 2) + h // 2][:, (h % 2) * 256:(h % 2 + 1) * 256]
                    new = gla_s[:, (n % 2) * 1024 + h * 256:(n % 2) * 1024 + (h + 1) * 256]
                    old = gla_s[:, ((n + 1) % 2) * 1024 + h * 256:((n + 1) % 2) * 1024 + (h + 1) * 256]
                    if n == 0:
                        nc.vector.tensor_copy(new, kv).then_inc(g_state, 1)
                    else:
                        dve.wait_ge(g_state, 4 * (n - 1) + h + 1)
                        nc.vector.scalar_tensor_tensor(out=new, in0=old, scalar=gla_decay[:, h * GC + n:h * GC + n + 1],
                                                       in1=kv, op0=ALU.mult, op1=ALU.add).then_inc(g_state, 1)
            for k in range(KD):
                dve.wait_ge(g_rs, k // 2 + 1)
                nc.vector.scalar_tensor_tensor(out=tile(gla_o, k), in0=tile(gla_o, k), scalar=col("gla_gain", k % 2),
                                               in1=gla_rs[k // 2][:, :], op0=ALU.mult, op1=ALU.mult).then_inc(g_on, 1)
                if k >= 2:
                    dve.wait_ge(h_ready, c["h"] + k - 1)
                dve.wait_ge(g_on, k + 1)
                nc.vector.tensor_tensor(hn[k % 2][:, :], tile(gla_o, k), tile(gla_r, k), ALU.mult).then_inc(hn_ready, 1)

        def turned_v(dve, j):
            dve.wait_ge(g_vturned, j + 1)
            nc.vector.tensor_copy(gla_vtok[:, :].rearrange("p (c v) -> p c v", c=4)[:, :, j * P:(j + 1) * P],
                                  bank[4 + j % 2][:, :].rearrange("p (c v) -> p c v", c=4)).then_inc(g_vcopied, 1)

        def gla_pool(pool, c):
            pool.wait_ge(acc_read, c["t"] + 1)
            nc.gpsimd.memset(tile(gla_reset, 0), 1.0).then_inc(g_reset, 1)
            pool.wait_ge(g_reset, 1)
            nc.gpsimd.memset(tile(gla_reset, 0)[:, 0:S:CH], 0.0).then_inc(g_reset, 1)
            norm_pool(pool, c)

        def turn(pe, out, src):
            for k in range(4):
                last = nc.tensor.transpose(out[:, k * P:(k + 1) * P], src[:, k * P:(k + 1) * P], ident)
            return last

        def gla_pe(pe, c):
            u0, t0 = c["u"], c["t"]

            def mult(j, ready=None):
                multiply(pe, u0 + j, t0 + j, None, 0, 0, KD, HH, HL, ready=ready)

            def o_step(n):
                pe.wait_ge(g_state, 4 * n + 4)
                if n >= 2:
                    pe.wait_ge(g_ocopied, n - 1)
                for j in range(2 * GH):
                    last = nc.tensor.matmul(bank[4 + n % 2][:, j * CH:(j + 1) * CH],
                                            gla_s[:, (n % 2) * 1024 + j * P:(n % 2) * 1024 + (j + 1) * P],
                                            tile(gla_q, j // 2)[:, n * CH:(n + 1) * CH], start=True, stop=True)
                last.then_inc(g_odone, 1)

            pe.wait_ge(params_in, 48)
            mult(0, ready=(h_ready, c["h"] - KD))
            later_pe(pe, c["norm"])
            for h in range(GH):
                mult(K0 + h)
                pe.wait_ge(acc_read, t0 + 1)
                if h >= 2:
                    pe.wait_ge(g_step, 3 * (h - 2) + 1)
                nc.tensor.matmul(bank[h % 2][:, :], small[0:16, h * P:(h + 1) * P], gla_low[0:16, :],
                                 start=True, stop=True).then_inc(g_gate, 1)
            for j in range(2 * GH):
                mult(V0 + j)
                pe.wait_ge(acc_read, t0 + V0 + j + 1)
                if j >= 2:
                    pe.wait_ge(g_vcopied, j - 1)
                turn(pe, bank[4 + j % 2], tile(gla_vf, j % 2)).then_inc(g_vturned, 1)
            for h in range(GH):
                mult(Q0 + h)
                pe.wait_ge(g_kdec, h + 1)
                if h >= 2:
                    pe.wait_ge(g_kcopied, h - 1)
                turn(pe, bank[2 + h % 2], tile(gla_kf, h)).then_inc(g_kturned, 1)
            for n in range(GC):
                mult(R0 + n)
                pe.wait_ge(g_kcopied, GH)
                pe.wait_ge(g_vcopied, 2 * GH)
                if n >= 2:
                    pe.wait_ge(g_state, 4 * (n - 1))
                lo = CH * (n % 2)
                for h in range(GH):
                    last = nc.tensor.matmul(bank[2 * (n % 2) + h // 2][:, (h % 2) * 256:(h % 2 + 1) * 256],
                                            gla_ktok[lo:lo + CH, h * S + (n // 2) * P:h * S + (n // 2 + 1) * P],
                                            gla_vtok[lo:lo + CH, (n // 2) * D + h * 256:(n // 2) * D + (h + 1) * 256],
                                            start=True, stop=True)
                last.then_inc(g_kv, 1)
                if n:
                    o_step(n - 1)
            o_step(GC - 1)
            for j in range(2 * GH):
                pe.wait_ge(g_sq, j + 1)
                nc.tensor.matmul(bank[j // 2][:, :], ones, gla_sq[j % 2][:, :], start=j % 2 == 0,
                                 stop=j % 2 == 1).then_inc(g_sum, 1)


        off[0] = FREE
        NP, HD = 4, 64
        MH = place("MH", KD * S, off[0], F32R)
        ML = place("ML", KD * S, off[0] + KD * TILE, F32R)
        off[0] += 2 * KD * TILE
        sb_sp, sb_w, sb_vtok, sb_xb = (scratch(n, 4) for n in ("sb_sp", "sb_w", "sb_vtok", "sb_xb"))
        sb_raw, sb_qn, sb_kn, sb_win = (scratch(n, 2) for n in ("sb_raw", "sb_qn", "sb_kn", "sb_win"))
        sb_vf, sb_pooled = sb_w, sb_sp
        b_vturned, b_vcopied, b_win, b_count, b_pooled, b_pool = (sem("sb_" + n) for n in (
            "v_turned", "v_copied", "window_step", "counted", "pooled", "pool_projected"))
        b_sq, b_sum, b_ln, b_rs, b_n = (sem("sb_" + n) for n in ("sq_ready", "sum_done", "ln_ready", "rs_ready", "qk_normed"))
        b_z, b_abs, b_soft, b_sp, b_arg, b_w, b_o = (sem("sb_" + n) for n in (
            "z_done", "act_step", "log_ready", "softplus_ready", "arg_done", "weights_ready", "o_done"))
        b_gain = sem("sb_gain_scaled")
        sb_qgain = place("sb_qgain", 1, TMP - 32)
        sb_rs, sb_ln = scratch("sb_rs", 1), scratch("sb_ln", 1)

        def span(kb):
            return slice(kb * P, S)

        def sb_act(act, c):
            u0, t0 = c["u"], c["t"]

            def read(j, out):
                act.wait_ge(unit_done, u0 + j + 1)
                split_hi(act, u0 + j + 2, None, 0, KD)
                act.wait_ge(scaled, c["scaled"] + j + 1)
                nc.scalar.activation(out, acc[(t0 + j) % 2][:, :], ACT.Copy).then_inc(acc_read, 1)

            def high(k):
                act.wait_ge(hn_ready, c["hn"] + k + 1)
                nc.scalar.activation(tile(MH, k), hn[k % 2][:, :], ACT.Copy).then_inc(hh_ready, 1)

            def read_qk(m):
                if m >= 2:
                    act.wait_ge(b_n, m - 1)
                if m == 0:
                    act.wait_ge(b_win, 20)
                read(8 + m, tile(sb_raw, m % 2))
                act.wait_ge(acc_read, t0 + 8 + m + 1)
                if m:
                    act.wait_ge(b_sum, m)
                nc.scalar.activation(sq[0][:, :], tile(sb_raw, m % 2), ACT.Square).then_inc(b_sq, 1)

            def rms_qk(m):
                act.wait_ge(b_sum, m + 1)
                if m:
                    act.wait_ge(b_n, m)
                nc.scalar.activation(sb_ln[:, :], bank[5][:, :], ACT.Ln, scale=1 / HD, bias=col("eps")).then_inc(b_ln, 1)
                act.wait_ge(b_ln, m + 1)
                nc.scalar.activation(sb_rs[:, :], sb_ln[:, :], ACT.Exp, scale=-0.5).then_inc(b_rs, 1)

            nc.scalar.activation(sb_qgain[:, :], col("sb_gain"), ACT.Copy, scale=HD ** -0.5).then_inc(b_gain, 1)
            for j in range(4):
                if j >= 2:
                    act.wait_ge(b_vturned, j - 1)
                read(j, tile(sb_vf, j % 2))
            for j in range(4):
                read(4 + j, tile(sb_xb, j))
            log_exp(act)
            read_qk(0)
            rms_qk(0)
            high(0)
            high(1)
            read_qk(1)
            rms_qk(1)
            high(2)
            high(3)
            for h in range(2 * NP):
                for kb in (3, 2, 1, 0):
                    step = 8 * h + 2 * (3 - kb)
                    a = tile(sb_sp, kb)[:, span(kb)]
                    act.wait_ge(b_z, 4 * h + 4 - kb)
                    nc.scalar.activation(a, bank[kb][:, span(kb)], ACT.Abs).then_inc(b_abs, 1)
                    act.wait_ge(b_abs, step + 1)
                    nc.scalar.activation(a, a, ACT.Exp, scale=-1.0).then_inc(b_abs, 1)
                    act.wait_ge(b_abs, step + 2)
                    nc.scalar.activation(a, a, ACT.Ln, bias=1.0).then_inc(b_soft, 1)
                if h < 6:
                    read_qk(2 + h)
                for kb in (3, 2, 1, 0):
                    act.wait_ge(b_arg, 4 * h + 4 - kb)
                    if h:
                        act.wait_ge(b_o, h)
                    nc.scalar.activation(tile(sb_w, kb)[:, span(kb)], bank[kb][:, span(kb)], ACT.Exp).then_inc(b_w, 1)
                if h < 6:
                    rms_qk(2 + h)
                if h % 2 == 0 and h:
                    high(4 + h // 2 - 1)
            high(7)

        def log_exp(act):
            nc.scalar.preload_act_table_set("natural_log_exp_and_others")

        def sb_dve(dve, c):
            u0, t0 = c["u"], c["t"]

            def lo(j):
                scale(dve, c, j)
                split_lo(dve, u0 + j + 2, None, 0, KD)

            def turned(j):
                dve.wait_ge(b_vturned, j + 1)
                nc.vector.tensor_copy(sb_vtok[:, :].rearrange("p (c v) -> p c v", c=4)[:, :, j * P:(j + 1) * P],
                                      bank[j % 2][:, :].rearrange("p (c v) -> p c v", c=4)).then_inc(b_vcopied, 1)

            def to_hn(k, wait, src, scalar):
                dve.wait_ge(*wait)
                if k >= 2:
                    dve.wait_ge(h_ready, c["h"] + k - 1)
                nc.vector.tensor_scalar(hn[k % 2][:, :], src, scalar, None, ALU.mult).then_inc(hn_ready, 1)

            def pooled(g):
                dve.wait_ge(b_win, 2 * (g + 1) + g * (g + 1))
                w, win = 2 << g, tile(sb_win, g % 2)
                nc.vector.tensor_tensor(win[:, 0:16], win[:, 0:16], col("pool_count", 16 * g, 16), ALU.mult).then_inc(b_count, 1)
                dve.wait_ge(b_count, g + 1)
                if g >= 2:
                    dve.wait_ge(b_pool, g - 1)
                nc.vector.scalar_tensor_tensor(out=tile(sb_pooled, g % 2), in0=win, scalar=1.0 / w, in1=tile(sb_xb, g),
                                               op0=ALU.mult, op1=ALU.subtract).then_inc(b_pooled, 1)

            def normed(m):
                dve.wait_ge(b_rs, m + 1)
                dst = tile((sb_qn, sb_kn)[m % 2], m // 2 % 2)
                if m >= 4:
                    dve.wait_ge(b_arg, 8 * (m // 2 - 1))
                gain = sb_qgain[:, 0:1] if m % 2 == 0 else col("sb_gain", 1)
                nc.vector.scalar_tensor_tensor(out=dst, in0=tile(sb_raw, m % 2), scalar=gain,
                                               in1=sb_rs[:, :], op0=ALU.mult, op1=ALU.mult).then_inc(b_n, 1)

            for j in range(4):
                lo(j)
                turned(j - 1) if j else None
            for j in range(4):
                lo(4 + j)
                turned(3) if j == 0 else None
                if j:
                    pooled(j - 1)
                if j >= 2:
                    to_hn(j - 2, (b_pool, j - 1), bank[2 + j % 2][:, :], col("pool_scale", j - 2))
            dve.wait_ge(b_gain, 1)
            lo(8)
            pooled(3)
            normed(0)
            to_hn(2, (b_pool, 3), bank[2][:, :], col("pool_scale", 2))
            lo(9)
            normed(1)
            to_hn(3, (b_pool, 4), bank[3][:, :], col("pool_scale", 3))
            for h in range(2 * NP):
                for kb in (3, 2, 1, 0):
                    a = tile(sb_sp, kb)[:, span(kb)]
                    dve.wait_ge(b_soft, 4 * h + 4 - kb)
                    nc.vector.scalar_tensor_tensor(out=a, in0=bank[kb][:, span(kb)], scalar=0.0, in1=a,
                                                   op0=ALU.max, op1=ALU.add).then_inc(b_sp, 1)
                if h < 6:
                    lo(10 + h)
                if h % 2 == 0 and h:
                    to_hn(4 + h // 2 - 1, (b_o, h), bank[4][:, :], 1.0)
                if h < 6:
                    normed(2 + h)
            to_hn(7, (b_o, 8), bank[4][:, :], 1.0)

        def sb_pool(pool, c):
            step = 0
            for g in range(4):
                src, win = tile(sb_xb, g), tile(sb_win, g % 2)
                pool.wait_ge(acc_read, c["t"] + 4 + g + 1)
                for d in range(g + 1):
                    sh, dst = 1 << d, win if (g - d) % 2 == 0 else tile(sb_raw, 0)
                    if g >= 2 and d <= 1:
                        pool.wait_ge(b_pooled, g - 1)
                    if step:
                        pool.wait_ge(b_win, step)
                    nc.gpsimd.tensor_copy(dst[:, 0:sh], src[:, 0:sh]).then_inc(b_win, 1)
                    nc.gpsimd.tensor_tensor(dst[:, sh:S], src[:, sh:S], src[:, 0:S - sh], ALU.add).then_inc(b_win, 1)
                    src, step = dst, step + 2
            for k in range(KD):
                pool.wait_ge(hh_ready, c["hh"] + k + 1)
                nc.gpsimd.tensor_tensor(tile(ML, k), hn[k % 2][:, :], tile(MH, k).bitcast(F32),
                                        ALU.subtract).then_inc(h_ready, 1)

        def sb_pe(pe, c):
            u0, t0 = c["u"], c["t"]

            def mult(j, ready=None):
                multiply(pe, u0 + j, t0 + j, None, 0, 0, KD, HH, HL, ready=ready)

            pe.wait_ge(params_in, 48)

            def project_pool(g):
                pe.wait_ge(b_pooled, g + 1)
                if g >= 2:
                    pe.wait_ge(hn_ready, c["hn"] + g - 1)
                nc.tensor.matmul(bank[2 + g % 2][:, :], small[:, S + g * P:S + (g + 1) * P], tile(sb_pooled, g % 2),
                                 start=True, stop=True).then_inc(b_pool, 1)

            def sum_qk(m):
                pe.wait_ge(b_sq, m + 1)
                if m:
                    pe.wait_ge(b_ln, m)
                nc.tensor.matmul(bank[5][:, :], halves, sq[0][:, :], start=True, stop=True).then_inc(b_sum, 1)

            def scores(h):
                i, r = h // 2, slice(HD * (h % 2), HD * (h % 2) + HD)
                if h % 2 == 0:
                    pe.wait_ge(b_n, 2 * i + 2)
                if h == 0:
                    pe.wait_ge(hn_ready, c["hn"] + 4)
                for kb in (3, 2, 1, 0):
                    if h:
                        pe.wait_ge(b_w, 4 * h - kb)
                    nc.tensor.matmul(bank[kb][:, span(kb)], tile(sb_kn, i % 2)[r, kb * P:(kb + 1) * P],
                                     tile(sb_qn, i % 2)[r, span(kb)], start=True, stop=False, skip_group_check=True)
                    nc.tensor.matmul(bank[kb][:, kb * P:(kb + 1) * P], ident, hidden, start=False, stop=True,
                                     skip_group_check=True).then_inc(b_z, 1)

            def sums(h):
                for kb in (3, 2, 1, 0):
                    pe.wait_ge(b_sp, 4 * h + 4 - kb)
                    last = nc.tensor.matmul(bank[kb][:, span(kb)], neg_lower, tile(sb_sp, kb)[:, span(kb)],
                                            start=False, stop=kb == 3, skip_group_check=True)
                    for jb in range(kb + 1, 4):
                        last = nc.tensor.matmul(bank[kb][:, span(jb)], neg_ones, tile(sb_sp, jb)[:, span(jb)],
                                                start=False, stop=jb == 3, skip_group_check=True)
                    last.then_inc(b_arg, 1)

            def values(h):
                r = slice(HD * (h % 2), HD * (h % 2) + HD)
                pe.wait_ge(b_w, 4 * h + 4)
                if h and h % 2 == 0:
                    pe.wait_ge(hn_ready, c["hn"] + 4 + h // 2)
                for kb in range(4):
                    last = nc.tensor.matmul(bank[4][r, span(kb)], sb_vtok[:, kb * S + h * HD:kb * S + (h + 1) * HD],
                                            tile(sb_w, kb)[:, span(kb)], start=kb == 0, stop=kb == 3)
                last.then_inc(b_o, 1)

            for j in range(4):
                mult(j, ready=(h_ready, c["h"] - KD) if j == 0 else None)
                if j == 0:
                    later_pe(pe, c["norm"])
                pe.wait_ge(acc_read, t0 + j + 1)
                if j >= 2:
                    pe.wait_ge(b_vcopied, j - 1)
                turn(pe, bank[j % 2], tile(sb_vf, j % 2)).then_inc(b_vturned, 1)
            for j in range(4):
                mult(4 + j)
                if j >= 2:
                    project_pool(j - 2)
            mult(8)
            project_pool(2)
            sum_qk(0)
            mult(9)
            sum_qk(1)
            project_pool(3)
            for h in range(2 * NP):
                if h == 0:
                    pe.wait_ge(b_vcopied, 4)
                scores(h)
                if h:
                    values(h - 1)
                if h < 6:
                    mult(10 + h)
                sums(h)
                if h < 6:
                    sum_qk(2 + h)
            values(7)


        NC, NH = S // P, 8
        off[0] = FREE

        def scratch1(name, n, dt=F32):
            t = place(name, n * S, off[0], dt)
            off[0] += n * TILE
            assert off[0] <= FREE + 32 * TILE
            return t

        O = place("O", 16 * S, FREE + 32 * TILE)
        OH = place("OH", 8 * S, FREE, F32R)
        OL = place("OL", 8 * S, FREE + 16 * TILE, F32R)
        Y1 = place("Y1", 8 * S, FREE + 32 * TILE)
        tab0 = FREE + 48 * TILE
        t_soft, t_ld, t_exp, t_nbe, t_beta, t_neg, t_sum, t_negsum = (place(n, k, tab0 + 4 * o) for n, k, o in (
            ("t_soft", 128, 0), ("t_ld", 96, 128), ("t_exp", 288, 224), ("t_nbe", 32, 512), ("t_beta", 32, 544),
            ("t_neg", 24, 576), ("t_sum", 32, 600), ("t_negsum", 32, 632)))
        conv_out = scratch1("conv_out", 4)
        l_qt, l_kt, l_qd, l_gb, l_ed, l_edt, l_a, l_qk, l_vb, l_kd = (scratch1("l_" + n, 1) for n in (
            "qt", "kt", "qd", "gb", "ed", "edt", "a", "qk", "vb", "kd"))
        l_m = [scratch1(f"l_m{j}", 1) for j in range(2)]
        l_x, l_xt, l_yt, l_small, l_z, l_t = (scratch1("l_" + n, 1) for n in ("x", "xt", "yt", "small", "z", "t"))
        l_rs = [scratch1(f"l_rs{j}", 1) for j in range(2)]
        l_sq = [scratch1(f"l_sq{j}", 1) for j in range(3)]
        l_r = l_small[:, 0:P]
        l_vn = [l_small[:, P:2 * P], l_small[:, 2 * P:3 * P]]
        l_state = l_small[:, 3 * P:4 * P]

        def chunk(t, k):
            return t[:, k * P:(k + 1) * P]

        def by_chunk(t):
            return t[:, :].rearrange("p (c n) -> p c n", c=NC)

        def half_blocks(t, l, odd):
            return t.rearrange("p (m two b) -> p m two b", two=2, b=1 << l)[:, :, odd, :]

        def each_chunk(m):
            return m.unsqueeze(1).to_broadcast([P, NC, P])

        def head_of(table, cols_, base, h0, i):
            v = table[:, base:base + NC * cols_].rearrange("p (c n) -> p c n", c=NC)
            v = v[:, :, h0:h0 + 1] if i is None else v[:, :, bass.ds(i + h0, 1)]
            return v.to_broadcast([P, NC, P])

        def head_col(table, k, h0, i):
            return table[:, k + h0:k + h0 + 1] if i is None else table[:, bass.ds(i + (k + h0), 1)]

        a_steps, a_pe, a_dve = sem("tables_act"), sem("tables_pe"), sem("tables_dve")

        def tables_in_act(act, c):
            act.wait_ge(unit_done, c["u"] + 1)
            split_hi(act, c["u"] + 2, None, 0, KD)
            nc.scalar.activation(l_x[0:32, :], acc[c["t"] % 2][0:32, :], ACT.Copy).then_inc(acc_read, 1)

        def tables_act(act):
            nc.scalar.activation(t_neg[:, :], col("rows", 24, 24), ACT.Exp).then_inc(a_steps, 1)
            act.wait_ge(a_dve, 2)
            nc.scalar.activation(l_t[:, 0:128], l_a[:, 0:128], ACT.Abs).then_inc(a_steps, 1)
            act.wait_ge(a_steps, 2)
            nc.scalar.activation(l_t[:, 0:128], l_t[:, 0:128], ACT.Exp, scale=-1.0).then_inc(a_steps, 1)
            act.wait_ge(a_steps, 3)
            nc.scalar.activation(l_t[:, 0:128], l_t[:, 0:128], ACT.Ln, bias=1.0).then_inc(a_steps, 1)

        def beta_act(act):
            act.wait_ge(a_dve, 3)
            beta = t_beta[:, :].rearrange("p (c n) -> p c n", c=NC)
            nc.scalar.activation(beta, by_chunk(t_soft)[:, :, 0:8], ACT.Exp, scale=-1.0).then_inc(a_steps, 1)

        def sums_exp_act(act):
            act.wait_ge(a_pe, 4)
            nc.scalar.activation(t_exp[:, :], bank[1][:, 0:288], ACT.Exp).then_inc(a_steps, 1)
            sums = bank[1][:, 0:96].rearrange("p (c n) -> p c n", c=NC)[:, :, 0:8]
            for table, sign in ((t_sum, 1.0), (t_negsum, -1.0)):
                nc.scalar.activation(table[:, :].rearrange("p (c n) -> p c n", c=NC), sums, ACT.Copy,
                                     scale=sign).then_inc(a_steps, 1)

        def tables_dve(dve):
            dve.wait_ge(a_pe, 1)
            arg, ps = l_a[:, 0:128].rearrange("p (c n) -> p c n", c=NC), bank[0][:, 0:128].rearrange("p (c n) -> p c n", c=NC)
            nc.vector.tensor_scalar(arg[:, :, 0:8], ps[:, :, 0:8], -1.0, None, ALU.mult).then_inc(a_dve, 1)
            nc.vector.tensor_tensor(arg[:, :, 8:32], ps[:, :, 8:32],
                                    col("rows", 0, 24).unsqueeze(1).to_broadcast([P, NC, 24]), ALU.add).then_inc(a_dve, 1)

        def softplus_dve(dve):
            dve.wait_ge(a_steps, 4)
            dve.wait_ge(a_dve, 2)
            nc.vector.scalar_tensor_tensor(out=t_soft[:, :], in0=l_a[:, 0:128], scalar=0.0, in1=l_t[:, 0:128],
                                           op0=ALU.max, op1=ALU.add).then_inc(a_dve, 1)
            dve.wait_ge(a_dve, 3)
            nc.vector.scalar_tensor_tensor(out=t_ld[:, :].rearrange("p (c n) -> p c n", c=NC),
                                           in0=by_chunk(t_soft)[:, :, 8:32], scalar=-1.0,
                                           in1=t_neg[:, :].unsqueeze(1).to_broadcast([P, NC, 24]),
                                           op0=ALU.mult, op1=ALU.mult).then_inc(a_dve, 1)

        def beta_exp_dve(dve):
            dve.wait_ge(a_steps, 6)
            eg = t_exp[:, 0:96].rearrange("p (c n) -> p c n", c=NC)[:, :, 0:8]
            nc.vector.scalar_tensor_tensor(out=t_nbe[:, :].rearrange("p (c n) -> p c n", c=NC), in0=eg, scalar=-1.0,
                                           in1=t_beta[:, :].rearrange("p (c n) -> p c n", c=NC),
                                           op0=ALU.mult, op1=ALU.mult).then_inc(a_dve, 1)

        def tables_pe(pe, c):
            pe.wait_ge(acc_read, c["t"] + 1)
            for k in range(NC):
                last = nc.tensor.transpose(bank[0][:, 32 * k:32 * k + 32], chunk(l_x, k)[0:32, :], ident[0:32, 0:32])
            last.then_inc(a_pe, 1)

        def chunk_sums_pe(pe):
            pe.wait_ge(a_dve, 4)
            for k, m in enumerate((upper, ones, lower)):
                nc.tensor.matmul(bank[1][:, 96 * k:96 * k + 96], m, t_ld[:, :], start=True, stop=True).then_inc(a_pe, 1)

        c_tap, c_step, c_silu, c_free = sem("l_tap_ready"), sem("l_conv_step"), sem("l_silu_ready"), sem("l_slot_free")

        class Slots:

            def __init__(self, c, h0, i, u, t, cols_, taps_):
                self.c, self.i, self.h0 = c, i, h0
                self.u, self.t, self.cols, self.taps = u, t, cols_, taps_

        def slots(c, h0, i=None):
            return Slots(c, h0, i, c["u"] + 1 + 4 * h0, c["t"] + 1 + 4 * h0,
                         cols.start["conv"] + 15 * h0 if h0 < NH else cols.start["ssd_conv"], 3 if h0 < NH else 4)

        def conv_col(s, j, m):
            k = s.cols + 5 * j + m
            return par[:, k:k + 1] if s.i is None else par[:, bass.ds(s.i * 15 + k, 1)]

        def slot_act(act, s, j):
            act.wait_ge(unit_done, at(s.u + j + 1, s.i, 4))
            split_hi(act, s.u + j + 2, s.i, 4, KD)
            if j < s.taps:
                if s.h0:
                    act.wait_ge(*[(c_qt, at(s.h0, s.i, 1)), (c_kt, at(s.h0, s.i, 1)), (p_vt, at(s.h0, s.i, 1)),
                                  (g_z, at(s.h0, s.i, 1))][j])
                nc.scalar.activation(tile(conv_out, j), acc[(s.t + j) % 2][:, :], ACT.Identity, scale=conv_col(s, j, 3),
                                     bias=conv_col(s, j, 4)).then_inc(c_tap, 1)

        def slot_lo(dve, s, j):
            split_lo(dve, s.u + j + 2, s.i, 4, KD)

        def slot_tap(dve, s, j, m):
            a, o = acc[(s.t + j) % 2], tile(conv_out, j)
            if j >= s.taps:
                if m == 3:
                    dve.wait_ge(unit_done, at(s.u + j + 1, s.i, 4))
                    if s.h0:
                        dve.wait_ge(g_z, at(s.h0, s.i, 1))
                    nc.vector.tensor_copy(o, a[:, :]).then_inc(acc_read, 1)
                return
            step = 2 * (3 * s.h0 + j)
            if m == 1:
                dve.wait_ge(c_tap, at(3 * s.h0 + j + 1, s.i, 3))
            else:
                dve.wait_ge(c_step, at(step + m - 1, s.i, 6))
            nc.vector.scalar_tensor_tensor(out=o[:, m:S], in0=a[:, 0:S - m], scalar=conv_col(s, j, 3 - m), in1=o[:, m:S],
                                           op0=ALU.mult, op1=ALU.add).then_inc(acc_read if m == 3 else c_step, 1)

        def slot_silu(act, s, j):
            act.wait_ge(acc_read, at(s.t + j + 1, s.i, 4))
            nc.scalar.activation(tile(conv_out, j), tile(conv_out, j), ACT.Silu).then_inc(c_silu, 1)

        def squares_act(act, s):
            for j in range(2):
                act.wait_ge(c_silu, at(4 * s.h0 + j + 1, s.i, 4))
                nc.scalar.activation(l_sq[j][:, :], tile(conv_out, j), ACT.Square).then_inc(s_sq, 1)

        def slot_pe(pe, s, j, part=None):
            multiply(pe, s.u + j, s.t + j, s.i, 4, 4, KD, HH, HL, part=part)

        g_gb, g_etm, g_qd, g_m, g_x0, g_z, g_o = (sem("l_" + n) for n in (
            "gb_ready", "edt_masked", "qd_ready", "m_ready", "x0_ready", "z_kept", "o_ready"))
        s_sq, s_ln, s_rs, s_egb, s_ed, s_edt, s_yt, s_vn, s_relu, s_sqo = (sem("l_" + n) for n in (
            "sq_ready", "ln_ready", "rs_ready", "egb_ready", "ed_ready", "edt_ready", "yt_copied", "vn_copied", "relu_ready", "o_squared"))
        p_sum, p_gcb, p_vt, p_kk, p_qk, p_kt, p_m0t = (sem("l_" + n) for n in (
            "sum_done", "gcb_done", "v_turned", "kk_done", "qk_done", "k_turned", "m0_turned"))
        p_yt, p_xyt, p_xy, p_p1, p_vn, p_s, p_o = (sem("l_" + n) for n in (
            "yt_done", "xyt_done", "xy_done", "p1_done", "vn_done", "s_done", "o_done"))
        c_qt, c_kt, c_vb, c_a, c_qk, c_kd, c_xt, c_x, c_r, c_st, c_t = (sem("l_" + n) for n in (
            "qt_ready", "kt_ready", "vb_ready", "a_ready", "qk_ready", "kd_ready", "xt_ready", "x_ready", "r_ready",
            "state_ready", "t_ready"))

        def gdn_act(act, s, h0, i):
            def n(base, per=1):
                return at(base + per * h0, i, per)

            def rms(k, width, src, out):
                act.wait_ge(p_sum, n(k + 1, 3))
                nc.scalar.activation(out[:, :], src[:, :], ACT.Ln, scale=1.0 / width, bias=col("eps")).then_inc(s_ln, 1)
                act.wait_ge(s_ln, n(k + 1, 3))
                nc.scalar.activation(out[:, :], out[:, :], ACT.Exp, scale=-0.5).then_inc(s_rs, 1)

            def decays(out, sign, sums, ready, step):
                for k in range(NC):
                    nc.scalar.activation(chunk(out, k), chunk(bank[4], k), ACT.Relu, scale=sign,
                                         bias=head_col(sums, 8 * k, h0, i)).then_inc(s_relu, 1)
                act.wait_ge(s_relu, n(4 * step + 4, 8))
                nc.scalar.activation(out[:, :], out[:, :], ACT.Exp, scale=-1.0).then_inc(ready, 1)

            def copy_vn(k):
                act.wait_ge(p_vn, n(k + 1, 4))
                nc.scalar.activation(l_vn[k % 2], bank[0][:, P:2 * P], ACT.Copy).then_inc(s_vn, 1)

            act.wait_ge(p_gcb, n(1))
            decays(l_ed, 1.0, t_negsum, s_ed, 0)
            if h0 or i is not None:
                act.wait_ge(c_t, n(0))
            for k in range(2):
                rms(k, 1.0, bank[k], l_rs[k])
            decays(l_edt, -1.0, t_sum, s_edt, 1)
            nc.scalar.activation(l_gb[:, :], bank[4][:, :], ACT.Exp).then_inc(s_egb, 1)
            slot_act(act, s, 0)
            for l in range(1, 7):
                act.wait_ge(p_yt, n(l, 6))
                nc.scalar.activation(l_yt[:, :], bank[4][:, :], ACT.Copy).then_inc(s_yt, 1)
                if l == 4:
                    slot_act(act, s, 1)
            copy_vn(0)
            act.wait_ge(g_z, n(1))
            nc.scalar.activation(l_z[:, :], l_z[:, :], ACT.Silu).then_inc(c_silu, 1)
            slot_silu(act, s, 0)
            slot_silu(act, s, 1)
            slot_act(act, s, 2)
            copy_vn(1)
            if s.taps == 3:
                squares_act(act, s)
            copy_vn(2)
            copy_vn(3)
            slot_silu(act, s, 2)
            act.wait_ge(p_o, n(1))
            nc.scalar.activation(l_sq[2][:, :], bank[2][:, :], ACT.Square).then_inc(s_sqo, 1)
            slot_act(act, s, 3)
            log_exp(act)
            rms(2, P, bank[3], l_rs[0])

        def gdn_dve(dve, s, h0, i):
            def n(base, per=1):
                return at(base + per * h0, i, per)

            dve.wait_ge(s_rs, n(1, 3))
            nc.vector.scalar_tensor_tensor(out=l_qt[:, :], in0=tile(conv_out, 0), scalar=P ** -0.5, in1=l_rs[0][:, :],
                                           op0=ALU.mult, op1=ALU.mult).then_inc(c_qt, 1)
            dve.wait_ge(s_rs, n(2, 3))
            nc.vector.tensor_tensor(l_kt[:, :], tile(conv_out, 1), l_rs[1][:, :], ALU.mult).then_inc(c_kt, 1)
            dve.wait_ge(p_vt, n(1))
            nc.vector.tensor_tensor(by_chunk(l_vb), by_chunk(bank[5]), head_of(t_beta, 8, 0, h0, i), ALU.mult).then_inc(c_vb, 1)
            dve.wait_ge(p_kk, n(1))
            dve.wait_ge(s_ed, n(1))
            for k in range(NC):
                last = nc.vector.scalar_tensor_tensor(out=chunk(l_a, k), in0=chunk(bank[0], k),
                                                      scalar=head_col(t_beta, 8 * k, h0, i), in1=chunk(l_ed, k),
                                                      op0=ALU.mult, op1=ALU.mult)
            last.then_inc(c_a, 1)
            dve.wait_ge(p_qk, n(1))
            dve.wait_ge(g_etm, n(1))
            nc.vector.tensor_tensor(l_qk[:, :], bank[1][:, :], l_edt[:, :], ALU.mult).then_inc(c_qk, 1)
            dve.wait_ge(p_kt, n(1))
            nc.vector.tensor_tensor(by_chunk(l_kd), by_chunk(bank[2]), head_of(t_exp, 24, 192, h0, i), ALU.mult).then_inc(c_kd, 1)
            dve.wait_ge(p_m0t, n(1))
            nc.vector.tensor_tensor(by_chunk(l_xt), each_chunk(ident), by_chunk(bank[3]), ALU.subtract).then_inc(c_xt, 1)
            slot_lo(dve, s, 0)

            def stream(k):
                slot_tap(dve, s, k // 4, k % 4) if k % 4 else slot_lo(dve, s, k // 4)

            def update(x, y, l, odd):
                x = half_blocks(x[:, :], l, odd)
                return nc.vector.tensor_tensor(x, x, y[:, 0:S // 2].rearrange("p (m b) -> p m b", b=1 << l), ALU.subtract)

            for l in range(1, 7):
                dve.wait_ge(p_xyt, n(l, 6))
                dve.wait_ge(c_xt, n(l, 7))
                update(l_xt, bank[5], l, 1).then_inc(c_xt, 1)
                if l < 6:
                    dve.wait_ge(p_xy, n(l, 5))
                    dve.wait_ge(g_x0, n(1)) if l == 1 else dve.wait_ge(c_x, n(l - 1, 5))
                    update(l_x, bank[3], l, 0).then_inc(c_x, 1)
                stream(l)
            stream(7)

            def state(k):
                dve.wait_ge(p_s, n(k + 1, 3))
                if k == 0:
                    nc.vector.tensor_copy(l_state, bank[1][:, 0:P]).then_inc(c_st, 1)
                else:
                    dve.wait_ge(c_st, n(k, 3))
                    nc.vector.scalar_tensor_tensor(out=l_state, in0=l_state, scalar=head_col(t_exp, 96 + 24 * k, h0, i),
                                                   in1=bank[1][:, 0:P], op0=ALU.mult, op1=ALU.add).then_inc(c_st, 1)

            def rest(k):
                dve.wait_ge(p_p1, n(k, 3))
                nc.vector.scalar_tensor_tensor(out=l_r, in0=bank[0][:, 0:P], scalar=head_col(t_nbe, 8 * k, h0, i),
                                               in1=chunk(l_vb, k), op0=ALU.mult, op1=ALU.add).then_inc(c_r, 1)

            state(0)
            rest(1)
            state(1)
            stream(8)
            rest(2)
            state(2)
            stream(9)
            rest(3)
            for k in range(10, 16):
                stream(k)
            dve.wait_ge(s_rs, n(3, 3))
            if i is not None or h0:
                dve.wait_ge(g_o, n(0))
            nc.vector.scalar_tensor_tensor(out=l_t[:, :], in0=bank[2][:, :], scalar=col("gdn_norm"), in1=l_rs[0][:, :],
                                           op0=ALU.mult, op1=ALU.mult).then_inc(c_t, 1)

        def decays_pool(pool, h0, i):
            if h0 or i is not None:
                pool.wait_ge(g_qd, at(h0, i, 1))
            nc.gpsimd.tensor_tensor(by_chunk(l_gb), head_of(t_ld, 24, 0, h0, i), each_chunk(ones), ALU.mult).then_inc(g_gb, 1)

        def gdn_pool(pool, s, h0, i):
            def n(base, per=1):
                return at(base + per * h0, i, per)

            def mask(l):
                if l >= 2:
                    pool.wait_ge(p_m0t, n(1)) if l == 2 else pool.wait_ge(p_yt, n(l - 2, 6))
                nc.gpsimd.tensor_tensor(by_chunk(l_m[l % 2]), by_chunk(l_a), each_chunk(level[l]), ALU.mult).then_inc(g_m, 1)

            pool.wait_ge(s_edt, n(1))
            nc.gpsimd.tensor_tensor(by_chunk(l_edt), by_chunk(l_edt), each_chunk(upper), ALU.mult).then_inc(g_etm, 1)
            pool.wait_ge(c_a, n(1))
            mask(0)
            mask(1)
            pool.wait_ge(g_m, n(1, 7))
            nc.gpsimd.tensor_tensor(by_chunk(l_x), each_chunk(ident), by_chunk(l_m[0]), ALU.subtract).then_inc(g_x0, 1)
            pool.wait_ge(g_x0, n(1))
            mask(2)
            pool.wait_ge(c_qt, n(1))
            pool.wait_ge(s_egb, n(1))
            nc.gpsimd.tensor_tensor(l_qd[:, :], l_qt[:, :], l_gb[:, :], ALU.mult).then_inc(g_qd, 1)
            pool.wait_ge(acc_read, at(s.t, s.i, 4))
            if h0 or i is not None:
                pool.wait_ge(g_o, n(0))
            nc.gpsimd.tensor_tensor(by_chunk(l_z), tile(conv_out, 3).rearrange("p (c n) -> p c n", c=NC),
                                    each_chunk(ones), ALU.mult).then_inc(g_z, 1)
            for l in range(3, 7):
                mask(l)
            if s.taps == 3:
                decays_pool(pool, h0 + 1, i)
            pool.wait_ge(c_t, n(1))
            pool.wait_ge(c_silu, n(4, 4))
            nc.gpsimd.tensor_tensor(tile(O, h0) if i is None else O[:, bass.ds(i * S + h0 * S, S)], l_t[:, :], l_z[:, :],
                                    ALU.mult).then_inc(g_o, 1)

        def gdn_pe(pe, s, h0, i):
            def n(base, per=1):
                return at(base + per * h0, i, per)

            def four(out, lhs, rhs):
                for k in range(NC):
                    last = nc.tensor.matmul(chunk(out, k), chunk(lhs, k) if lhs is not upper else upper,
                                            chunk(rhs, k) if rhs is not upper and rhs is not ident else rhs, start=True, stop=True)
                return last

            def blocks(out, lhs, rhs, l, odd):
                for k in range(NC):
                    last = nc.tensor.matmul(out[:, 64 * k:64 * k + 64].rearrange("p (m b) -> p m b", b=1 << l),
                                            chunk(lhs, k), half_blocks(chunk(rhs, k), l, odd), start=True, stop=True)
                return last

            pe.wait_ge(g_gb, n(1))
            four(bank[4], l_gb, upper).then_inc(p_gcb, 1)
            for k in range(2):
                pe.wait_ge(s_sq, n(k + 1, 2))
                nc.tensor.matmul(bank[k][:, :], ones, l_sq[k][:, :], start=True, stop=True).then_inc(p_sum, 1)
            slot_pe(pe, s, 0, 0)
            pe.wait_ge(c_silu, n(3, 4))
            turn(pe, bank[5], tile(conv_out, 2)).then_inc(p_vt, 1)
            slot_pe(pe, s, 0, 1)
            pe.wait_ge(c_kt, n(1))
            four(bank[0], l_kt, l_kt).then_inc(p_kk, 1)
            pe.wait_ge(c_qt, n(1))
            four(bank[1], l_kt, l_qt).then_inc(p_qk, 1)
            if h0 or i is not None:
                pe.wait_ge(c_t, n(0))
            turn(pe, bank[2], l_kt).then_inc(p_kt, 1)
            slot_pe(pe, s, 0, 2)
            pe.wait_ge(g_m, n(1, 7))
            four(bank[3], l_m[0], ident).then_inc(p_m0t, 1)
            slot_pe(pe, s, 0, 3)
            pe.wait_ge(s_egb, n(1))
            pe.wait_ge(c_vb, n(1))
            for l in range(1, 7):
                pe.wait_ge(g_m, n(l + 1, 7))
                pe.wait_ge(c_xt, n(l, 7))
                four(bank[4], l_m[l % 2], l_xt).then_inc(p_yt, 1)
                slot_pe(pe, s, *divmod(l + 3, 4))
                pe.wait_ge(s_yt, n(l, 6))
                pe.wait_ge(g_x0, n(1)) if l == 1 else pe.wait_ge(c_x, n(l - 1, 5))
                blocks(bank[5], l_x, l_yt, l, 1).then_inc(p_xyt, 1)
                if l < 6:
                    blocks(bank[3], l_yt, l_x, l, 0).then_inc(p_xy, 1)
            pe.wait_ge(c_qk, n(1))
            pe.wait_ge(c_kd, n(1))
            pe.wait_ge(g_qd, n(1))
            for k in range(NC):
                if k:
                    pe.wait_ge(c_st, n(k, 3))
                    nc.tensor.matmul(bank[0][:, 0:P], chunk(l_kt, k), l_state, start=True, stop=True).then_inc(p_p1, 1)
                    slot_pe(pe, s, *divmod(11 + k, 4))
                    pe.wait_ge(c_r, n(k, 3))
                else:
                    pe.wait_ge(c_xt, n(7, 7))
                nc.tensor.matmul(bank[0][:, P:2 * P], chunk(l_xt, k), l_r if k else chunk(l_vb, 0), start=True,
                                 stop=True).then_inc(p_vn, 1)
                if k == 0:
                    slot_pe(pe, s, 2, 2)
                pe.wait_ge(s_vn, n(k + 1, 4))
                if k < NC - 1 and k:
                    nc.tensor.matmul(chunk(bank[2], k), l_state, chunk(l_qd, k), start=True, stop=False, skip_group_check=True)
                if k < NC - 1:
                    nc.tensor.matmul(bank[1][:, 0:P], chunk(l_kd, k), l_vn[k % 2], start=True, stop=True).then_inc(p_s, 1)
                elif k:
                    nc.tensor.matmul(chunk(bank[2], k), l_state, chunk(l_qd, k), start=True, stop=False, skip_group_check=True)
                last = nc.tensor.matmul(chunk(bank[2], k), l_vn[k % 2], chunk(l_qk, k), start=k == 0, stop=True,
                                        skip_group_check=True)
                if k == 0:
                    slot_pe(pe, s, 2, 3)
            last.then_inc(p_o, 1)
            slot_pe(pe, s, 3, 3)
            pe.wait_ge(s_sqo, n(1))
            nc.tensor.matmul(bank[3][:, :], ones, l_sq[2][:, :], start=True, stop=True).then_inc(p_sum, 1)

        def heads(eng, c, head):
            head(eng, slots(c, 1), 0, None)
            with eng.Fori(0, NH - 2) as i:
                head(eng, slots(c, 2, i), 1, i)
            head(eng, slots(c, NH), NH - 1, None)

        def gdn_first(c, act=None, dve=None, pe=None):
            s = slots(c, 0)
            for j in range(4):
                if act:
                    slot_act(act, s, j)
                    if j == 0:
                        tables_act(act)
                    if j == 1:
                        beta_act(act)
                if dve:
                    if j == 0:
                        tables_dve(dve)
                    slot_lo(dve, s, j)
                    for m in (1, 2, 3):
                        slot_tap(dve, s, j, m)
                    if j == 0:
                        softplus_dve(dve)
                if pe:
                    slot_pe(pe, s, j)
                    if j == 0:
                        tables_pe(pe, c)
            if act:
                for j in range(3):
                    slot_silu(act, s, j)
                squares_act(act, s)


        def at_tile(name, k, n=1):
            return place(name, n * S, FREE + k * TILE)

        x_rest, b_c, x_second = at_tile("sd_x_rest", 4, 2), at_tile("sd_b_c", 6, 2), at_tile("sd_x_second", 8, 4)
        sd_b, sd_c = [tile(conv_out, 0), tile(b_c, 0)], [tile(conv_out, 1), tile(b_c, 1)]
        sd_x = [[tile(conv_out, 2), tile(conv_out, 3), tile(x_rest, 0), tile(x_rest, 1)],
                [tile(x_second, k) for k in range(4)]]
        sd_z, sd_btok, sd_xdt, sd_cbm, sd_xdd, sd_ytok, sd_t, sd_st = (at_tile("sd_" + n, k, m) for n, k, m in (
            ("z", 12, 4), ("btok", 16, 1), ("xdt", 17, 4), ("cbm", 25, 1), ("xdd", 26, 1), ("ytok", 27, 1), ("t", 28, 1),
            ("st", 29, 1)))
        sd_u, sd_e, sd_sq = ([at_tile(f"sd_{n}{j}", k + j) for j in range(2)] for n, k in (("u", 21), ("e", 23), ("sq", 30)))
        d_u, d_xdd, d_scaled = sem("ssd_u_ready"), sem("ssd_xdd_ready"), sem("ssd_state_scaled")
        d_bt, d_cb, d_d, d_xt, d_yo, d_yd, d_s, d_yt, d_sum = (sem("ssd_" + n) for n in (
            "b_turned", "cb_done", "decay_done", "x_turned", "yoff_done", "ydiag_done", "state_done", "y_turned", "sum_done"))
        d_e, d_sq, d_ln, d_rs, d_zs = (sem("ssd_" + n) for n in ("exp_ready", "sq_ready", "ln_ready", "rs_ready", "z_silu"))
        d_btok, d_cbm, d_xdt, d_g, d_t, d_ytok, d_st, d_yf, d_yg, d_o = (sem("ssd_" + n) for n in (
            "btok_ready", "cbm_ready", "xdt_ready", "g_ready", "t_ready", "ytok_ready", "state_ready", "yf_ready",
            "gated", "o_ready"))

        def of_heads(table, col0, heads_, width):
            return table[:, col0:col0 + heads_].unsqueeze(2).to_broadcast([P, heads_, width])

        def by_head(t, heads_=8):
            return t[:, :].rearrange("p (h n) -> p h n", h=heads_)

        REST = [(sd_x[0][2], 4), (sd_x[0][3], 5)] + [(tile(sd_z, k), None) for k in range(4)] + [
            (sd_b[1], 6), (sd_c[1], 7)] + [(sd_x[1][k], 8 + k) for k in range(4)] + [
            (tile(sd_z, k), None) for k in range(4)]

        def unit_counts(c, k):
            return c["u"] + 37 + k, c["t"] + 37 + k, 24 + (REST[k][1] or 0)

        def rest_act(act, c, k):
            u, t, m = unit_counts(c, k)
            act.wait_ge(unit_done, u + 1)
            split_hi(act, u + 2, None, 0, KD)
            if REST[k][1]:
                w = cols.start["ssd_conv"] + 5 * REST[k][1]
                nc.scalar.activation(REST[k][0][:, :], acc[t % 2][:, :], ACT.Identity, scale=par[:, w + 3:w + 4],
                                     bias=par[:, w + 4:w + 5]).then_inc(c_tap, 1)

        def rest_dve(dve, c, k):
            u, t, m = unit_counts(c, k)
            o, a = REST[k][0], acc[t % 2]
            split_lo(dve, u + 2, None, 0, KD)
            if REST[k][1]:
                w = cols.start["ssd_conv"] + 5 * REST[k][1]
                dve.wait_ge(c_tap, m + 1)
                for b in (1, 2, 3):
                    if b > 1:
                        dve.wait_ge(c_step, 2 * m + b - 1)
                    nc.vector.scalar_tensor_tensor(out=o[:, b:S], in0=a[:, 0:S - b], scalar=par[:, w + 3 - b:w + 4 - b],
                                                   in1=o[:, b:S], op0=ALU.mult, op1=ALU.add
                                                   ).then_inc(acc_read if b == 3 else c_step, 1)
            else:
                dve.wait_ge(unit_done, u + 1)
                nc.vector.tensor_copy(o[:, :], a[:, :]).then_inc(acc_read, 1)

        def rest_silu(act, c, k, done=None):
            act.wait_ge(acc_read, c["t"] + 37 + k + 1)
            o = REST[k][0]
            nc.scalar.activation(o[:, :], o[:, :], ACT.Silu).then_inc(done or c_silu, 1)

        def rest_pe(pe, c, k, part=None):
            u, t, _ = unit_counts(c, k)
            multiply(pe, u, t, None, 0, 0, KD, HH, HL, part=part)

        def ssd_act(act, c):
            def chunks(g, first):
                log_exp(act)
                for k in range(NC):
                    n = 4 * g + k
                    for q in range(2):
                        act.wait_ge(d_d, 2 * n + q + 1)
                        if n:
                            act.wait_ge(d_yd, n)
                        nc.scalar.activation(sd_e[q][:, :], bank[q][:, :], ACT.Exp).then_inc(d_e, 1)
                    rest_act(act, c, first + k)
                for k in range(NC):
                    rest_silu(act, c, first + k, d_zs)

            def gate(g):
                log_exp(act)
                for k in range(4):
                    act.wait_ge(d_yg, 4 * g + k + 1)
                    if k >= 2:
                        act.wait_ge(d_sum, 4 * g + k - 1)
                    nc.scalar.activation(sd_sq[k % 2][:, :], sd_x[g][k], ACT.Square).then_inc(d_sq, 1)
                act.wait_ge(d_sum, 4 * g + 4)
                nc.scalar.activation(sd_t[:, :], bank[3][:, :], ACT.Ln, scale=1 / 512, bias=col("eps")).then_inc(d_ln, 1)
                act.wait_ge(d_ln, g + 1)
                nc.scalar.activation(sd_t[:, :], sd_t[:, :], ACT.Exp, scale=-0.5).then_inc(d_rs, 1)

            act.wait_ge(g_o, NH)
            slot_silu(act, slots(c, NH), 3)
            for k in range(2):
                rest_act(act, c, k)
            for k in range(2):
                rest_silu(act, c, k)
            chunks(0, 2)
            rest_act(act, c, 6)
            gate(0)
            for k in range(7, 12):
                rest_act(act, c, k)
            for k in range(6, 12):
                rest_silu(act, c, k)
            chunks(1, 12)
            for k in range(8):
                nc.scalar.activation(tile(HH, k), tile(O, k), ACT.Copy).then_inc(hh_ready, 1)
            gate(1)
            for k in range(8):
                act.wait_ge(d_o, k + 1)
                nc.scalar.activation(tile(OH, k), tile(O, 8 + k), ACT.Copy).then_inc(hh_ready, 1)

        def ssd_dve(dve, c):
            def start(g):
                dve.wait_ge(d_bt, g + 1)
                nc.vector.tensor_copy(sd_btok[:, :], bank[4][:, :]).then_inc(d_btok, 1)
                dve.wait_ge(d_cb, g + 1)
                nc.vector.tensor_tensor(by_chunk(sd_cbm), by_chunk(bank[5]), each_chunk(upper), ALU.mult).then_inc(d_cbm, 1)

            def chunks(g, first):
                for k in range(NC):
                    n, head0 = 4 * g + k, 8 + 8 * g
                    dve.wait_ge(d_xt, n + 1)
                    nc.vector.tensor_tensor(by_head(tile(sd_xdt, k)), by_head(bank[2]),
                                            of_heads(t_soft, 32 * k + 16 + 8 * g, 8, 64), ALU.mult).then_inc(d_xdt, 1)
                    for q in range(2):
                        dve.wait_ge(d_e, 2 * n + q + 1)
                        dve.wait_ge(d_cbm, g + 1)
                        nc.vector.tensor_tensor(by_chunk(sd_e[q]), by_chunk(sd_e[q]), each_chunk(chunk(sd_cbm, k)),
                                                ALU.mult).then_inc(d_g, 1)
                    if n:
                        dve.wait_ge(d_yt, n)
                    if k:
                        dve.wait_ge(d_yo, 3 * g + k)
                        nc.vector.tensor_tensor(by_head(sd_t), by_head(bank[3]), of_heads(t_exp, 24 * k + head0, 8, 64),
                                                ALU.mult).then_inc(d_t, 1)
                        dve.wait_ge(d_yd, n + 1)
                        dve.wait_ge(d_t, 3 * g + k)
                        nc.vector.tensor_tensor(sd_ytok[:, :], sd_t[:, :], bank[4][:, :], ALU.add).then_inc(d_ytok, 1)
                    else:
                        dve.wait_ge(d_yd, n + 1)
                        nc.vector.tensor_copy(sd_ytok[:, :], bank[4][:, :]).then_inc(d_ytok, 1)
                    if k < NC - 1:
                        dve.wait_ge(d_s, 3 * g + k + 1)
                        if k:
                            dve.wait_ge(d_scaled, 2 * g + k)
                            nc.vector.tensor_tensor(sd_st[:, :], sd_st[:, :], bank[2][:, :], ALU.add).then_inc(d_st, 1)
                        else:
                            nc.vector.tensor_copy(sd_st[:, :], bank[2][:, :]).then_inc(d_st, 1)
                    if g and k == 0:
                        dve.wait_ge(d_yg, 4)
                    rest_dve(dve, c, first + k)
                    dve.wait_ge(d_yt, n + 1)
                    for j in range(4):
                        x = chunk(sd_x[g][j], k)
                        last = nc.vector.scalar_tensor_tensor(out=x, in0=x, scalar=col("ssd_d", 4 * g + j),
                                                              in1=chunk(bank[5], j), op0=ALU.mult, op1=ALU.add)
                    last.then_inc(d_yf, 1)

            def gated(g):
                for k in range(4):
                    dve.wait_ge(d_zs, 4 * g + k + 1)
                    dve.wait_ge(d_yf, 4 * g + 4)
                    x = sd_x[g][k]
                    nc.vector.tensor_tensor(x, x, tile(sd_z, k), ALU.mult).then_inc(d_yg, 1)

            def normed(g):
                dve.wait_ge(d_rs, g + 1)
                for k in range(4):
                    nc.vector.scalar_tensor_tensor(out=tile(O, 8 + 4 * g + k), in0=sd_x[g][k],
                                                   scalar=col("ssd_norm", 4 * g + k), in1=sd_t[:, :], op0=ALU.mult,
                                                   op1=ALU.mult).then_inc(d_o, 1)

            dve.wait_ge(g_o, NH)
            rest_dve(dve, c, 0)
            rest_dve(dve, c, 1)
            start(0)
            chunks(0, 2)
            gated(0)
            rest_dve(dve, c, 6)
            normed(0)
            for k in range(7, 12):
                rest_dve(dve, c, k)
            start(1)
            chunks(1, 12)
            gated(1)
            for k in range(8):
                dve.wait_ge(hh_ready, c["hh"] + k + 1)
                nc.vector.tensor_tensor(tile(HL, k), tile(O, k), tile(HH, k).bitcast(F32), ALU.subtract).then_inc(h_ready, 1)
            normed(1)
            for k in range(8):
                dve.wait_ge(hh_ready, c["hh"] + 8 + k + 1)
                nc.vector.tensor_tensor(tile(OL, k), tile(O, 8 + k), tile(OH, k).bitcast(F32), ALU.subtract).then_inc(h_ready, 1)

        def ssd_pool(pool, c):
            def u_of(g, k):
                n = 4 * g + k
                for q in range(2):
                    if n:
                        pool.wait_ge(d_d, 2 * (n - 1) + q + 1)
                    nc.gpsimd.tensor_tensor(by_chunk(sd_u[q]), of_heads(t_ld, 24 * k + 8 + 8 * g + 4 * q, 4, P),
                                            each_chunk(lower), ALU.mult).then_inc(d_u, 1)

            pool.wait_ge(g_o, NH)
            u_of(0, 0)
            for g in range(2):
                for k in range(NC):
                    n = 4 * g + k
                    if k < NC - 1:
                        u_of(g, k + 1)
                        pool.wait_ge(d_xdt, n + 1)
                        if 3 * g + k:
                            pool.wait_ge(d_s, 3 * g + k)
                        nc.gpsimd.tensor_tensor(by_head(sd_xdd), by_head(tile(sd_xdt, k)),
                                                of_heads(t_exp, 192 + 24 * k + 8 + 8 * g, 8, 64), ALU.mult).then_inc(d_xdd, 1)
                        if k:
                            pool.wait_ge(d_yo, 3 * g + k)
                            pool.wait_ge(d_st, 3 * g + k)
                            nc.gpsimd.tensor_tensor(by_head(sd_st), by_head(sd_st),
                                                    of_heads(t_exp, 96 + 24 * k + 8 + 8 * g, 8, 64), ALU.mult).then_inc(d_scaled, 1)
                    elif g == 0:
                        u_of(1, 0)

        def ssd_pe(pe, c):
            def decays(g, k):
                n = 4 * g + k
                for q in range(2):
                    pe.wait_ge(d_u, 2 * n + q + 1)
                    if n:
                        pe.wait_ge(d_e, 2 * (n - 1) + q + 1)
                    for j in range(4):
                        last = nc.tensor.matmul(chunk(bank[q], j), chunk(sd_u[q], j), upper, start=True, stop=True)
                    last.then_inc(d_d, 1)

            def start(g):
                pe.wait_ge(c_silu, 38 + 6 * g)
                if g:
                    pe.wait_ge(d_ytok, 4 * g)
                    pe.wait_ge(d_yf, 4 * g)
                turn(pe, bank[4], sd_b[g]).then_inc(d_bt, 1)
                for k in range(NC):
                    last = nc.tensor.matmul(chunk(bank[5], k), chunk(sd_b[g], k), chunk(sd_c[g], k), start=True, stop=True)
                last.then_inc(d_cb, 1)
                decays(g, 0)

            def chunks(g, first):
                for k in range(NC):
                    n = 4 * g + k
                    if k:
                        pe.wait_ge(d_st, 3 * g + k)
                    for j in range(4):
                        last = nc.tensor.transpose(chunk(bank[2], j), chunk(sd_x[g][j], k), ident)
                    last.then_inc(d_xt, 1)
                    rest_pe(pe, c, first + k, 0)
                    rest_pe(pe, c, first + k, 1)
                    if k:
                        if n > 1:
                            pe.wait_ge(d_t, 3 * g + k - 1)
                        nc.tensor.matmul(bank[3][:, :], chunk(sd_c[g], k), sd_st[:, :], start=True, stop=True).then_inc(d_yo, 1)
                    pe.wait_ge(d_xdt, n + 1)
                    pe.wait_ge(d_g, 2 * n + 2)
                    pe.wait_ge(d_btok, g + 1)
                    if n:
                        pe.wait_ge(d_ytok, n)
                    for j in range(8):
                        last = nc.tensor.matmul(bank[4][:, 64 * j:64 * j + 64], chunk(sd_e[j // 4], j % 4),
                                                tile(sd_xdt, k)[:, 64 * j:64 * j + 64], start=True, stop=True)
                    last.then_inc(d_yd, 1)
                    if k < NC - 1:
                        pe.wait_ge(d_xdd, 3 * g + k + 1)
                        nc.tensor.matmul(bank[2][:, :], chunk(sd_btok, k), sd_xdd[:, :], start=True, stop=True).then_inc(d_s, 1)
                        decays(g, k + 1)
                    rest_pe(pe, c, first + k, 2)
                    rest_pe(pe, c, first + k, 3)
                    pe.wait_ge(d_ytok, n + 1)
                    pe.wait_ge(d_yf, n) if n else pe.wait_ge(d_cbm, 1)
                    for j in range(4):
                        last = nc.tensor.transpose(chunk(bank[5], j), chunk(sd_ytok, j), ident)
                    last.then_inc(d_yt, 1)

            def sums(g):
                for k in range(4):
                    pe.wait_ge(d_sq, 4 * g + k + 1)
                    nc.tensor.matmul(bank[3][:, :], ones, sd_sq[k % 2][:, :], start=k == 0, stop=k == 3).then_inc(d_sum, 1)

            rest_pe(pe, c, 0)
            rest_pe(pe, c, 1)
            pe.wait_ge(g_o, NH)
            start(0)
            chunks(0, 2)
            rest_pe(pe, c, 6)
            sums(0)
            for k in range(7, 12):
                rest_pe(pe, c, k)
            start(1)
            chunks(1, 12)
            sums(1)

        def l1_act(act, c):
            log_exp(act)
            tables_in_act(act, c)
            gdn_first(c, act=act)
            log_exp(act)
            sums_exp_act(act)
            act.wait_ge(a_steps, 8)
            heads(act, c, lambda eng, s, h0, i: gdn_act(eng, s, h0, i))
            ssd_act(act, c)

        def l1_dve(dve, c):
            split_lo(dve, c["u"] + 2, None, 0, KD)
            gdn_first(c, dve=dve)
            beta_exp_dve(dve)
            dve.wait_ge(a_dve, 5)
            heads(dve, c, lambda eng, s, h0, i: gdn_dve(eng, s, h0, i))
            ssd_dve(dve, c)

        def l1_pool(pool, c):
            pool.wait_ge(a_dve, 4)
            decays_pool(pool, 0, None)
            heads(pool, c, lambda eng, s, h0, i: gdn_pool(eng, s, h0, i))
            ssd_pool(pool, c)

        def l1_pe(pe, c):
            multiply(pe, c["u"], c["t"], None, 0, 0, KD, HH, HL, ready=(h_ready, c["h"] - KD))
            gdn_first(c, pe=pe)
            chunk_sums_pe(pe)
            pe.wait_ge(a_steps, 8)
            heads(pe, c, lambda eng, s, h0, i: gdn_pe(eng, s, h0, i))
            ssd_pe(pe, c)

        n = dict(u=0, t=0, sq=0, rms=0, hn=0, h=0, ffn=0, pair=0, scaled=0, ssum=0, add=0, hh=0, tap=0, conv=0, x=0, w8=0, w11=0)
        made = lambda k: (x_loaded[k // 2], 16)
        stages = []
        for at_, (kind, arg) in enumerate(plan):
            c = dict(n)
            if kind == "norm":
                stages.append((kind, arg, c, made))
                for key, more in (("sq", KD), ("ssum", KD), ("rms", 1), ("hn", KD), ("hh", KD), ("h", KD)):
                    n[key] += more
            elif kind == "later":
                stages.append((kind, arg, c, made))
                for key, more in (("sq", KD), ("ssum", KD - POOLED + 1), ("add", POOLED - 1), ("rms", 1), ("hh", KD), ("h", KD)):
                    n[key] += more
                n["norm"] = c
            elif kind == "post":
                stages.append((kind, arg, c, Y1 if plan[at_ - 1][0] == "project1" else Y))
                for key, more in (("sq", KD), ("ssum", KD), ("rms", 1), ("hn", KD), ("x", KD)):
                    n[key] += more
                made = lambda k, x0=c["x"]: (x_ready, x0 + k + 1)
            elif kind == "up":
                stages.append((kind, arg, c, None))
                for key, more in (("u", 2 * KF), ("t", 2 * KF), ("w8", 2 * KF), ("ffn", 1), ("pair", KF), ("scaled", 2 * KF),
                                  ("tap", 2 * KF), ("conv", 2 * KF)):
                    n[key] += more
            elif kind == "gla":
                stages.append((kind, arg, c, None))
                for key, more in (("u", 25), ("t", 25), ("w8", 25), ("scaled", 25), ("hn", KD), ("hh", KD), ("h", KD)):
                    n[key] += more
            elif kind == "l1":
                stages.append((kind, arg, c, None))
                for key, more in (("u", 53), ("t", 53), ("w8", 53), ("hh", 2 * KD), ("h", 2 * KD)):
                    n[key] += more
            elif kind == "project1":
                stages.append((kind, arg, c, all(k == "post" for k, _ in plan[at_ + 1:])))
                for key, more in (("u", 2 * KD), ("t", KD), ("w8", 2 * KD)):
                    n[key] += more
            elif kind == "sb":
                stages.append((kind, arg, c, None))
                for key, more in (("u", 16), ("t", 16), ("w8", 16), ("scaled", 16), ("hn", KD), ("hh", KD), ("h", KD)):
                    n[key] += more
            elif kind == "project":
                stages.append((kind, arg, c, at_ == len(plan) - 1))
                for key, more in (("u", KD), ("t", KD), ("w8", KD)):
                    n[key] += more
                made = lambda k, t0=c["t"]: (acc_read, t0 + k + 1)
            elif kind == "down":
                stages.append((kind, arg, c, at_ == len(plan) - 1 or all(k == "post" for k, _ in plan[at_ + 1:])))
                for key, more in (("u", 2 * KD), ("t", KD), ("w11", 2 * KD)):
                    n[key] += more
                made = lambda k, t0=c["t"]: (acc_read, t0 + k + 1)

        block = ctx.enter_context(nc.Block())

        @block.sync
        def _(sp):
            sp.dma_start(cst[:, :], cst_in).then_inc(params_in, 16)
            sp.dma_start(par[:, :], par_in).then_inc(params_in, 16)
            for k in range(0, KD, 2):
                sp.dma_start(X[:, k * S:(k + 2) * S], x_in[:, k * S:(k + 2) * S]).then_inc(x_loaded[k // 2], 16)
            for kind, arg, c, _ in stages:
                if kind == "l1" or stages[1][0] != "l1" and c is stages[0][2]:
                    sp.dma_start(small[:, :], small_in).then_inc(params_in, 16)
                if kind == "up":
                    load_units(sp, w8, c["w8"], c["u"], 2 * KF)
                if kind == "gla":
                    load_units(sp, w8, c["w8"], c["u"], 25)
                if kind == "l1":
                    load_units(sp, w8, c["w8"], c["u"], 53)
                if kind == "project1":
                    load_units(sp, w8, c["w8"], c["u"], 2 * KD)
                if kind == "sb":
                    load_units(sp, w8, c["w8"], c["u"], 16)
                if kind == "project":
                    load_units(sp, w8, c["w8"], c["u"], KD)
                if kind == "down":
                    load_units(sp, w11, c["w11"], c["u"], 2 * KD)
            for k in range(KD):
                sp.wait_ge(*made(k))
                sp.dma_start(out[:, k * S:(k + 1) * S], tile(X, k)).then_inc(out_stored, 16)
            sp.wait_ge(out_stored, 16 * KD)

        @block.scalar
        def _(act):
            act.wait_ge(params_in, 32)
            if plan[0][0] == "later":
                for u in range(SPLIT):
                    split_hi(act, u, None, 0, KD)
            for kind, arg, c, more in stages:
                if kind == "norm":
                    norm_act(act, c, more)
                elif kind == "later":
                    later_act(act, c, arg, more)
                elif kind == "post":
                    post_act(act, c, more)
                elif kind == "up":
                    up_act(act, c)
                elif kind == "l1":
                    l1_act(act, c)
                elif kind == "project1":
                    back_act(act, c, KD, 2, None if more else KD)
                elif kind == "sb":
                    sb_act(act, c)
                elif kind == "gla":
                    gla_act(act, c)
                elif kind == "project":
                    back_act(act, c, KD, 1, None if more else KD)
                elif kind == "down":
                    back_act(act, c, HALF, 2, None if more else KD)

        @block.vector
        def _(dve):
            dve.wait_ge(params_in, 32)
            if plan[0][0] == "later":
                for u in range(SPLIT):
                    split_lo(dve, u, None, 0, KD)
            else:
                split_lo(dve, 0, None, 0, KD)
            for kind, arg, c, more in stages:
                if kind == "norm":
                    scaled_dve(dve, c, X, arg, h_ready, c["h"])
                    split_lo(dve, 1, None, 0, KD)
                elif kind == "later":
                    later_dve(dve, c, arg)
                elif kind == "post":
                    scaled_dve(dve, c, more, arg, x_ready, c["x"])
                elif kind == "up":
                    up_dve(dve, c)
                elif kind == "l1":
                    l1_dve(dve, c)
                elif kind == "project1":
                    back_dve(dve, c, KD, 2, None if more else KD, Y1)
                elif kind == "sb":
                    sb_dve(dve, c)
                elif kind == "gla":
                    gla_dve(dve, c)
                elif kind == "project":
                    back_dve(dve, c, KD, 1, None if more else KD)
                elif kind == "down":
                    back_dve(dve, c, HALF, 2, None if more else KD, Y if arg else None)

        @block.gpsimd
        def _(pool):
            for kind, arg, c, more in stages:
                if kind == "norm":
                    norm_pool(pool, c)
                elif kind == "later":
                    later_pool(pool, c)
                elif kind == "post":
                    post_pool(pool, c)
                elif kind == "l1":
                    l1_pool(pool, c)
                elif kind == "sb":
                    sb_pool(pool, c)
                elif kind == "gla":
                    gla_pool(pool, c)
                elif kind == "up":
                    up_pool(pool, c)

        @block.tensor
        def _(pe):
            pe.wait_ge(params_in, 32)
            for kind, arg, c, more in stages:
                if kind in ("norm", "post"):
                    sums_pe(pe, c, KD)
                elif kind == "up":
                    up_pe(pe, c)
                elif kind == "l1":
                    l1_pe(pe, c)
                elif kind == "project1":
                    back_pe(pe, c, KD, 2, (HH, OH), (HL, OL), (h_ready, c["h"] - 2 * KD))
                elif kind == "sb":
                    sb_pe(pe, c)
                elif kind == "gla":
                    gla_pe(pe, c)
                elif kind == "project":
                    back_pe(pe, c, KD, 1, *((HH, HL) if arg == "HH" else (MH, ML)), (h_ready, c["h"] - KD))
                elif kind == "down":
                    back_pe(pe, c, HALF, 2, FH, FL, (f_ready, c["pair"] - KF))


def channels(a):
    return a.reshape(-1, P).T


def units(w, kt):
    k, m = w.shape
    return w.reshape(k // (kt * P), kt, P, m // P, P).transpose(3, 0, 2, 1, 4).reshape(-1, P, kt * P)


def pairs(w):
    k, m = w.shape
    return w.reshape(k, 2, m // 2 // P, P).transpose(0, 2, 1, 3).reshape(k, m)


def constants():
    r = np.arange(P)
    p, f = r[:, None], r[None, :]
    parts = [p == f, np.ones((P, P)), p <= f, p > f, p // 64 == f // 64]
    for b in (1, 2, 4, 8, 16, 32, 64):
        parts.append((p // (2 * b) == f // (2 * b)) & (p // b % 2 == 1) & (f // b % 2 == 0))
    parts += [np.where(p >= f, -1.0, 0.0), -np.ones((P, P)), np.where(p >= f, -1e30, 0.0)]
    return np.concatenate([np.asarray(a, np.float32) for a in parts], axis=1)


def tile_of(w, j):
    return w[:, j * P:(j + 1) * P]


PLAN = [("norm", ("g_pre_mix", 0)), ("l1", None), ("project1", None), ("post", ("g_post_mix", 0)),
        ("later", ("g_pre_ffn", 0)), ("up", 0), ("down", True), ("post", ("g_post_ffn", 0)),
        ("later", ("g_even", 0)), ("sb", None), ("project", "MH"),
        ("later", ("g_ffn_2", 0)), ("up", 1), ("down", False),
        ("later", ("g_odd", 0)), ("gla", None), ("project", "HH"),
        ("later", ("g_ffn_2", KD)), ("up", 2), ("down", False)]


def kernel(**a):
    import concourse.bacc as bacc
    from concourse.bass_utils import run_bass_kernel_spmd as run

    a = {name: np.asarray(value) for name, value in a.items()}
    x = a.pop("x")
    ffn_norm, ffn_up, ffn_down = a["ffn_norm_2"], a["ffn_w_up_2"], a["ffn_w_down_2"]
    ffn_conv = [np.concatenate([a["ffn_conv_w"][0], a["ffn_conv_b"][0][None]])] + [
        np.concatenate([a["ffn_conv_w_2"][k], a["ffn_conv_b_2"][k][None]]) for k in range(2)]
    a = {name: value[0] for name, value in a.items()}

    cols = columns()
    par = np.zeros((P, cols.n), np.float32)

    def put(name, value):
        par[:, cols.start[name]:cols.start[name] + value.shape[1]] = value

    put("eps", np.full((P, 1), EPS, np.float32))
    for name, source in (("g_pre_mix", "pre_mix_norm"), ("g_post_mix", "post_mix_norm"), ("g_pre_ffn", "pre_ffn_norm"),
                         ("g_post_ffn", "post_ffn_norm"), ("g_even", "mix_norm_even_2"), ("g_odd", "mix_norm_odd_2"),
                         ("gdn_norm", "gdn_norm_w"), ("ssd_norm", "ssd_norm_w"), ("pool_scale", "pool_scale_2"),
                         ("gla_b", "gla_b_a_2"), ("gla_gain", "gla_o_gain_2")):
        put(name, channels(a[source]))
    put("g_ffn_2", channels(ffn_norm))
    put("ssd_d", channels(np.repeat(a["ssd_d"], 64)))
    put("sb_gain", np.stack([np.tile(a["sb_q_gain_2"], 2), np.tile(a["sb_k_gain_2"], 2)], 1))
    put("ffn", np.concatenate([pairs(f).reshape(4, 2 * KF, P).transpose(2, 1, 0).reshape(P, -1) for f in ffn_conv], 1))
    taps = np.concatenate([a["gdn_conv_w"], np.zeros((1, 3 * D), np.float32)])
    put("conv", taps.reshape(5, 3, 8, P).transpose(3, 2, 1, 0).reshape(P, -1))
    taps = np.concatenate([a["ssd_conv_w"], a["ssd_conv_b"][None]]).reshape(5, 12, P)
    put("ssd_conv", taps[:, [8, 10, 0, 1, 2, 3, 9, 11, 4, 5, 6, 7]].transpose(2, 1, 0).reshape(P, -1))
    put("rows", np.tile(np.concatenate([a[n] for n in ("gdn_dt_bias", "ssd_dt_bias", "gdn_a_log", "ssd_a_log")]), (P, 1)))
    frames = np.arange(1, 17)
    put("pool_count", np.tile(np.concatenate([w / np.minimum(frames, w) for w in (2, 4, 8, 16)]), (P, 1)))

    small = np.zeros((P, 2 * S), np.float32)
    small[0:16, 0:S] = a["gla_w_a2_2"]
    small[:, S:] = a["pool_w_2"].transpose(1, 0, 2).reshape(P, S)

    q, k, v, z, b_a, a_a, z_s, x_s, b_s, c_s, dt_s = np.split(
        a["w_in"], np.cumsum([D, D, D, D, 8, 8, D, D, 2 * P, 2 * P]), axis=1)
    first = [np.concatenate([b_a, a_a, dt_s, np.zeros((D, P - 32), np.float32)], axis=1)]
    first += [tile_of(w, h) for h in range(8) for w in (q, k, v, z)]
    for g in range(2):
        first += [tile_of(b_s, g), tile_of(c_s, g)] + [tile_of(w, 4 * g + j) for w in (x_s, z_s) for j in range(4)]
    q, k, v, pooled = np.split(a["w_in_even_2"], 4, axis=1)
    even = [v, pooled] + [tile_of(w, i) for i in range(4) for w in (q, k)]
    even_out = np.concatenate([a["w_out_even_2"][S:], a["w_out_even_2"][:S]])
    q, k, v, r, low = np.split(a["w_in_odd_2"], [S, 2 * S, 2 * S + D, 2 * S + 2 * D], axis=1)
    odd = [np.pad(low, ((0, 0), (0, P - 16))), k, v, q, r]
    w8 = [np.concatenate(first, axis=1), a["w_out"], pairs(a["w_up"]), np.concatenate(even, axis=1), even_out,
          pairs(ffn_up[0]), np.concatenate(odd, axis=1), a["w_out_odd_2"], pairs(ffn_up[1])]
    arrays = {
        "x": x[0].T.reshape(KD, P, S).transpose(1, 0, 2).reshape(P, -1),
        "w8": np.concatenate([units(w, KD) for w in w8]),
        "w11": np.concatenate([units(w, HALF) for w in (a["w_down"], ffn_down[0], ffn_down[1])]),
        "par": par, "cst": constants(), "small": small}

    nc = bacc.Bacc("TRN2", target_bir_lowering=False, num_devices=1)
    arrays = {name: np.ascontiguousarray(value) for name, value in arrays.items()}
    aps = [nc.dram_tensor(name, value.shape, F32, kind="ExternalInput").ap() for name, value in arrays.items()]
    out = nc.dram_tensor("out", [P, KD * S], F32, kind="ExternalOutput").ap()
    program(nc, *aps, out, PLAN)
    result = run(nc, [arrays], core_ids=[0])
    return result.results[0]["out"].reshape(P, KD, S).transpose(1, 0, 2).reshape(D, S).T[None]
```
